# Optimizing a Trainium2 kernel written in Bass

```python
import jax, jax.numpy as jnp
from jax import lax
import numpy as np

D_MODEL = 1024
BATCH = 1
SEQ = 256
DEPTH = 2

GRID_W = 64
CTX_LEN = 256
D_MIX = D_MODEL
HEAD_DIM = 64
POOL_GROUPS = 4
POOL_WINDOWS = (2, 4, 8, 16)
POOL_DIM = D_MIX // 4
POOL_GROUP_DIM = POOL_DIM // POOL_GROUPS
NA_HEADS = (D_MIX - POOL_DIM) // 2 // HEAD_DIM
NA_DIM = NA_HEADS * HEAD_DIM
NA_KH = 8
NA_KW = 16
RET_HEADS = (D_MIX - POOL_DIM - NA_DIM) // HEAD_DIM
RET_DIM = RET_HEADS * HEAD_DIM
RET_CHUNK = 128
D_FF = 2816
CONV_W = 3
ROPE_BASE = 10000.0
ROT_QUARTER = HEAD_DIM // 4
EPS = 1e-6
NEG_INF = -1e30
IN_SIZES = (POOL_DIM, NA_DIM, NA_DIM, NA_DIM, RET_DIM, RET_DIM, RET_DIM, RET_DIM)
IN_DIM = sum(IN_SIZES)
SPLIT_POINTS = tuple(int(s) for s in np.cumsum(IN_SIZES)[:-1])


def rmsnorm(t, g):
    tf = t.astype(jnp.float32)
    y = tf * lax.rsqrt(jnp.mean(tf * tf, axis=-1, keepdims=True) + EPS) * g.astype(jnp.float32)
    return y.astype(t.dtype)

def modulate(t, shift, scale):
    return t * (1 + scale) + shift

def heads(t, n):
    return t.reshape(t.shape[0], t.shape[1], n, HEAD_DIM)

def pool_mixer(p, w_grp, scale):
    B, L, _ = p.shape
    pf = p.astype(jnp.float32).reshape(B, L, POOL_GROUPS, POOL_GROUP_DIM)
    csum = jnp.concatenate([jnp.zeros_like(pf[:, :1]), jnp.cumsum(pf, axis=1)], axis=1)
    t = jnp.arange(L)[:, None]
    win = jnp.asarray(POOL_WINDOWS, dtype=jnp.int32)[None, :]
    lo = jnp.clip(t - win // 2, 0, L)
    hi = jnp.clip(t - win // 2 + win, 0, L)
    g = jnp.arange(POOL_GROUPS)[None, :]
    total = csum[:, hi, g] - csum[:, lo, g]
    mean = total / (hi - lo).astype(jnp.float32)[None, :, :, None]
    y = jnp.einsum('blgc,gcd->blgd', mean - pf, w_grp.astype(jnp.float32))
    return (y.reshape(B, L, POOL_DIM) * scale.astype(jnp.float32)).astype(p.dtype)

def neighborhood_attention(q, k, v, kc, vc, rpb, rows):
    B, L, H, dh = q.shape
    kh = min(NA_KH, rows)
    span = 2 * NA_KW
    n_cb = GRID_W // NA_KW
    qg = (q * dh ** -0.5).reshape(B, rows, GRID_W, H, dh)
    kg = k.reshape(B, rows, GRID_W, H, dh)
    vg = v.reshape(B, rows, GRID_W, H, dh)
    qcol = np.arange(GRID_W).reshape(n_cb, NA_KW)
    win_start = np.clip(qcol - NA_KW // 2, 0, GRID_W - NA_KW)
    col_start = np.clip(np.arange(n_cb) * NA_KW - NA_KW // 2, 0, GRID_W - span)
    kcol = col_start[:, None] + np.arange(span)
    col_valid = (kcol[:, None, :] >= win_start[:, :, None]) & (kcol[:, None, :] < win_start[:, :, None] + NA_KW)
    dc_idx = np.clip(kcol[:, None, :] - qcol[:, :, None] + NA_KW - 1, 0, 2 * NA_KW - 2)
    rpb_c = rpb.astype(jnp.float32)[:, :, dc_idx]
    valid = jnp.asarray(col_valid)[:, :, None, :]

    def one_row(r):
        rs = jnp.clip(r - kh // 2, 0, rows - kh)
        qr = lax.dynamic_index_in_dim(qg, r, axis=1, keepdims=False)
        kr = lax.dynamic_slice_in_dim(kg, rs, kh, axis=1)
        vr = lax.dynamic_slice_in_dim(vg, rs, kh, axis=1)
        kb = kr[:, :, kcol]
        vb = vr[:, :, kcol]
        qb = qr.reshape(B, n_cb, NA_KW, H, dh)
        dr_idx = rs + jnp.arange(kh) - r + NA_KH - 1
        bias = rpb_c[:, dr_idx].transpose(0, 2, 3, 1, 4)
        s_loc = jnp.einsum('bnqhd,binshd->bhnqis', qb, kb).astype(jnp.float32)
        s_loc = jnp.where(valid, s_loc + bias, NEG_INF)
        s_ctx = jnp.einsum('bnqhd,bkhd->bhnqk', qb, kc).astype(jnp.float32)
        s = jnp.concatenate([s_loc.reshape(B, H, n_cb, NA_KW, kh * span), s_ctx], axis=-1)
        p = jax.nn.softmax(s, axis=-1).astype(v.dtype)
        p_loc = p[..., :kh * span].reshape(B, H, n_cb, NA_KW, kh, span)
        p_ctx = p[..., kh * span:]
        o = jnp.einsum('bhnqis,binshd->bnqhd', p_loc, vb) + jnp.einsum('bhnqk,bkhd->bnqhd', p_ctx, vc)
        return o.reshape(B, GRID_W, H, dh)

    out = lax.map(one_row, jnp.arange(rows))
    return out.transpose(1, 0, 2, 3, 4).reshape(B, L, H, dh)

def context_attention(q, k, v):
    s = jnp.einsum('bqhd,bkhd->bhqk', q * HEAD_DIM ** -0.5, k).astype(jnp.float32)
    p = jax.nn.softmax(s, axis=-1).astype(v.dtype)
    return jnp.einsum('bhqk,bkhd->bqhd', p, v)

def axial_rotary(t, cos_r, sin_r, cos_c, sin_c):
    def rot(u, cos, sin):
        u1, u2 = jnp.split(u, 2, axis=-1)
        cos = cos[None, :, None, :]
        sin = sin[None, :, None, :]
        return jnp.concatenate([u1 * cos - u2 * sin, u1 * sin + u2 * cos], axis=-1)
    tr, tc = jnp.split(t, 2, axis=-1)
    return jnp.concatenate([rot(tr, cos_r, sin_r), rot(tc, cos_c, sin_c)], axis=-1)

def retention_chunks(q, k, v, log_gamma, state, with_outputs):
    B, L, H, _ = q.shape
    n = L // RET_CHUNK
    lg = log_gamma.astype(jnp.float32)
    idx = jnp.arange(RET_CHUNK, dtype=jnp.float32)
    diff = idx[:, None] - idx[None, :]
    intra = jnp.exp(jnp.where(diff[None] >= 0, diff[None] * lg[:, None, None], -jnp.inf))
    q_dec = jnp.exp((idx + 1)[None, :] * lg[:, None])
    k_dec = jnp.exp((RET_CHUNK - 1 - idx)[None, :] * lg[:, None])
    c_dec = jnp.exp(RET_CHUNK * lg)

    def to_chunks(t):
        return t.reshape(B, n, RET_CHUNK, H, t.shape[-1]).transpose(1, 0, 3, 2, 4)

    def step(s, blk):
        qb, kb, vb = blk
        s_new = s * c_dec[None, :, None, None] + jnp.einsum('bhcd,bhce->bhde', kb * k_dec[None, :, :, None], vb)
        if not with_outputs:
            return s_new, None
        a = jnp.einsum('bhid,bhjd->bhij', qb, kb) * intra[None]
        y = jnp.einsum('bhij,bhje->bhie', a, vb) + jnp.einsum('bhid,bhde->bhie', qb, s) * q_dec[None, :, :, None]
        return s_new, y

    s_fin, ys = lax.scan(step, state, (to_chunks(q), to_chunks(k), to_chunks(v)))
    if not with_outputs:
        return None, s_fin
    return ys.transpose(1, 0, 3, 2, 4).reshape(B, L, H, v.shape[-1]), s_fin

def bidirectional_retention(q, k, v, qc, kc, vc, dec_f, dec_b, need_ctx):
    B = q.shape[0]
    s0 = jnp.zeros((B, RET_HEADS, HEAD_DIM, HEAD_DIM), jnp.float32)
    rev = lambda t: jnp.flip(t, axis=1)
    yc_f, s_f = retention_chunks(qc, kc, vc, dec_f, s0, need_ctx)
    yx_f, _ = retention_chunks(q, k, v, dec_f, s_f, True)
    yc_b, s_b = retention_chunks(rev(qc), rev(kc), rev(vc), dec_b, s0, need_ctx)
    yx_b, _ = retention_chunks(rev(q), rev(k), rev(v), dec_b, s_b, True)
    yc = yc_f + rev(yc_b) if need_ctx else None
    return yx_f + rev(yx_b), yc

def retention_output(y, gate, gn_g):
    B, L = y.shape[:2]
    mu = jnp.mean(y, axis=-1, keepdims=True)
    var = jnp.mean((y - mu) ** 2, axis=-1, keepdims=True)
    yn = ((y - mu) * lax.rsqrt(var + EPS)).reshape(B, L, RET_DIM) * gn_g.astype(jnp.float32)
    return (jax.nn.silu(gate.astype(jnp.float32)) * yn).astype(gate.dtype)

def mixing_layer(px, pc, pool_w, pool_scale, na_rpb, dec_f, dec_b, gn_g, rope, rows, need_ctx):
    B, L, _ = px.shape
    xs = jnp.split(px, SPLIT_POINTS, axis=-1)
    cs = jnp.split(pc, SPLIT_POINTS, axis=-1)
    f32 = jnp.float32
    pool_x = pool_mixer(xs[0], pool_w, pool_scale)
    na_q, na_k, na_v = [heads(t, NA_HEADS) for t in xs[1:4]]
    nc_q, nc_k, nc_v = [heads(t, NA_HEADS) for t in cs[1:4]]
    na_x = neighborhood_attention(na_q, na_k, na_v, nc_k, nc_v, na_rpb, rows).reshape(B, L, NA_DIM)
    rq = axial_rotary(heads(xs[4], RET_HEADS).astype(f32), *rope)
    rk = axial_rotary(heads(xs[5], RET_HEADS).astype(f32), *rope) * HEAD_DIM ** -0.5
    rv = heads(xs[6], RET_HEADS).astype(f32)
    cq = heads(cs[4], RET_HEADS).astype(f32)
    ck = heads(cs[5], RET_HEADS).astype(f32) * HEAD_DIM ** -0.5
    cv = heads(cs[6], RET_HEADS).astype(f32)
    ret_x, ret_c = bidirectional_retention(rq, rk, rv, cq, ck, cv, dec_f, dec_b, need_ctx)
    ret_x = retention_output(ret_x, xs[7], gn_g)
    yx = jnp.concatenate([pool_x, na_x.astype(px.dtype), ret_x.astype(px.dtype)], axis=-1)
    if not need_ctx:
        return yx, None
    pool_c = pool_mixer(cs[0], pool_w, pool_scale)
    na_c = context_attention(nc_q, nc_k, nc_v).reshape(B, pc.shape[1], NA_DIM)
    ret_c = retention_output(ret_c, cs[7], gn_g)
    yc = jnp.concatenate([pool_c, na_c.astype(pc.dtype), ret_c.astype(pc.dtype)], axis=-1)
    return yx, yc

def conv_ffn(h, w_up, conv_w, conv_b, w_down):
    u = h @ w_up
    up = jnp.pad(u, ((0, 0), (1, 1), (0, 0)))
    u = up[:, :-2] * conv_w[0] + up[:, 1:-1] * conv_w[1] + up[:, 2:] * conv_w[2] + conv_b
    a, b = jnp.split(u, 2, axis=-1)
    return (jax.nn.silu(a) * b) @ w_down

def first_inputs(seed: int = 0) -> dict:
    key = jax.random.key(seed)
    ks = jax.random.split(key, 24)
    f32 = jnp.float32
    nrm = lambda k, shape, s: jax.random.normal(k, shape, f32) * s
    exps_f = 5.0 + jnp.arange(RET_HEADS, dtype=f32)[None, :] + 0.25 * jax.random.uniform(ks[11], (DEPTH, RET_HEADS), f32)
    exps_b = 5.0 + jnp.arange(RET_HEADS, dtype=f32)[None, :] + 0.25 * jax.random.uniform(ks[12], (DEPTH, RET_HEADS), f32)
    return {
        "x": nrm(ks[0], (BATCH, SEQ, D_MODEL), 1.0),
        "c": nrm(ks[1], (BATCH, D_MODEL), 1.0),
        "ctx": nrm(ks[2], (BATCH, CTX_LEN, D_MODEL), 1.0),
        "c_ctx": nrm(ks[3], (D_MODEL,), 1.0),
        "w_mod": nrm(ks[4], (DEPTH, D_MODEL, 6 * D_MODEL), 0.5 * D_MODEL ** -0.5),
        "b_mod": nrm(ks[5], (DEPTH, 6 * D_MODEL), 0.02),
        "norm1_g": 1.0 + nrm(ks[6], (DEPTH, D_MODEL), 0.02),
        "w_in": nrm(ks[7], (DEPTH, D_MODEL, IN_DIM), D_MODEL ** -0.5),
        "pool_w": nrm(ks[8], (DEPTH, POOL_GROUPS, POOL_GROUP_DIM, POOL_GROUP_DIM), POOL_GROUP_DIM ** -0.5),
        "pool_scale": 1.0 + nrm(ks[9], (DEPTH, POOL_DIM), 0.1),
        "na_rpb": nrm(ks[10], (DEPTH, NA_HEADS, 2 * NA_KH - 1, 2 * NA_KW - 1), 0.1),
        "ret_decay_fwd": jnp.log1p(-jnp.exp2(-exps_f)),
        "ret_decay_bwd": jnp.log1p(-jnp.exp2(-exps_b)),
        "ret_gn_g": 1.0 + nrm(ks[13], (DEPTH, RET_DIM), 0.02),
        "w_out": nrm(ks[14], (DEPTH, D_MIX, D_MODEL), D_MIX ** -0.5),
        "norm2_g": 1.0 + nrm(ks[15], (DEPTH, D_MODEL), 0.02),
        "w_up": nrm(ks[16], (DEPTH, D_MODEL, 2 * D_FF), D_MODEL ** -0.5),
        "conv_w": nrm(ks[17], (DEPTH, CONV_W, 2 * D_FF), CONV_W ** -0.5),
        "conv_b": nrm(ks[18], (DEPTH, 2 * D_FF), 0.02),
        "w_down": nrm(ks[19], (DEPTH, D_FF, D_MODEL), D_FF ** -0.5),
        "final_g": 1.0 + nrm(ks[20], (D_MODEL,), 0.02),
    }

def first_block(x, c, ctx, c_ctx, w_mod, b_mod, norm1_g, w_in, pool_w, pool_scale, na_rpb, ret_decay_fwd, ret_decay_bwd, ret_gn_g, w_out, norm2_g, w_up, conv_w, conv_b, w_down, final_g):
    B, L, _ = x.shape
    rows = L // GRID_W
    pos = jnp.arange(L)
    inv = ROPE_BASE ** (-jnp.arange(ROT_QUARTER, dtype=jnp.float32) / ROT_QUARTER)
    ang_r = (pos // GRID_W).astype(jnp.float32)[:, None] * inv[None, :]
    ang_c = (pos % GRID_W).astype(jnp.float32)[:, None] * inv[None, :]
    rope = (jnp.cos(ang_r), jnp.sin(ang_r), jnp.cos(ang_c), jnp.sin(ang_c))
    silu_c = jax.nn.silu(c)[:, None, :]
    silu_cc = jax.nn.silu(c_ctx)
    h = x
    hc = ctx
    for l in range(DEPTH):
        need_ctx = l < DEPTH - 1
        mx = jnp.split(silu_c @ w_mod[l] + b_mod[l], 6, axis=-1)
        mc = jnp.split(silu_cc @ w_mod[l] + b_mod[l], 6, axis=-1)
        ax = modulate(rmsnorm(h, norm1_g[l]), mx[0], mx[1])
        ac = modulate(rmsnorm(hc, norm1_g[l]), mc[0], mc[1])
        yx, yc = mixing_layer(ax @ w_in[l], ac @ w_in[l], pool_w[l], pool_scale[l], na_rpb[l],
                              ret_decay_fwd[l], ret_decay_bwd[l], ret_gn_g[l], rope, rows, need_ctx)
        h = h + mx[2] * (yx @ w_out[l])
        h = h + mx[5] * conv_ffn(modulate(rmsnorm(h, norm2_g[l]), mx[3], mx[4]), w_up[l], conv_w[l], conv_b[l], w_down[l])
        if need_ctx:
            hc = hc + mc[2] * (yc @ w_out[l])
            hc = hc + mc[5] * conv_ffn(modulate(rmsnorm(hc, norm2_g[l]), mc[3], mc[4]), w_up[l], conv_w[l], conv_b[l], w_down[l])
    return rmsnorm(h, final_g)


GROUP_WIDTH = D_MODEL // 2
GROUP_HEADS = GROUP_WIDTH // HEAD_DIM
RW_HEADS = GROUP_HEADS
RW_DIM = GROUP_WIDTH
DECAY_LORA = 64
AAA_LORA = 64
GATE_LORA = 128
RW_GN_EPS = 64e-5
MLA_HEADS = GROUP_HEADS
MLA_NOPE = HEAD_DIM
MLA_ROPE = HEAD_DIM // 2
MLA_V = HEAD_DIM
MLA_Q_RANK = D_MODEL // 4
MLA_KV_RANK = D_MODEL // 8
FOX_HEADS = GROUP_HEADS
FOX_DIM = GROUP_WIDTH
MOBA_HEADS = GROUP_HEADS
MOBA_DIM = GROUP_WIDTH
MOBA_BLOCK = 256
MOBA_TOPK = 3
MOBA_Q_CHUNK = 32
Q_BLOCK = 128
ROPE_THETA = 10000.0
NORM_EPS = 1e-6
D_FF_2 = 256 * ((8 * D_MODEL // 3 + 255) // 256)
N_EXPERTS = 8
TOP_K = 2
D_EXPERT = 7 * D_MODEL // 2

RW_SIZES = (RW_DIM, RW_DIM, RW_DIM, DECAY_LORA, AAA_LORA, GATE_LORA)
RW_COLS = sum(RW_SIZES)
MLA_SIZES = (MLA_Q_RANK, MLA_KV_RANK, MLA_ROPE)
IN0_COLS = RW_COLS + sum(MLA_SIZES)
FOX_SIZES = (FOX_DIM, FOX_DIM, FOX_DIM, FOX_HEADS)
FOX_COLS = sum(FOX_SIZES)
MOBA_SIZES = (MOBA_DIM, MOBA_DIM, MOBA_DIM)
IN1_COLS = FOX_COLS + sum(MOBA_SIZES)
MIX0_OUT = RW_DIM + MLA_HEADS * MLA_V
MIX1_OUT = FOX_DIM + MOBA_DIM


def split_cols(t, sizes):
    return jnp.split(t, [int(i) for i in np.cumsum(sizes)[:-1]], axis=-1)

def to_heads(t, n_heads):
    b, s, _ = t.shape
    return t.reshape(b, s, n_heads, -1)

def rmsnorm_2(x, g, eps=NORM_EPS):
    xf = x.astype(jnp.float32)
    xf = xf * lax.rsqrt(jnp.mean(xf * xf, axis=-1, keepdims=True) + eps)
    return (xf * g.astype(jnp.float32)).astype(x.dtype)

def rope_tables(seq_len, dim):
    inv_freq = ROPE_THETA ** (-jnp.arange(0, dim, 2, dtype=jnp.float32) / dim)
    ang = jnp.arange(seq_len, dtype=jnp.float32)[:, None] * inv_freq[None, :]
    return jnp.cos(ang), jnp.sin(ang)

def apply_rope(x, cos_r, sin_r):
    xf = x.astype(jnp.float32)
    x1, x2 = jnp.split(xf, 2, axis=-1)
    c, s = cos_r[:, None, :], sin_r[:, None, :]
    return jnp.concatenate([x1 * c - x2 * s, x2 * c + x1 * s], axis=-1).astype(x.dtype)

def swiglu(t, w_gate, w_up, w_down):
    return (jax.nn.silu(t @ w_gate) * (t @ w_up)) @ w_down

def block_causal_attention(q, k, v, scale, log_decay_cum=None):
    b, h, s, _ = q.shape
    k_pos = jnp.arange(s)

    def one_block(i):
        start = i * Q_BLOCK
        qb = lax.dynamic_slice_in_dim(q, start, Q_BLOCK, axis=2)
        logits = jnp.einsum('bhqd,bhkd->bhqk', qb, k).astype(jnp.float32) * scale
        q_pos = start + jnp.arange(Q_BLOCK)
        if log_decay_cum is not None:
            dq = lax.dynamic_slice_in_dim(log_decay_cum, start, Q_BLOCK, axis=2)
            logits = logits + dq[..., :, None] - log_decay_cum[..., None, :]
        logits = jnp.where(k_pos[None, :] <= q_pos[:, None], logits, -jnp.inf)
        p = jax.nn.softmax(logits, axis=-1).astype(v.dtype)
        return jnp.einsum('bhqk,bhkd->bhqd', p, v)

    out = lax.map(one_block, jnp.arange(s // Q_BLOCK))
    return out.transpose(1, 2, 0, 3, 4).reshape(b, h, s, -1)

def rwkv7_time_mix(r, k, v, w_down, a_down, g_down, w0, w2, a0, a2, g2,
                   k_k, k_a, r_k, lnx_g, lnx_b):
    out_dtype = r.dtype
    f32 = jnp.float32
    r, k, v, w_down, a_down, g_down = (t.astype(f32) for t in (r, k, v, w_down, a_down, g_down))
    b, s, c = r.shape
    h, n = RW_HEADS, HEAD_DIM
    log_w = -jax.nn.softplus(-(w0 + jnp.tanh(w_down) @ w2)) - 0.5
    decay = jnp.exp(-jnp.exp(log_w))
    a = jax.nn.sigmoid(a0 + a_down @ a2)
    g = jax.nn.sigmoid(g_down) @ g2
    kk = (k * k_k).reshape(b, s, h, n)
    kk = kk / jnp.maximum(jnp.linalg.norm(kk, axis=-1, keepdims=True), 1e-12)
    k = k * (1.0 + (a - 1.0) * k_a)
    r_h, w_h, k_h, v_h, a_h = (t.reshape(b, s, h, n) for t in (r, decay, k, v, a))
    b_h = kk * a_h
    xs = tuple(jnp.moveaxis(t, 1, 0) for t in (r_h, w_h, k_h, v_h, kk, b_h))

    def step(state, inp):
        r_t, w_t, k_t, v_t, kk_t, b_t = inp
        sa = jnp.einsum('bhvk,bhk->bhv', state, -kk_t)
        state = (state * w_t[:, :, None, :] + sa[..., None] * b_t[:, :, None, :]
                 + v_t[..., None] * k_t[:, :, None, :])
        return state, jnp.einsum('bhvk,bhk->bhv', state, r_t)

    state0 = jnp.zeros((b, h, n, n), f32)
    _, y = lax.scan(step, state0, xs)
    y = jnp.moveaxis(y, 0, 1)
    mu = jnp.mean(y, axis=-1, keepdims=True)
    var = jnp.mean(jnp.square(y - mu), axis=-1, keepdims=True)
    y = ((y - mu) * lax.rsqrt(var + RW_GN_EPS)).reshape(b, s, c) * lnx_g + lnx_b
    bonus = jnp.sum(r_h * k_h * r_k, axis=-1, keepdims=True) * v_h
    y = (y + bonus.reshape(b, s, c)) * g
    return y.astype(out_dtype)

def mla_attention(q_lat, kv_lat, k_rope, q_norm, w_uq, kv_norm, w_ukv, cos_r, sin_r):
    b, s, _ = q_lat.shape
    h = MLA_HEADS
    q = to_heads(rmsnorm_2(q_lat, q_norm) @ w_uq, h)
    q_nope, q_pe = q[..., :MLA_NOPE], apply_rope(q[..., MLA_NOPE:], cos_r, sin_r)
    kv = to_heads(rmsnorm_2(kv_lat, kv_norm) @ w_ukv, h)
    k_nope, v = kv[..., :MLA_NOPE], kv[..., MLA_NOPE:]
    k_pe = apply_rope(k_rope[:, :, None, :], cos_r, sin_r)
    q = jnp.concatenate([q_nope, q_pe], axis=-1)
    k = jnp.concatenate([k_nope, jnp.broadcast_to(k_pe, (b, s, h, MLA_ROPE))], axis=-1)
    out = block_causal_attention(q.transpose(0, 2, 1, 3), k.transpose(0, 2, 1, 3),
                                 v.transpose(0, 2, 1, 3), (MLA_NOPE + MLA_ROPE) ** -0.5)
    return out.transpose(0, 2, 1, 3).reshape(b, s, h * MLA_V)

def forgetting_attention(q, k, v, f_logit, b_f):
    b, s, _ = q.shape
    h = FOX_HEADS
    log_f = jax.nn.log_sigmoid(f_logit.astype(jnp.float32) + b_f.astype(jnp.float32))
    d_cum = jnp.cumsum(log_f, axis=1).transpose(0, 2, 1)
    qh, kh, vh = (to_heads(t, h).transpose(0, 2, 1, 3) for t in (q, k, v))
    out = block_causal_attention(qh, kh, vh, HEAD_DIM ** -0.5, d_cum)
    return out.transpose(0, 2, 1, 3).reshape(b, s, h * HEAD_DIM)

def moba_attention(q, k, v, cos_r, sin_r):
    b, s, _ = q.shape
    h, d = MOBA_HEADS, HEAD_DIM
    qh = apply_rope(to_heads(q, h), cos_r, sin_r).transpose(0, 2, 1, 3)
    kh = apply_rope(to_heads(k, h), cos_r, sin_r).transpose(0, 2, 1, 3)
    vh = to_heads(v, h).transpose(0, 2, 1, 3)
    nb = -(-s // MOBA_BLOCK)
    pad = nb * MOBA_BLOCK - s
    kp = jnp.pad(kh, ((0, 0), (0, 0), (0, pad), (0, 0)))
    vp = jnp.pad(vh, ((0, 0), (0, 0), (0, pad), (0, 0)))
    k_blocks = kp.reshape(b, h, nb, MOBA_BLOCK, d)
    v_blocks = vp.reshape(b, h, nb, MOBA_BLOCK, d)
    k_mean = jnp.mean(k_blocks.astype(jnp.float32), axis=3).astype(kh.dtype)
    n_sel = min(MOBA_TOPK, nb)
    n_sel_keys = n_sel * MOBA_BLOCK
    scale = d ** -0.5
    b_idx = jnp.arange(b)[:, None, None, None]
    h_idx = jnp.arange(h)[None, :, None, None]
    blk_ids = jnp.arange(nb)
    offs = jnp.arange(MOBA_BLOCK)

    def one_chunk(i):
        start = i * MOBA_Q_CHUNK
        qc = lax.dynamic_slice_in_dim(qh, start, MOBA_Q_CHUNK, axis=2)
        q_pos = start + jnp.arange(MOBA_Q_CHUNK)
        own = start // MOBA_BLOCK
        gate = jnp.einsum('bhqd,bhnd->bhqn', qc, k_mean).astype(jnp.float32)
        gate = jnp.where(blk_ids < own, gate, -jnp.inf)
        _, sel = lax.top_k(gate, n_sel)
        sel_valid = sel < own
        k_sel = k_blocks[b_idx, h_idx, sel]
        v_sel = v_blocks[b_idx, h_idx, sel]
        s_sel = jnp.einsum('bhqd,bhqjld->bhqjl', qc, k_sel).astype(jnp.float32) * scale
        s_sel = jnp.where(sel_valid[..., None], s_sel, -jnp.inf)
        k_own = lax.dynamic_slice_in_dim(kp, own * MOBA_BLOCK, MOBA_BLOCK, axis=2)
        v_own = lax.dynamic_slice_in_dim(vp, own * MOBA_BLOCK, MOBA_BLOCK, axis=2)
        s_own = jnp.einsum('bhqd,bhld->bhql', qc, k_own).astype(jnp.float32) * scale
        s_own = jnp.where((own * MOBA_BLOCK + offs)[None, :] <= q_pos[:, None], s_own, -jnp.inf)
        logits = jnp.concatenate([s_sel.reshape(b, h, MOBA_Q_CHUNK, n_sel_keys), s_own], axis=-1)
        p = jax.nn.softmax(logits, axis=-1).astype(vh.dtype)
        p_sel = p[..., :n_sel_keys].reshape(b, h, MOBA_Q_CHUNK, n_sel, MOBA_BLOCK)
        p_own = p[..., n_sel_keys:]
        return (jnp.einsum('bhqjl,bhqjld->bhqd', p_sel, v_sel)
                + jnp.einsum('bhql,bhld->bhqd', p_own, v_own))

    out = lax.map(one_chunk, jnp.arange(s // MOBA_Q_CHUNK))
    out = out.transpose(1, 2, 0, 3, 4).reshape(b, h, s, d)
    return out.transpose(0, 2, 1, 3).reshape(b, s, h * d)

def moe_swiglu(t, router, w_gate, w_up, w_down):
    logits = (t @ router).astype(jnp.float32)
    top_logits, top_idx = lax.top_k(logits, TOP_K)
    gates = jax.nn.softmax(top_logits, axis=-1)
    combine = jnp.sum(jax.nn.one_hot(top_idx, N_EXPERTS, dtype=jnp.float32) * gates[..., None], axis=1)
    out = jnp.zeros_like(t)
    for e in range(N_EXPERTS):
        out = out + combine[:, e:e + 1].astype(t.dtype) * swiglu(t, w_gate[e], w_up[e], w_down[e])
    return out

def even_layer(h, norm_mix, w_in, shift_mu, rw_w0, rw_w2, rw_a0, rw_a2, rw_g2, rw_kk, rw_ka,
               rw_rk, rw_lnx_g, rw_lnx_b, mla_qnorm, mla_wuq, mla_kvnorm, mla_wukv, w_out,
               norm_ffn, ffn_wg, ffn_wu, ffn_wd, cos_r, sin_r):
    u = rmsnorm_2(h, norm_mix)
    proj = u @ w_in
    rw_cols, mla_cols = proj[..., :RW_COLS], proj[..., RW_COLS:]
    rw_prev = jnp.pad(rw_cols[:, :-1], ((0, 0), (1, 0), (0, 0)))
    rw_cols = rw_cols + shift_mu * (rw_prev - rw_cols)
    y_a = rwkv7_time_mix(*split_cols(rw_cols, RW_SIZES), rw_w0, rw_w2, rw_a0, rw_a2, rw_g2,
                         rw_kk, rw_ka, rw_rk, rw_lnx_g, rw_lnx_b)
    y_b = mla_attention(*split_cols(mla_cols, MLA_SIZES), mla_qnorm, mla_wuq, mla_kvnorm,
                        mla_wukv, cos_r, sin_r)
    h = h + jnp.concatenate([y_a, y_b], axis=-1) @ w_out
    return h + swiglu(rmsnorm_2(h, norm_ffn), ffn_wg, ffn_wu, ffn_wd)

def odd_layer(h, norm_mix, w_in, fox_bf, w_out, norm_ffn, router, moe_wg, moe_wu, moe_wd,
              cos_r, sin_r):
    b, s, d = h.shape
    u = rmsnorm_2(h, norm_mix)
    proj = u @ w_in
    fox_cols, moba_cols = proj[..., :FOX_COLS], proj[..., FOX_COLS:]
    y_c = forgetting_attention(*split_cols(fox_cols, FOX_SIZES), fox_bf)
    y_d = moba_attention(*split_cols(moba_cols, MOBA_SIZES), cos_r, sin_r)
    h = h + jnp.concatenate([y_c, y_d], axis=-1) @ w_out
    t = rmsnorm_2(h, norm_ffn).reshape(b * s, d)
    return h + moe_swiglu(t, router, moe_wg, moe_wu, moe_wd).reshape(b, s, d)

def second_inputs(seed: int = 0) -> dict:
    key = jax.random.key(seed)
    ks = iter(jax.random.split(key, 40))
    D = D_MODEL

    def nrm(shape, scale):
        return scale * jax.random.normal(next(ks), shape, jnp.float32)

    def gain(n):
        return 1.0 + nrm((n,), 0.05)

    return {
        'x': nrm((BATCH, SEQ, D), 1.0),
        'norm_mix_0': gain(D),
        'w_in_0': nrm((D, IN0_COLS), D ** -0.5),
        'shift_mu_0': jax.random.uniform(next(ks), (RW_COLS,), jnp.float32, 0.2, 0.8),
        'rw_w0_0': jax.random.uniform(next(ks), (RW_DIM,), jnp.float32, -6.0, -1.0),
        'rw_w2_0': nrm((DECAY_LORA, RW_DIM), DECAY_LORA ** -0.5),
        'rw_a0_0': nrm((RW_DIM,), 0.1),
        'rw_a2_0': nrm((AAA_LORA, RW_DIM), AAA_LORA ** -0.5),
        'rw_g2_0': nrm((GATE_LORA, RW_DIM), GATE_LORA ** -0.5),
        'rw_kk_0': 0.85 + nrm((RW_DIM,), 0.05),
        'rw_ka_0': 1.0 + nrm((RW_DIM,), 0.05),
        'rw_rk_0': nrm((RW_HEADS, HEAD_DIM), 0.1),
        'rw_lnx_g_0': gain(RW_DIM),
        'rw_lnx_b_0': nrm((RW_DIM,), 0.02),
        'mla_qnorm_0': gain(MLA_Q_RANK),
        'mla_wuq_0': nrm((MLA_Q_RANK, MLA_HEADS * (MLA_NOPE + MLA_ROPE)), MLA_Q_RANK ** -0.5),
        'mla_kvnorm_0': gain(MLA_KV_RANK),
        'mla_wukv_0': nrm((MLA_KV_RANK, MLA_HEADS * (MLA_NOPE + MLA_V)), MLA_KV_RANK ** -0.5),
        'w_out_0': nrm((MIX0_OUT, D), MIX0_OUT ** -0.5),
        'norm_ffn_0': gain(D),
        'ffn_wg_0': nrm((D, D_FF_2), D ** -0.5),
        'ffn_wu_0': nrm((D, D_FF_2), D ** -0.5),
        'ffn_wd_0': nrm((D_FF_2, D), D_FF_2 ** -0.5),
        'norm_mix_1': gain(D),
        'w_in_1': nrm((D, IN1_COLS), D ** -0.5),
        'fox_bf_1': 3.0 + nrm((FOX_HEADS,), 0.5),
        'w_out_1': nrm((MIX1_OUT, D), MIX1_OUT ** -0.5),
        'norm_ffn_1': gain(D),
        'router_1': nrm((D, N_EXPERTS), D ** -0.5),
        'moe_wg_1': nrm((N_EXPERTS, D, D_EXPERT), D ** -0.5),
        'moe_wu_1': nrm((N_EXPERTS, D, D_EXPERT), D ** -0.5),
        'moe_wd_1': nrm((N_EXPERTS, D_EXPERT, D), D_EXPERT ** -0.5),
        'final_norm': gain(D),
    }

def second_block(x, norm_mix_0, w_in_0, shift_mu_0, rw_w0_0, rw_w2_0, rw_a0_0, rw_a2_0, rw_g2_0,
              rw_kk_0, rw_ka_0, rw_rk_0, rw_lnx_g_0, rw_lnx_b_0, mla_qnorm_0, mla_wuq_0,
              mla_kvnorm_0, mla_wukv_0, w_out_0, norm_ffn_0, ffn_wg_0, ffn_wu_0, ffn_wd_0,
              norm_mix_1, w_in_1, fox_bf_1, w_out_1, norm_ffn_1, router_1, moe_wg_1, moe_wu_1,
              moe_wd_1, final_norm):
    seq_len = x.shape[1]
    rope_mla = rope_tables(seq_len, MLA_ROPE)
    rope_full = rope_tables(seq_len, HEAD_DIM)
    layer_params = (
        (norm_mix_0, w_in_0, shift_mu_0, rw_w0_0, rw_w2_0, rw_a0_0, rw_a2_0, rw_g2_0, rw_kk_0,
         rw_ka_0, rw_rk_0, rw_lnx_g_0, rw_lnx_b_0, mla_qnorm_0, mla_wuq_0, mla_kvnorm_0,
         mla_wukv_0, w_out_0, norm_ffn_0, ffn_wg_0, ffn_wu_0, ffn_wd_0),
        (norm_mix_1, w_in_1, fox_bf_1, w_out_1, norm_ffn_1, router_1, moe_wg_1, moe_wu_1,
         moe_wd_1),
    )
    h = x
    for layer in range(DEPTH):
        if layer % 2 == 0:
            h = even_layer(h, *layer_params[layer], *rope_mla)
        else:
            h = odd_layer(h, *layer_params[layer], *rope_full)
    return rmsnorm_2(h, final_norm)


def setup_inputs(seed=0):
    out = dict(first_inputs(seed))
    for name, value in second_inputs(seed + 1).items():
        if name != "x":
            out[name + "_2"] = value
    return out


def reference(
    x, c, ctx, c_ctx, w_mod, b_mod, norm1_g, w_in, pool_w, pool_scale, na_rpb, ret_decay_fwd,
    ret_decay_bwd, ret_gn_g, w_out, norm2_g, w_up, conv_w, conv_b, w_down, final_g,
    norm_mix_0_2, w_in_0_2, shift_mu_0_2, rw_w0_0_2, rw_w2_0_2, rw_a0_0_2, rw_a2_0_2, rw_g2_0_2,
    rw_kk_0_2, rw_ka_0_2, rw_rk_0_2, rw_lnx_g_0_2, rw_lnx_b_0_2, mla_qnorm_0_2, mla_wuq_0_2,
    mla_kvnorm_0_2, mla_wukv_0_2, w_out_0_2, norm_ffn_0_2, ffn_wg_0_2, ffn_wu_0_2, ffn_wd_0_2,
    norm_mix_1_2, w_in_1_2, fox_bf_1_2, w_out_1_2, norm_ffn_1_2, router_1_2, moe_wg_1_2,
    moe_wu_1_2, moe_wd_1_2, final_norm_2,
):
    x = first_block(
        x, c, ctx, c_ctx, w_mod, b_mod, norm1_g, w_in, pool_w, pool_scale, na_rpb,
        ret_decay_fwd, ret_decay_bwd, ret_gn_g, w_out, norm2_g, w_up, conv_w, conv_b, w_down,
        final_g,
    )
    return second_block(
        x, norm_mix_0_2, w_in_0_2, shift_mu_0_2, rw_w0_0_2, rw_w2_0_2, rw_a0_0_2, rw_a2_0_2,
        rw_g2_0_2, rw_kk_0_2, rw_ka_0_2, rw_rk_0_2, rw_lnx_g_0_2, rw_lnx_b_0_2, mla_qnorm_0_2,
        mla_wuq_0_2, mla_kvnorm_0_2, mla_wukv_0_2, w_out_0_2, norm_ffn_0_2, ffn_wg_0_2,
        ffn_wu_0_2, ffn_wd_0_2, norm_mix_1_2, w_in_1_2, fox_bf_1_2, w_out_1_2, norm_ffn_1_2,
        router_1_2, moe_wg_1_2, moe_wu_1_2, moe_wd_1_2, final_norm_2,
    )


_drawn_inputs = setup_inputs


def setup_inputs(seed=0):
    import zlib

    import numpy as np

    out = dict(_drawn_inputs(seed))
    spreads = {}
    factors = {'na_rpb': 5.777, 'ret_gn_g': 3.933, 'mla_qnorm_0_2': 3.989, 'rw_lnx_b_0_2': 2.743}
    for name, (base, spread) in spreads.items():
        noise = np.random.default_rng([zlib.crc32(name.encode()), seed]).standard_normal(out[name].shape)
        drawn = base * np.exp(spread * noise) if base else spread * noise
        out[name] = __import__('jax').numpy.asarray(drawn.astype(out[name].dtype))
    for name, factor in factors.items():
        out[name] = (out[name] * factor).astype(out[name].dtype)
    return out
```

```python
from contextlib import ExitStack

import numpy as np

import concourse.bass as bass
from concourse import mybir

F32 = mybir.dt.float32
ALU = mybir.AluOpType
ACT = mybir.ActivationFunctionType
AX = mybir.AxisListType

P = 128
D = 1024
KD = D // P
L = 256
T2 = 2 * L
HD = 64
GRID_W, NA_KW, NA_KH = 64, 16, 8
POOL_WINDOWS = (2, 4, 8, 16)
NAH = RETH = 6
FF = 2816
KF = FF // P
NH2 = 8
NE, FE = 8, 3584
KE = FE // P
FC = 448
ES = 2 * FE // FC + 8
SLOTS = P
CH = 32
EPS = 1e-6
SLOT = 4096
RING = 4
NEG = -1e30


def tables_a():
    p = np.arange(P)
    out = {}
    out["ident"] = np.eye(P)
    out["ones"] = np.ones((P, P))
    out["headones"] = (p[:, None] // HD == p[None, :] // HD) * 1.0
    c = p % HD
    half, within = c // 32, c % 32
    inv = (10000.0 ** (-np.arange(16, dtype=np.float32) / 16)).astype(np.float32)
    t = np.arange(L)
    pos = np.where(half[:, None] == 0, (t // GRID_W)[None, :], (t % GRID_W)[None, :]).astype(np.float32)
    ang = pos * inv[within % 16][:, None]
    out["rot_cos"] = np.cos(ang)
    out["rot_sin"] = np.where((within < 16)[:, None], -np.sin(ang), np.sin(ang))
    out["rot_swap"] = (p[:, None] == (p ^ 16)[None, :]) * 1.0
    qc = p % GRID_W
    kc = np.arange(L) % GRID_W
    ws = np.clip(qc - NA_KW // 2, 0, GRID_W - NA_KW)
    ok = (kc[None, :] >= ws[:, None]) & (kc[None, :] < ws[:, None] + NA_KW)
    out["na_mask"] = np.where(ok, 0.0, NEG)
    m = np.zeros((L, 4, L))
    for g, w in enumerate(POOL_WINDOWS):
        lo, hi = np.clip(t - w // 2, 0, L), np.clip(t - w // 2 + w, 0, L)
        inside = (t[:, None] >= lo[None, :]) & (t[:, None] < hi[None, :])
        m[:, g, :] = inside / (hi - lo)[None, :] - np.eye(L)
    out["pool"] = m.reshape(2, P, 4, L).transpose(1, 0, 2, 3).reshape(P, -1)
    d = np.arange(3 * P)[None, :] - P - p[:, None]
    out["d_fwd"] = np.maximum(d, 0)
    out["d_bwd"] = np.maximum(-d, 0)
    out["m_fwd"] = (d >= 0) * 1.0
    out["m_bwd"] = (d <= 0) * 1.0
    out["d_cf"] = L + d
    out["d_cb"] = L - d
    return out


def tables_b():
    p = np.arange(P)
    t = np.arange(L)
    out = {}
    out["ident"] = np.eye(P)
    out["ones"] = np.ones((P, P))
    out["headones"] = (p[:, None] // HD == p[None, :] // HD) * 1.0
    out["causal"] = np.where(p[None, :] <= p[:, None], 0.0, NEG)
    same = p[:, None] // CH == p[None, :] // CH
    strict, incl = (same & (p[:, None] < p[None, :])) * 1.0, (same & (p[:, None] <= p[None, :])) * 1.0
    out["chunk_masks"] = np.stack([strict, incl, strict, incl], 1).reshape(P, -1)
    out["strict_low"] = np.stack([strict.T] * 4, 1).reshape(P, -1)
    out["keep"] = np.broadcast_to(np.arange(4 * L) % CH != 0, (P, 4 * L)) * 1.0
    i16 = (10000.0 ** (-np.arange(0, 32, 2, dtype=np.float32) / 32)).astype(np.float32)
    a = t.astype(np.float32)[None, :] * i16[(p % 32) % 16][:, None]
    rows = (p >= 64) & (p < 96)
    out["mla_cos"] = np.where(rows[:, None], np.cos(a), 1.0)
    out["mla_sin"] = np.where(rows[:, None], np.where((p % 32 < 16)[:, None], -np.sin(a), np.sin(a)), 0.0)
    out["mla_swap"] = ((p[:, None] == (p ^ 16)[None, :]) & rows[:, None]) * 1.0
    i32 = (10000.0 ** (-np.arange(0, 64, 2, dtype=np.float32) / 64)).astype(np.float32)
    a = t.astype(np.float32)[None, :] * i32[(p % 64) % 32][:, None]
    out["full_cos"] = np.cos(a)
    out["full_sin"] = np.where((p % 64 < 32)[:, None], -np.sin(a), np.sin(a))
    out["full_swap"] = (p[:, None] == (p ^ 32)[None, :]) * 1.0
    out["row"] = ((p[:, None, None] == np.arange(8)[None, :, None]) * np.ones((1, 1, P))).reshape(P, -1)
    out["before"] = (p[:, None] < p[None, :]) * 1.0
    out["slot_no"] = np.broadcast_to(np.arange(128.0), (P, P))
    out["expert_no"] = np.broadcast_to(np.arange(8.0), (P, 8))
    return out


def packed(tables):
    at, parts, n = {}, [], 0
    for name, v in tables.items():
        v = np.ascontiguousarray(v, np.float32)
        at[name] = (n, v.shape[1])
        parts.append(v)
        n += v.shape[1]
    return np.concatenate(parts, 1), at


VECTORS = [
    ("c", 1, D), ("c_ctx", 1, D), ("b_mod", 2, 6 * D), ("norm1_g", 2, D), ("norm2_g", 2, D), ("pool_scale", 2, 256),
    ("ret_gn_g", 2, 384), ("conv_w", 6, 2 * FF), ("conv_b", 2, 2 * FF), ("final_g", 1, D), ("norm_mix_0_2", 1, D),
    ("shift_mu_0_2", 1, 1792), ("rw_w0_0_2", 1, 512), ("rw_a0_0_2", 1, 512), ("rw_kk_0_2", 1, 512),
    ("rw_ka_0_2", 1, 512), ("rw_rk_0_2", 1, 512), ("rw_lnx_g_0_2", 1, 512), ("rw_lnx_b_0_2", 1, 512),
    ("mla_qnorm_0_2", 1, 256), ("mla_kvnorm_0_2", 1, 128), ("norm_ffn_0_2", 1, D), ("norm_mix_1_2", 1, D),
    ("norm_ffn_1_2", 1, D), ("final_norm_2", 1, D),
]
SPREAD = [("ret_decay_fwd", 12), ("ret_decay_bwd", 12)]


def vector_places():
    at, n = {}, 0
    for name, rows, width in VECTORS:
        at[name] = n
        n += rows * width // P
    for name, width in SPREAD:
        at[name] = n
        n += width
    at["fox_bf_1_2"] = n
    return at, n + 1


def slabs():
    out = []

    def cols(w, layer, lists, kt=KD):
        for c in lists:
            out.append((w, layer, kt, c))

    def r(a, n):
        return [(a, n)]

    for l in range(2):
        cols("w_mod", l, [r(512 * i, 512) for i in range(12)])
        cols("w_in", l, [r(0, 256)] + [r(256 + 384 * i, 384) for i in range(7)])
        cols("w_out", l, [r(512 * i, 512) for i in range(2)])
        cols("w_up", l, [[(256 * i, 256), (FF + 256 * i, 256)] for i in range(KF // 2)])
        cols("w_down", l, [r(P * i, P) for i in range(KD)], KF)
    cols("w_in_0_2", None, [r(512 * i, 512) for i in range(4)] + [r(2048, 160)])
    out.append(("lora", None, 0, None))
    cols("w_out_0_2", None, [r(512 * i, 512) for i in range(2)])
    for i in range(KF // 2):
        out.append(("ffn_gu", None, KD, [(256 * i, 256)]))
    cols("ffn_wd_0_2", None, [r(P * i, P) for i in range(KD)], KF)
    cols("w_in_1_2", None, [r(512 * i, 512) for i in range(3)] + [r(1544 + 512 * i, 512) for i in range(3)] + [r(1536, 8)])
    cols("w_out_1_2", None, [r(512 * i, 512) for i in range(2)])
    cols("router_1_2", None, [r(0, 8)])
    for e in range(NE):
        for i in range(FE // FC):
            out.append(("moe_wg_1_2", e, KD, [(FC * i, FC)]))
            out.append(("moe_wu_1_2", e, KD, [(FC * i, FC)]))
        for half in range(2):
            for q in range(4):
                out.append(("moe_down", e, KE // 4, (half, q)))
    return out


LORA = {"wa2": (0, 512), "g2": (512, 512), "wuq": (1024, 1536), "wukv": (2560, 1024)}


def slab_width(s):
    name, _, kt, lists = s
    if name == "moe_down":
        return kt * 512
    if name == "lora":
        return 3584
    n = kt * sum(n for _, n in lists)
    return 2 * n if name == "ffn_gu" else n


def lay_out(x):
    every = slabs()
    stream = np.zeros((len(every), P, SLOT), np.float32)
    for n, (name, layer, kt, lists) in enumerate(every):
        if name == "lora":
            lo = stream[n]
            lo[0:64, 0:512] = x["rw_w2_0_2"]
            lo[64:128, 0:512] = x["rw_a2_0_2"]
            lo[:, 512:1024] = x["rw_g2_0_2"]
            lo[:, 1024:2560] = x["mla_wuq_0_2"].reshape(2, P, 768).transpose(1, 0, 2).reshape(P, -1)
            lo[:, 2560:3584] = x["mla_wukv_0_2"]
            continue
        if name == "moe_down":
            half, q = lists
            w = x["moe_wd_1_2"][layer, kt * P * q:kt * P * (q + 1), 512 * half:512 * half + 512]
            stream[n, :, :kt * 512] = w.reshape(kt, P, 512).transpose(1, 0, 2).reshape(P, -1)
            continue
        if name == "ffn_gu":
            ws = [x["ffn_wg_0_2"], x["ffn_wu_0_2"]]
        else:
            ws = [x[name] if layer is None else x[name][layer]]
        parts = [w[:, a:a + m] for w in ws for a, m in lists]
        m = sum(w.shape[1] for w in parts)
        v = stream[n, :, :kt * m].reshape(P, kt, m)
        at = 0
        for w in parts:
            v[:, :, at:at + w.shape[1]] = w.reshape(kt, P, -1).transpose(1, 0, 2)
            at += w.shape[1]
    at, n = vector_places()
    vec = np.zeros((P, n), np.float32)
    for name, rows, width in VECTORS:
        k = rows * width // P
        vec[:, at[name]:at[name] + k] = np.ascontiguousarray(x[name]).reshape(k, P).T
    for name, width in SPREAD:
        vec[:, at[name]:at[name] + width] = np.ascontiguousarray(x[name]).reshape(1, width)
    vec[0:8, at["fox_bf_1_2"]] = x["fox_bf_1_2"]
    tok = np.concatenate([x["x"][0], x["ctx"][0]], 0)
    hT = np.ascontiguousarray(tok.reshape(T2, KD, P).transpose(2, 1, 0))
    pw = np.zeros((P, 2, 4, 64), np.float32)
    pw[0:64] = x["pool_w"].transpose(2, 0, 1, 3)
    pw[64:128] = pw[0:64]
    q = np.arange(L)
    dr = (q[None, :] // GRID_W) - (q[:, None] // GRID_W) + NA_KH - 1
    dc = np.clip((q[None, :] % GRID_W) - (q[:, None] % GRID_W) + NA_KW - 1, 0, 2 * NA_KW - 2)
    rpb = np.ascontiguousarray(x["na_rpb"][:, :, dr, dc].reshape(2, NAH, 2, P, L).transpose(0, 3, 1, 2, 4))
    return {"stream": stream, "vec": vec, "h0": hT, "pool_w": pw, "rpb": rpb.reshape(2, P, NAH * 2 * L),
            "tab_a": packed(tables_a())[0], "tab_b": packed(tables_b())[0]}


SEMAPHORES = (
    "act_attention", "dve_attention", "pe_attention", "act_delta", "dve_delta", "pe_delta", "act_experts",
    "dve_experts", "pe_experts", "act_feedforward", "dve_feedforward", "pe_feedforward", "act_first", "dve_first",
    "pe_first", "act_latent", "dve_latent", "pe_latent", "act_modulation", "dve_modulation", "pe_modulation",
    "act_norm", "dve_norm", "pe_norm", "dve_over", "act_pooling", "pe_pooling", "act_projection", "dve_projection",
    "pe_projection", "dve_residual", "pe_residual", "act_result", "pe_result", "act_retention", "dve_retention",
    "pe_retention", "pool_retention", "dve_round", "act_routing", "dve_routing", "pe_routing", "dve_start",
)


class Program:

    def __init__(self, nc, io, earlier, stop=None):
        self.nc, self.io, self.earlier, self.now = nc, io, earlier, {}
        self.stop = stop
        self.bank_of, self.users = {}, {}
        self.turn = {"short": 0, "long": 0}

    def count(self, sem, key=None):
        self.counts[sem] += 1
        if key is not None:
            self.also(sem, key)

    def also(self, sem, key):
        self.now[key] = (sem, self.counts[sem])

    def at(self, *key):
        return self.earlier[key if len(key) > 1 else key[0]][1] if self.earlier else 1

    def moment(self, key):
        name, value = self.earlier[key] if self.earlier else ("dve_start", 1)
        return self.s[name], value

    def per(self, sem):
        return self.earlier.get(("per", sem), 1)

    def enter(self, sem):
        self.counts[sem] += self.per(sem)
        self.entered = (sem, self.counts[sem])

    def leave(self):
        sem, start = self.entered
        self.now[("per", sem)] = self.counts[sem] - start

    def use_of(self, i):
        if i < 2 * FE // FC:
            return (("gate", "up")[i % 2], i // 2)
        return ("down", (i - 2 * FE // FC) // 4, (i - 2 * FE // FC) % 4)

    def so_far(self, sem):
        return self.counts[sem]

    def sb(self, name, *shape):
        return self.ctx.enter_context(self.nc.sbuf_tensor(name, [P, *shape], F32))

    def next_bank(self, kind):
        banks = range(0, 6) if kind == "short" else range(6, 8)
        return banks[self.turn[kind] % len(banks)]

    def bank_free(self, kind="short"):
        b = self.next_bank(kind)
        return self.moment(("free", self.users[b]) if b in self.users else "eps")

    def open(self, key, kind="short"):
        b = self.next_bank(kind)
        self.turn[kind] += 1
        self.users[b] = key
        self.bank_of[key] = b
        self.now[("bank", key)] = b
        return self.psum[b]

    def bank(self, key):
        return self.psum[self.earlier.get(("bank", key), 0)]

    def next_weights(self):
        n = self.next_slab
        self.next_slab += 1
        return n, self.ring[:, n % RING, :]

    def v(self, name, i=0):
        a = self.vec_at[name] + i
        return self.vec[:, a:a + 1]

    def tab(self, name):
        a, n = self.tab_at[name]
        return self.tabs[:, a:a + n]


def mm(pe, out, lhsT, rhs, start=True, stop=True):
    return pe.matmul(out, lhsT, rhs, start=start, stop=stop)


def loads_sp(g, sp):
    for n, s in enumerate(g.slabs):
        if s[0] == "moe_wg_1_2":
            break
        if n >= RING:
            sp.wait_ge(*g.moment(("used", n - RING)))
        w = slab_width(s)
        sp.dma_start(g.ring[:, n % RING, 0:w], g.io["stream"][n, :, 0:w]).then_inc(g.slab_in[n % RING], 16)


def consts_act(g, act):
    for name, dst in (("vec", g.vec[:, :]), ("h0", g.hT[:, :, :]), ("tab_a", g.tabs[:, 0:g.io["tab_a"].shape[1]]),
                      ("pool_w", g.pool_w[:, :, :, :])):
        act.dma_start(dst, g.io[name]).then_inc(g.const_in[name], 16)
        g.const_issued.append(name)


def silu_act(g, act):
    act.wait_ge(g.const_in["vec"], 16)
    for i, n in enumerate(("c", "c_ctx")):
        a = g.vec_at[n]
        act.activation(g.cs[:, :, i], g.vec[:, a:a + KD], ACT.Silu).then_inc(g.s["act_modulation"], 1)
        g.count("act_modulation", ("silu_c", i))


def mod_pe(g, pe, l):
    pe.wait_ge(g.s["act_modulation"], g.at("silu_c", 0))
    pe.wait_ge(g.s["act_modulation"], g.at("silu_c", 1))
    for i in range(12):
        n, w = g.next_weights()
        pe.wait_ge(g.slab_in[n % RING], 16 * (n // RING + 1))
        w = w.rearrange("p (k c) -> p k c", k=KD)
        pe.wait_ge(*g.bank_free())
        ps = g.open(("mod", l, i))
        for j in range(4):
            for k in range(KD):
                last = mm(pe, ps[:, 2 * j:2 * j + 2], w[:, k, P * j:P * j + P], g.cs[:, k, :], k == 0, k == KD - 1)
        last.then_inc(g.s["pe_modulation"], 1)
        g.count("pe_modulation", ("used", n))
        g.also("pe_modulation", ("mm", "mod", l, i))


def mod_dve(g, dve, l):
    dve.wait_ge(g.const_in["vec"], 16)
    a = g.vec_at["b_mod"] + 48 * l
    for i in range(12):
        dve.wait_ge(g.s["pe_modulation"], g.at("mm", "mod", l, i))
        ps = g.bank(("mod", l, i))[:, 0:8].rearrange("p (c s) -> p c s", s=2)
        b = g.vec[:, a + 4 * i:a + 4 * i + 4].unsqueeze(2).broadcast_to((P, 4, 2))
        dve.tensor_tensor(g.mod[:, l, 4 * i:4 * i + 4, :], ps, b, ALU.add).then_inc(g.s["dve_modulation"], 1)
        g.count("dve_modulation", ("free", ("mod", l, i)))
    dve.wait_ge(g.s["dve_modulation"], g.so_far("dve_modulation"))
    for n, (name, c) in enumerate((("norm1_g", 8), ("norm2_g", 32))):
        a = g.vec_at[name] + KD * l
        gain = g.vec[:, a:a + KD].unsqueeze(2).broadcast_to((P, KD, 2))
        dve.scalar_tensor_tensor(g.gain[:, l, n, :, :], g.mod[:, l, c:c + KD, :], 1.0, gain,
                                            ALU.add, ALU.mult).then_inc(g.s["dve_modulation"], 1)
        g.count("dve_modulation", ("gain", l, n))


def norm_act(g, act, key, src, T, scales, shifts, ready):
    for moment in ready:
        act.wait_ge(*g.moment(moment))
    for k in range(KD):
        act.activation(g.aT[:, k, 0:T], src[:, k, 0:T], ACT.Square).then_inc(g.s["act_norm"], 1)
        g.count("act_norm", ("square", key, k))
    act.wait_ge(g.s["pe_norm"], g.at("mm", "sumsq", key))
    act.activation(g.rstd[:, 0:T], g.bank(("sumsq", key))[:, 0:T], ACT.Sqrt, bias=g.eps[:, 0:1],
                              scale=1.0 / D).then_inc(g.s["act_norm"], 1)
    g.count("act_norm", ("free", ("sumsq", key)))
    if shifts is not None:
        for k in range(KD):
            act.wait_ge(g.s["dve_norm"], g.at("normed", key, k))
            for s in range(T // L):
                c = slice(L * s, L * s + L)
                act.activation(g.aT[:, k, c], g.aT[:, k, c], ACT.Identity, bias=shifts(k, s),
                                          scale=scales(k, s)).then_inc(g.s["act_norm"], 1)
                g.count("act_norm", ("aT", key))


def norm_pe(g, pe, key, T):
    pe.wait_ge(*g.bank_free())
    ps = g.open(("sumsq", key))
    for k in range(KD):
        pe.wait_ge(g.s["act_norm"], g.at("square", key, k))
        last = mm(pe, ps[:, 0:T], g.tab("ones"), g.aT[:, k, 0:T], k == 0, k == KD - 1)
    last.then_inc(g.s["pe_norm"], 1)
    g.count("pe_norm", ("mm", "sumsq", key))


def norm_dve(g, dve, key, src, T, scales, shifts, dst=None):
    dve.wait_ge(g.s["act_norm"], g.at("free", ("sumsq", key)))
    dve.reciprocal(g.rstd[:, 0:T], g.rstd[:, 0:T]).then_inc(g.s["dve_norm"], 1)
    g.count("dve_norm")
    dve.wait_ge(g.s["dve_norm"], g.so_far("dve_norm"))
    dst = g.aT if dst is None else dst
    for k in range(KD):
        if shifts is not None:
            dve.tensor_tensor(dst[:, k, 0:T], src[:, k, 0:T], g.rstd[:, 0:T], ALU.mult).then_inc(g.s["dve_norm"], 1)
            g.count("dve_norm", ("normed", key, k))
        else:
            dve.scalar_tensor_tensor(dst[:, k, 0:T], src[:, k, 0:T], scales(k, 0), g.rstd[:, 0:T],
                                                ALU.mult, ALU.mult).then_inc(g.s["dve_norm"], 1)
            g.count("dve_norm", ("aT", key))


def units_of(heads, qts=2):
    return [(h, q) for h in range(heads) for q in range(qts)]


def attn_pe(g, pe, name, a):
    for moment in a["ready"]:
        pe.wait_ge(*g.moment(moment))
    us = units_of(a["heads"])
    n = len(us)
    for i in range(n + 2):
        if i < n:
            h, q = us[i]
            pe.wait_ge(*g.bank_free())
            ps = g.open(("S", name, i))
            for col, pairs in a["scores"](h, q):
                for m, (x, y) in enumerate(pairs):
                    w = y.shape[-1]
                    last = mm(pe, ps[:, col:col + w], x, y, m == 0, m == len(pairs) - 1)
            last.then_inc(g.s["pe_attention"], 1)
            g.count("pe_attention", ("mm", "S", name, i))
        if 1 <= i <= n:
            j = i - 1
            pe.wait_ge(g.s["dve_attention"], g.at("P", name, j))
            pe.wait_ge(*g.bank_free())
            ps = g.open(("T", name, j))
            for t in range(a["width"](us[j][1]) // P):
                last = pe.transpose(ps[:, P * t:P * t + P], g.probs[:, j % 3, P * t:P * t + P], g.tab("ident"))
            last.then_inc(g.s["pe_attention"], 1)
            g.count("pe_attention", ("mm", "T", name, j))
        if i >= 2:
            j = i - 2
            h, q = us[j]
            pair = ("O", name, h // 2)
            if h % 2 == 0 and q == 0:
                pe.wait_ge(*g.bank_free("long"))
                g.open(pair, "long")
            ps = g.psum[g.bank_of[pair]]
            pe.wait_ge(g.s["act_attention"], g.at("PT", name, j))
            nt = a["width"](q) // P
            r = slice(HD * (h % 2), HD * (h % 2) + HD)
            for t in range(nt):
                last = mm(pe, ps[r, P * q:P * q + P], a["values"](h, t), g.probsT[:, j % 3, P * t:P * t + P],
                          t == 0, t == nt - 1)
            last.then_inc(g.s["pe_attention"], 1)
            g.count("pe_attention", ("mm", "PV", name, j))


def attn_dve(g, dve, name, a):
    us = units_of(a["heads"])
    n = len(us)
    for i in range(n + 1):
        if i < n:
            h, q = us[i]
            ps = g.bank(("S", name, i))
            dve.wait_ge(g.s["pe_attention"], g.at("mm", "S", name, i))
            for col, extra in a["add"](h, q):
                w = extra.shape[-1]
                dve.tensor_tensor(ps[:, col:col + w], ps[:, col:col + w], extra, ALU.add).then_inc(g.s["dve_attention"], 1)
                g.count("dve_attention")
                dve.wait_ge(g.s["dve_attention"], g.so_far("dve_attention"))
            dve.tensor_reduce(g.nmax[:, i % 4:i % 4 + 1], ps[:, 0:a["width"](q)], AX.X, ALU.max,
                                         negate=True).then_inc(g.s["dve_attention"], 1)
            g.count("dve_attention", ("nmax", name, i))
        if i >= 1:
            j = i - 1
            w = a["width"](us[j][1])
            dve.wait_ge(g.s["act_attention"], g.at("exp", name, j))
            dve.reciprocal(g.rinv[:, j % 4:j % 4 + 1], g.rsum[:, j % 4:j % 4 + 1]).then_inc(g.s["dve_attention"], 1)
            g.count("dve_attention")
            dve.wait_ge(g.s["dve_attention"], g.so_far("dve_attention"))
            dve.tensor_scalar(g.probs[:, j % 3, 0:w], g.probs[:, j % 3, 0:w], g.rinv[:, j % 4:j % 4 + 1],
                                         None, ALU.mult).then_inc(g.s["dve_attention"], 1)
            g.count("dve_attention", ("P", name, j))


def attn_act(g, act, name, a):
    us = units_of(a["heads"])
    n = len(us)
    for i in range(n + 2):
        if i < n:
            w = a["width"](us[i][1])
            act.wait_ge(g.s["dve_attention"], g.at("nmax", name, i))
            if i >= 3:
                act.wait_ge(g.s["pe_attention"], g.at("mm", "T", name, i - 3))
            act.activation(g.probs[:, i % 3, 0:w], g.bank(("S", name, i))[:, 0:w], ACT.Exp,
                                      bias=g.nmax[:, i % 4:i % 4 + 1], accum_out=g.rsum[:, i % 4:i % 4 + 1]).then_inc(g.s["act_attention"], 1)
            g.count("act_attention", ("exp", name, i))
            g.also("act_attention", ("free", ("S", name, i)))
        if i >= 1 and i <= n:
            j = i - 1
            w = a["width"](us[j][1])
            act.wait_ge(g.s["pe_attention"], g.at("mm", "T", name, j))
            if j >= 3:
                act.wait_ge(g.s["pe_attention"], g.at("mm", "PV", name, j - 3))
            act.activation(g.probsT[:, j % 3, 0:w], g.bank(("T", name, j))[:, 0:w], ACT.Copy).then_inc(g.s["act_attention"], 1)
            g.count("act_attention", ("PT", name, j))
            g.also("act_attention", ("free", ("T", name, j)))
        if i >= 2:
            j = i - 2
            h, q = us[j]
            if h % 2 and q == 1:
                act.wait_ge(g.s["pe_attention"], g.at("mm", "PV", name, j))
                act.activation(a["out"](h // 2), g.bank(("O", name, h // 2))[:, 0:L], ACT.Copy).then_inc(g.s["act_attention"], 1)
                g.count("act_attention", ("free", ("O", name, h // 2)))
    g.also("act_attention", ("attended", name))




T_BLOCKS = ("naq", "nak", "rq", "rk", "gate")
IN_ORDER = ("naq", "nak", "nav", "rq", "rk", "rv", "gate")


def proj_T(l, name):
    return T2 if l == 0 or name in ("nak", "rk", "nav", "rv") else L


def proj_pe(g, pe, l):
    pe.wait_ge(g.s["act_norm"], g.at("aT", ("n1", l)))
    n, w = g.next_weights()
    pe.wait_ge(g.slab_in[n % RING], 16 * (n // RING + 1))
    for t in range(proj_T(l, "pool") // P):
        pe.wait_ge(*g.bank_free())
        ps = g.open(("pool", l, t))
        for k in range(KD):
            last = mm(pe, ps[:, 0:256], g.aT[:, k, P * t:P * t + P], w[:, 256 * k:256 * k + 256], k == 0, k == KD - 1)
        last.then_inc(g.s["pe_projection"], 1)
        g.count("pe_projection", ("mm", "pool", l, t))
    g.also("pe_projection", ("used", n))
    for name in IN_ORDER:
        n, w = g.next_weights()
        pe.wait_ge(g.slab_in[n % RING], 16 * (n // RING + 1))
        T = proj_T(l, name)
        if name in T_BLOCKS:
            for j in range(3):
                pe.wait_ge(*g.bank_free())
                ps = g.open((name, l, j))
                for k in range(KD):
                    a = 384 * k + P * j
                    last = mm(pe, ps[:, 0:T], w[:, a:a + P], g.aT[:, k, 0:T], k == 0, k == KD - 1)
                last.then_inc(g.s["pe_projection"], 1)
                g.count("pe_projection", ("mm", name, l, j))
        else:
            for t in range(T // P):
                pe.wait_ge(*g.bank_free())
                ps = g.open((name, l, t))
                for k in range(KD):
                    last = mm(pe, ps[:, 0:384], g.aT[:, k, P * t:P * t + P], w[:, 384 * k:384 * k + 384],
                              k == 0, k == KD - 1)
                last.then_inc(g.s["pe_projection"], 1)
                g.count("pe_projection", ("mm", name, l, t))
        g.also("pe_projection", ("used", n))
    for name in ("rq", "rk"):
        for j in range(3):
            pe.wait_ge(*g.moment(("raw", name, l, j)))
            pe.wait_ge(*g.bank_free())
            ps = g.open(("swap", name, l, j))
            mm(pe, ps[:, 0:L], g.tab("rot_swap"), g.m1[name][:, j, 0:L]).then_inc(g.s["pe_projection"], 1)
            g.count("pe_projection", ("mm", "swap", name, l, j))


def proj_act(g, act, l):
    for t in range(proj_T(l, "pool") // P):
        act.wait_ge(g.s["pe_projection"], g.at("mm", "pool", l, t))
        act.activation(g.m1["pool"][:, t, :], g.bank(("pool", l, t))[:, 0:256], ACT.Copy).then_inc(g.s["act_projection"], 1)
        g.count("act_projection", ("free", ("pool", l, t)))
    g.also("act_projection", ("have", "pool", l))
    for name in ("naq", "nav", "rq", "rv", "gate"):
        T = proj_T(l, name)
        for j in range(3 if name in T_BLOCKS else T // P):
            act.wait_ge(g.s["pe_projection"], g.at("mm", name, l, j))
            n = T if name in T_BLOCKS else 384
            f, scale = (ACT.Silu, 1.0) if name == "gate" else (ACT.Copy, HD ** -0.5 if name == "naq" else 1.0)
            act.activation(g.m1[name][:, j, 0:n], g.bank((name, l, j))[:, 0:n], f, scale=scale).then_inc(g.s["act_projection"], 1)
            g.count("act_projection", ("free", (name, l, j)))
            g.also("act_projection", ("raw", name, l, j))
        g.also("act_projection", ("have", name, l))


def proj_dve(g, dve, l):
    dve.wait_ge(g.const_in["tab_a"], 16)
    for name in ("nak", "rk"):
        for j in range(3):
            dve.wait_ge(g.s["pe_projection"], g.at("mm", name, l, j))
            s = HD ** -0.5 if name == "rk" else 1.0
            dve.tensor_scalar(g.m1[name][:, j, :], g.bank((name, l, j))[:, :], s, None, ALU.mult).then_inc(g.s["dve_projection"], 1)
            g.count("dve_projection", ("free", (name, l, j)))
            g.also("dve_projection", ("raw", name, l, j))
        g.also("dve_projection", ("have", name, l))
    for name in ("rq", "rk"):
        for j in range(3):
            x = g.m1[name][:, j, 0:L]
            dve.wait_ge(g.s["pe_projection"], g.at("mm", "swap", name, l, j))
            dve.tensor_tensor(g.tmp[:, 0:L], g.bank(("swap", name, l, j))[:, 0:L], g.tab("rot_sin"), ALU.mult).then_inc(g.s["dve_projection"], 1)
            g.count("dve_projection", ("free", ("swap", name, l, j)))
            dve.tensor_tensor(x, x, g.tab("rot_cos"), ALU.mult).then_inc(g.s["dve_projection"], 1)
            g.count("dve_projection")
            dve.wait_ge(g.s["dve_projection"], g.so_far("dve_projection"))
            dve.tensor_tensor(x, x, g.tmp[:, 0:L], ALU.add).then_inc(g.s["dve_projection"], 1)
            g.count("dve_projection", ("rotated", name, l, j))
            dve.wait_ge(g.s["dve_projection"], g.so_far("dve_projection"))


def pool_pe(g, pe, l):
    pe.wait_ge(g.const_in["tab_a"], 16)
    pe.wait_ge(g.const_in["pool_w"], 16)
    pe.wait_ge(g.s["act_projection"], g.at("have", "pool", l))
    segs = proj_T(l, "pool") // L
    band = g.tab("pool").rearrange("p (s g t) -> p s g t", s=2, g=4)
    for s in range(segs):
        pe.wait_ge(*g.bank_free())
        ps = g.open(("band", l, s))
        for q in range(4):
            r = slice(HD * (q % 2), HD * (q % 2) + HD)
            for t in range(2):
                last = mm(pe, ps[r, L * (q // 2):L * (q // 2) + L], g.m1["pool"][:, 2 * s + t, HD * q:HD * q + HD],
                          band[:, t, q, :], t == 0, t == 1)
        last.then_inc(g.s["pe_pooling"], 1)
        g.count("pe_pooling", ("mm", "band", l, s))
    for s in range(segs):
        pe.wait_ge(g.s["act_pooling"], g.at("banded", l, s))
        for odd in range(2):
            pe.wait_ge(*g.bank_free())
            ps = g.open(("pooled", l, s, odd))
            r = slice(HD * odd, HD * odd + HD)
            for q in (odd, 2 + odd):
                c = slice(L * (q // 2), L * (q // 2) + L)
                last = mm(pe, ps[r, c], g.pool_w[r, l, q, :], g.banded[r, s, c])
            last.then_inc(g.s["pe_pooling"], 1)
            g.count("pe_pooling", ("mm", "pooled", l, s, odd))


def pool_act(g, act, l):
    segs = proj_T(l, "pool") // L
    for s in range(segs):
        act.wait_ge(g.s["pe_pooling"], g.at("mm", "band", l, s))
        act.activation(g.banded[:, s, :], g.bank(("band", l, s))[:, :], ACT.Copy).then_inc(g.s["act_pooling"], 1)
        g.count("act_pooling", ("banded", l, s))
        g.also("act_pooling", ("free", ("band", l, s)))
    for s in range(segs):
        for odd in range(2):
            act.wait_ge(g.s["pe_pooling"], g.at("mm", "pooled", l, s, odd))
            r = slice(HD * odd, HD * odd + HD)
            for j in range(2):
                act.activation(g.aT[r, j, L * s:L * s + L], g.bank(("pooled", l, s, odd))[r, L * j:L * j + L],
                                          ACT.Copy, scale=g.v("pool_scale", 2 * l + j)[r, :]).then_inc(g.s["act_pooling"], 1)
                g.count("act_pooling", ("free", ("pooled", l, s, odd)))
    g.also("act_pooling", ("y pool", l))


def na_of(g, l):
    m = g.m1

    def half(h):
        return slice(HD * (h % 2), HD * (h % 2) + HD)

    def scores(h, q):
        x = m["naq"][half(h), h // 2, P * q:P * q + P]
        k = m["nak"]
        return [(0, [(x, k[half(h), h // 2, 0:L])]), (L, [(x, k[half(h), h // 2, L:T2])])]

    return dict(heads=NAH, scores=scores, width=lambda q: T2, out=lambda p: g.aT[:, 2 + p, 0:L],
                     add=lambda h, q: [(0, g.bias[:, 2 * h + q, :])], ready=[("have", "naq", l), ("have", "nak", l),
                     ("have", "nav", l)], values=lambda h, t: m["nav"][:, t, HD * h:HD * h + HD])


def ctx_attn_of(g, l):
    m = g.m1

    def half(h):
        return slice(HD * (h % 2), HD * (h % 2) + HD)

    def scores(h, q):
        return [(0, [(m["naq"][half(h), h // 2, L + P * q:L + P * q + P], m["nak"][half(h), h // 2, L:T2])])]

    return dict(heads=NAH, scores=scores, width=lambda q: L, out=lambda p: g.aT[:, 2 + p, L:T2],
                     add=lambda h, q: [], ready=[("have", "naq", l)],
                     values=lambda h, t: m["nav"][:, 2 + t, HD * h:HD * h + HD])


def bias_act(g, act, l):
    if l:
        act.wait_ge(g.s["dve_retention"], g.at("y ret", l - 1))
    act.dma_start(g.bias_flat, g.io["rpb"][l]).then_inc(g.bias_in, 16)
    g.biases += 1


def bias_dve(g, dve, l):
    dve.wait_ge(g.bias_in, 16 * (l + 1))
    m = g.tab("na_mask").unsqueeze(1).broadcast_to((P, 2 * NAH, L))
    dve.tensor_tensor(g.bias[:, :, :], g.bias[:, :, :], m, ALU.add).then_inc(g.s["dve_attention"], 1)
    g.count("dve_attention")
    dve.wait_ge(g.s["dve_attention"], g.so_far("dve_attention"))


def shifted(g, table):
    v = table.rearrange("p (a b) -> p a b", a=3)[:, 0:2, :]
    ap = [list(x) for x in v.ap]
    assert ap[-2] == [P, 2] or tuple(ap[-2]) == (P, 2), ap
    ap[-1] = [1, L]
    return bass.AP(v.tensor, v.offset, ap)


def ret_act(g, act, l):
    for h in range(RETH):
        if h:
            act.wait_ge(g.s["pool_retention"], g.at("decays", l, h - 1))
        e = g.ret_e
        for n, (table, lg) in enumerate((("d_fwd", "ret_decay_fwd"), ("d_bwd", "ret_decay_bwd"),
                                         ("d_cf", "ret_decay_fwd"), ("d_cb", "ret_decay_bwd"))):
            act.activation(e[:, n, :], g.tab(table), ACT.Exp, scale=g.v(lg, RETH * l + h)).then_inc(g.s["act_retention"], 1)
            g.count("act_retention", ("powers", l, h))
        if h >= 2 and h % 2 == 0:
            ret_out(g, act, l, h // 2 - 1)
    ret_out(g, act, l, RETH // 2 - 1)
    T = T2 if l == 0 else L
    for j in range(3):
        act.wait_ge(g.s["dve_retention"], g.at("centred", l, j))
        act.activation(g.m1["nak"][:, j, 0:T], g.m1["naq"][:, j, 0:T], ACT.Square).then_inc(g.s["act_retention"], 1)
        g.count("act_retention", ("gn sq", l, j))
    for j in range(3):
        act.wait_ge(g.s["pe_retention"], g.at("mm", "gn var", l, j))
        act.activation(g.m1["nak"][:, j, 0:T], g.bank(("gn var", l, j))[:, 0:T], ACT.Sqrt,
                                  bias=g.eps[:, 0:1], scale=1.0 / HD).then_inc(g.s["act_retention"], 1)
        g.count("act_retention", ("free", ("gn var", l, j)))


def ret_out(g, act, l, j):
    T = T2 if l == 0 else L
    act.wait_ge(g.s["pe_retention"], g.at("mm", "ro", l, j))
    act.activation(g.m1["naq"][:, j, 0:T], g.bank(("ro", l, j))[:, 0:T], ACT.Copy).then_inc(g.s["act_retention"], 1)
    g.count("act_retention", ("free", ("ro", l, j)))


def ret_pool(g, pool, l):
    pool.wait_ge(g.const_in["tab_a"], 16)
    for h in range(RETH):
        e, f = g.ret_e, g.ret_f[:, h % 2]
        pool.wait_ge(g.s["act_retention"], g.at("powers", l, h))
        pool.tensor_tensor(e[:, 0, :], e[:, 0, :], g.tab("m_fwd"), ALU.mult).then_inc(g.s["pool_retention"], 1)
        g.count("pool_retention")
        pool.tensor_tensor(e[:, 1, :], e[:, 1, :], g.tab("m_bwd"), ALU.mult).then_inc(g.s["pool_retention"], 1)
        g.count("pool_retention")
        pool.wait_ge(g.s["pool_retention"], g.so_far("pool_retention"))
        if h >= 2:
            pool.wait_ge(g.s["dve_retention"], g.at("decayed", l, h - 2))
        elif l:
            pool.wait_ge(g.s["dve_retention"], g.at("decayed", l - 1, RETH - 2 + h))
        pool.tensor_tensor(f[:, 0, :], e[:, 0, :], e[:, 1, :], ALU.add).then_inc(g.s["pool_retention"], 1)
        g.count("pool_retention")
        pool.tensor_tensor(f[:, 1, :], e[:, 2, :], e[:, 3, :], ALU.add).then_inc(g.s["pool_retention"], 1)
        g.count("pool_retention", ("decays", l, h))


def ret_parts(l):
    return [(0, 0, 0), (0, L, 1)] + ([(L, L, 0)] if l == 0 else [])


def ret_pe(g, pe, l):
    pe.wait_ge(g.s["dve_projection"], g.at("rotated", "rk", l, 2))
    pe.wait_ge(g.s["act_projection"], g.at("have", "rv", l))
    pe.wait_ge(g.s["act_projection"], g.at("have", "gate", l))
    parts = ret_parts(l)
    n = RETH * len(parts)
    m = g.m1

    def scores(i):
        h, (q0, k0, _) = i // len(parts), parts[i % len(parts)]
        r = slice(HD * (h % 2), HD * (h % 2) + HD)
        pe.wait_ge(*g.bank_free())
        ps = g.open(("rs", l, i))
        for s in range(2):
            kt = k0 + P * (1 - s)
            last = mm(pe, ps[:, L * s:L * s + L], m["rk"][r, h // 2, kt:kt + P], m["rq"][r, h // 2, q0:q0 + L])
        last.then_inc(g.s["pe_retention"], 1)
        g.count("pe_retention", ("mm", "rs", l, i))

    def outputs(i):
        h, p = i // len(parts), i % len(parts)
        q0, k0, _ = parts[p]
        r = slice(HD * (h % 2), HD * (h % 2) + HD)
        if h % 2 == 0 and p == 0:
            pe.wait_ge(*g.bank_free("long"))
            g.open(("ro", l, h // 2), "long")
        ps = g.psum[g.bank_of[("ro", l, h // 2)]]
        pe.wait_ge(g.s["dve_retention"], g.at("weighted", l, i))
        for s in range(2):
            first = s == 0 and (q0, k0) != (0, L)
            stop = s == 1 and (q0, k0) != (0, 0)
            last = mm(pe, ps[r, q0:q0 + L], m["rv"][:, k0 // P + 1 - s, HD * h:HD * h + HD],
                      g.ret_a[:, i % 3, L * s:L * s + L], first, stop)
        last.then_inc(g.s["pe_retention"], 1)
        g.count("pe_retention", ("mm", "ro unit", l, i))
        if h % 2 and p == len(parts) - 1:
            g.also("pe_retention", ("mm", "ro", l, h // 2))

    for i in range(n + 2):
        if i < n:
            scores(i)
        if i >= 2:
            outputs(i - 2)
    T = T2 if l == 0 else L
    for what, src in (("gn mean", "naq"), ("gn var", "nak")):
        for j in range(3):
            pe.wait_ge(g.s["act_retention"], g.at(("free", ("ro", l, j)) if what == "gn mean" else ("gn sq", l, j)))
            pe.wait_ge(*g.bank_free())
            ps = g.open((what, l, j))
            mm(pe, ps[:, 0:T], g.tab("headones"), m[src][:, j, 0:T]).then_inc(g.s["pe_retention"], 1)
            g.count("pe_retention", ("mm", what, l, j))


def ret_dve(g, dve, l):
    parts = ret_parts(l)
    for i in range(RETH * len(parts)):
        h, (_, _, table) = i // len(parts), parts[i % len(parts)]
        dve.wait_ge(g.s["pe_retention"], g.at("mm", "rs", l, i))
        dve.wait_ge(g.s["pool_retention"], g.at("decays", l, h))
        if i >= 3:
            dve.wait_ge(g.s["pe_retention"], g.at("mm", "ro unit", l, i - 3))
        dve.tensor_tensor(g.ret_a[:, i % 3, :].rearrange("p (s t) -> p s t", s=2),
                                     g.bank(("rs", l, i))[:, :].rearrange("p (s t) -> p s t", s=2),
                                     shifted(g, g.ret_f[:, h % 2, table, :]), ALU.mult).then_inc(g.s["dve_retention"], 1)
        g.count("dve_retention", ("weighted", l, i))
        g.also("dve_retention", ("free", ("rs", l, i)))
        g.also("dve_retention", ("decayed", l, h))
    T = T2 if l == 0 else L
    y, r = g.m1["naq"], g.m1["nak"]
    for j in range(3):
        dve.wait_ge(g.s["pe_retention"], g.at("mm", "gn mean", l, j))
        dve.scalar_tensor_tensor(y[:, j, 0:T], g.bank(("gn mean", l, j))[:, 0:T], -1.0 / HD, y[:, j, 0:T],
                                            ALU.mult, ALU.add).then_inc(g.s["dve_retention"], 1)
        g.count("dve_retention", ("centred", l, j))
        g.also("dve_retention", ("free", ("gn mean", l, j)))
    for j in range(3):
        dve.wait_ge(g.s["act_retention"], g.at("free", ("gn var", l, j)))
        dve.reciprocal(r[:, j, 0:T], r[:, j, 0:T]).then_inc(g.s["dve_retention"], 1)
        g.count("dve_retention")
        dve.wait_ge(g.s["dve_retention"], g.so_far("dve_retention"))
        dve.tensor_tensor(y[:, j, 0:T], y[:, j, 0:T], r[:, j, 0:T], ALU.mult).then_inc(g.s["dve_retention"], 1)
        g.count("dve_retention")
        dve.wait_ge(g.s["dve_retention"], g.so_far("dve_retention"))
        dve.scalar_tensor_tensor(g.aT[:, 5 + j, 0:T], y[:, j, 0:T], g.v("ret_gn_g", 3 * l + j),
                                            g.m1["gate"][:, j, 0:T], ALU.mult, ALU.mult).then_inc(g.s["dve_retention"], 1)
        g.count("dve_retention", ("y ret", l))
        dve.wait_ge(g.s["dve_retention"], g.so_far("dve_retention"))


def out_pe(g, pe, key, T, ready):
    for moment in ready:
        pe.wait_ge(*g.moment(moment))
    for i in range(2):
        n, w = g.next_weights()
        pe.wait_ge(g.slab_in[n % RING], 16 * (n // RING + 1))
        for j in range(4):
            pe.wait_ge(*g.bank_free())
            ps = g.open(("wo", key, 4 * i + j))
            for k in range(KD):
                a = 512 * k + P * j
                last = mm(pe, ps[:, 0:T], w[:, a:a + P], g.aT[:, k, 0:T], k == 0, k == KD - 1)
            last.then_inc(g.s["pe_residual"], 1)
            g.count("pe_residual", ("mm", "wo", key, 4 * i + j))
        g.also("pe_residual", ("used", n))


def add_dve(g, dve, what, key, T, gate):
    for m in range(KD):
        dve.wait_ge(*g.moment(("mm", what, key, m)))
        ps = g.bank((what, key, m))
        if gate is None:
            dve.tensor_tensor(g.hT[:, m, 0:T], ps[:, 0:T], g.hT[:, m, 0:T], ALU.add).then_inc(g.s["dve_residual"], 1)
            g.count("dve_residual", ("free", (what, key, m)))
        else:
            for s in range(T // L):
                c = slice(L * s, L * s + L)
                dve.scalar_tensor_tensor(g.hT[:, m, c], ps[:, c], gate(m, s), g.hT[:, m, c],
                                                    ALU.mult, ALU.add).then_inc(g.s["dve_residual"], 1)
                g.count("dve_residual", ("free", (what, key, m)))
    g.also("dve_residual", ("h", what, key))


def ffn1_pe(g, pe, l, T):
    pe.wait_ge(g.s["act_norm"], g.at("aT", ("n2", l)))
    for i in range(KF // 2):
        n, w = g.next_weights()
        pe.wait_ge(g.slab_in[n % RING], 16 * (n // RING + 1))
        for j in range(2):
            for ab in range(2):
                pe.wait_ge(*g.bank_free())
                ps = g.open(("up", l, 2 * i + j, ab))
                for k in range(KD):
                    a = 512 * k + 256 * ab + P * j
                    last = mm(pe, ps[:, 0:T], w[:, a:a + P], g.aT[:, k, 0:T], k == 0, k == KD - 1)
                last.then_inc(g.s["pe_feedforward"], 1)
                g.count("pe_feedforward", ("mm", "up", l, 2 * i + j, ab))
        g.also("pe_feedforward", ("used", n))
    down_pe(g, pe, ("dn", l), T, KF, ("hidden", l))


def down_pe(g, pe, key, T, kt, ready):
    for m in range(KD):
        n, w = g.next_weights()
        pe.wait_ge(g.slab_in[n % RING], 16 * (n // RING + 1))
        pe.wait_ge(*g.bank_free())
        ps = g.open((*key, m))
        for k in range(kt):
            if m == 0:
                pe.wait_ge(g.s["dve_feedforward"], g.at(*ready, k))
            last = mm(pe, ps[:, 0:T], w[:, P * k:P * k + P], g.hid[:, k, 0:T], k == 0, k == kt - 1)
        last.then_inc(g.s["pe_feedforward"], 1)
        g.count("pe_feedforward", ("mm", *key, m))
        g.also("pe_feedforward", ("used", n))


def ffn1_act(g, act, l, T):
    for t in range(KF + 1):
        if t < KF:
            for ab in range(2):
                act.wait_ge(g.s["pe_feedforward"], g.at("mm", "up", l, t, ab))
                if t >= 2:
                    act.wait_ge(g.s["dve_feedforward"], g.at("hidden", l, t - 2))
                c = t + KF * ab
                act.activation(g.conv[:, t % 2, ab, 0:T], g.bank(("up", l, t, ab))[:, 0:T], ACT.Identity,
                                          bias=g.v("conv_b", 2 * KF * l + c),
                                          scale=g.v("conv_w", 2 * KF * (3 * l + 1) + c)).then_inc(g.s["act_feedforward"], 1)
                g.count("act_feedforward", ("middle", l, t, ab))
        if t >= 1:
            act.wait_ge(g.s["dve_feedforward"], g.at("conv", l, t - 1, 0))
            act.activation(g.conv[:, (t - 1) % 2, 0, 0:T], g.conv[:, (t - 1) % 2, 0, 0:T], ACT.Silu).then_inc(g.s["act_feedforward"], 1)
            g.count("act_feedforward", ("silu", l, t - 1))


def ffn1_dve(g, dve, l, T):
    for t in range(KF + 1):
        if t < KF:
            for ab in range(2):
                c = t + KF * ab
                ps = g.bank(("up", l, t, ab))[:, 0:T].rearrange("p (s t) -> p s t", t=L)
                u = g.conv[:, t % 2, ab, 0:T].rearrange("p (s t) -> p s t", t=L)
                dve.wait_ge(g.s["act_feedforward"], g.at("middle", l, t, ab))
                dve.scalar_tensor_tensor(u[:, :, 1:L], ps[:, :, 0:L - 1], g.v("conv_w", 2 * KF * 3 * l + c),
                                                    u[:, :, 1:L], ALU.mult, ALU.add).then_inc(g.s["dve_feedforward"], 1)
                g.count("dve_feedforward")
                dve.wait_ge(g.s["dve_feedforward"], g.so_far("dve_feedforward"))
                dve.scalar_tensor_tensor(u[:, :, 0:L - 1], ps[:, :, 1:L],
                                                    g.v("conv_w", 2 * KF * (3 * l + 2) + c), u[:, :, 0:L - 1],
                                                    ALU.mult, ALU.add).then_inc(g.s["dve_feedforward"], 1)
                g.count("dve_feedforward", ("conv", l, t, ab))
                g.also("dve_feedforward", ("free", ("up", l, t, ab)))
        if t >= 1:
            dve.wait_ge(g.s["act_feedforward"], g.at("silu", l, t - 1))
            dve.wait_ge(g.s["dve_feedforward"], g.so_far("dve_feedforward"))
            b = (t - 1) % 2
            dve.tensor_tensor(g.hid[:, t - 1, 0:T], g.conv[:, b, 0, 0:T], g.conv[:, b, 1, 0:T], ALU.mult).then_inc(g.s["dve_feedforward"], 1)
            g.count("dve_feedforward", ("hidden", l, t - 1))


SHIFTED = 14
LN_DECAY = -float(np.exp(-0.5))


def second_places(g):
    b, t = g.big, g.tmp
    g.prj = b[:, 0:SHIFTED * 257].rearrange("p (a b) -> p a b", a=SHIFTED)
    g.lat = g.part(b, 3600, 4, L)
    g.tok = g.part(b, 4624, 4, 512)
    g.lnw, g.cum = g.part(b, 4624, 4, L), g.part(b, 5648, 4, L)
    g.rw_a, g.rw_kk = g.part(b, 6672, 4, L), g.part(b, 7696, 4, L)
    g.nv, g.z, g.wt, g.u = b[:, 6672:7184], b[:, 7184:7696], g.part(b, 7696, 4, P), b[:, 8208:8720]
    g.rw_g = g.part(b, 8720, 4, L)
    g.bt, g.kt = g.part(b, 9744, 4, L), g.part(b, 10768, 4, L)
    g.ar = b[:, 11792:13840].rearrange("p (j t w c) -> p j t w c", j=4, t=2, w=2)
    g.y = g.part(b, 13840, 4, L)
    g.lend = g.cend
    g.mp = g.aT[:, :, :].rearrange("p h (w c) -> p h w c", w=4)
    g.dm, g.fm = g.part(t, 0, 8, P), g.part(t, 1024, 8, P)
    g.states = g.part(t, 2048, 5, L)
    g.w4 = g.part(t, 3328, 4, L)
    g.w4b = g.part(t, 0, 4, L)
    g.w4c = g.part(t, 1024, 4, L)
    g.d14 = g.part(t, 0, SHIFTED, L)
    g.mq, g.mk, g.mv = g.part(b, 9744, 8, L), g.part(b, 11792, 8, L), g.part(b, 13840, 2, 512)
    g.rope8 = g.part(b, 0, 8, L)
    g.hid2 = g.part(b, 0, KE, L)
    g.gate2 = g.part(t, 0, 4, L)
    g.q2 = {n: g.part(b, 1024 * i, 4, L) for i, n in enumerate(("fq", "fk", "mq", "mk"))}
    g.q2.update({n: g.part(b, 4096 + 1024 * i, 2, 512) for i, n in enumerate(("fv", "mv"))})
    g.negd, g.lsig = b[:, 6144:6400], b[:, 6400:6656]
    g.oneb = b[:, 6656:6912]
    g.t_tok, g.hb, g.hT2 = g.part(b, 0, 2, D), b[:, 2048:5632], g.part(b, 5632, KE, P)
    g.xg, g.sg, g.yb = g.part(b, 9216, KD, P), g.part(b, 10240, 2, FC), b[:, 11136:12160]
    g.perm, g.pw, g.pwt = g.part(b, 12160, 2, P), g.part(b, 12416, 2, P), b[:, 12672:12928]
    g.rt_flat, g.cur = b[:, 12928:12964], b[:, 12964:12968]
    g.rt = g.rt_flat.rearrange("p (e c) -> p e c", c=4)
    g.lg, g.chosen = g.part(b, 12968, 2, 80), g.part(b, 13128, 2, 8)
    g.outs = g.part(b, 0, 2, D)


def even_proj_pe(g, pe):
    pe.wait_ge(g.s["dve_norm"], g.at("aT", "mix0"))
    t = 0
    for i in range(5):
        n, w = g.next_weights()
        pe.wait_ge(g.slab_in[n % RING], 16 * (n // RING + 1))
        cols = 512 if i < 4 else 160
        for j in range(-(-cols // P)):
            m = min(P, cols - P * j)
            pe.wait_ge(*g.bank_free())
            ps = g.open(("e", t))
            out = ps[0:P, 0:L] if m == P else ps[64:96, 0:L]
            for k in range(KD):
                a = cols * k + P * j
                last = mm(pe, out, w[:, a:a + m], g.aT[:, k, 0:L], k == 0, k == KD - 1)
            last.then_inc(g.s["pe_projection"], 1)
            g.count("pe_projection", ("mm", "e", t))
            t += 1
        g.also("pe_projection", ("used", n))


def even_proj_act(g, act):
    for t in range(18):
        act.wait_ge(g.s["pe_projection"], g.at("mm", "e", t))
        r = slice(0, P) if t < 17 else slice(64, 96)
        dst = g.prj[:, t, 1:257] if t < SHIFTED else g.lat[r, t - SHIFTED, :]
        act.activation(dst, g.bank(("e", t))[r, 0:L], ACT.Copy).then_inc(g.s["act_projection"], 1)
        g.count("act_projection", ("free", ("e", t)))
    g.also("act_projection", ("projected", 0))


def delta_in_dve(g, dve):
    dve.wait_ge(g.s["dve_norm"], g.at("aT", "mix0"))
    dve.memset(g.prj[:, :, 0:1], 0.0).then_inc(g.s["dve_delta"], 1)
    g.count("dve_delta")
    dve.wait_ge(g.s["dve_delta"], g.so_far("dve_delta"))
    dve.wait_ge(g.s["act_projection"], g.at("projected", 0))
    dve.tensor_tensor(g.d14[:, :, :], g.prj[:, :, 0:L], g.prj[:, :, 1:257], ALU.subtract).then_inc(g.s["dve_delta"], 1)
    g.count("dve_delta")
    dve.wait_ge(g.s["dve_delta"], g.so_far("dve_delta"))
    for t in [12, 13] + list(range(12)):
        dve.scalar_tensor_tensor(g.prj[:, t, 1:257], g.d14[:, t, :], g.v("shift_mu_0_2", t),
                                            g.prj[:, t, 1:257], ALU.mult, ALU.add).then_inc(g.s["dve_delta"], 1)
        g.count("dve_delta", ("shifted", t))
    r, k = g.prj[:, 0:4, 1:257], g.prj[:, 4:8, 1:257]
    dve.wait_ge(g.s["dve_delta"], g.so_far("dve_delta"))
    for j in range(4):
        dve.tensor_scalar(g.rw_kk[:, j, :], k[:, j, :], g.v("rw_kk_0_2", j), None, ALU.mult).then_inc(g.s["dve_delta"], 1)
        g.count("dve_delta", ("kk", j))
    dve.wait_ge(g.s["act_delta"], g.at("kk norm", 1))
    dve.tensor_scalar(g.w4b[:, :, :], g.w4b[:, :, :], 1e-12, None, ALU.max).then_inc(g.s["dve_delta"], 1)
    g.count("dve_delta")
    dve.wait_ge(g.s["dve_delta"], g.so_far("dve_delta"))
    dve.reciprocal(g.w4b[:, :, :], g.w4b[:, :, :]).then_inc(g.s["dve_delta"], 1)
    g.count("dve_delta")
    dve.wait_ge(g.s["dve_delta"], g.so_far("dve_delta"))
    dve.tensor_tensor(g.rw_kk[:, :, :], g.rw_kk[:, :, :], g.w4b[:, :, :], ALU.mult).then_inc(g.s["dve_delta"], 1)
    g.count("dve_delta")
    dve.wait_ge(g.s["act_delta"], g.at("sig w", 3))
    dve.wait_ge(g.s["act_delta"], g.at("rw a", 3))
    dve.tensor_scalar(g.lnw[:, :, :], g.lnw[:, :, :], LN_DECAY, None, ALU.mult).then_inc(g.s["dve_delta"], 1)
    g.count("dve_delta")
    dve.wait_ge(g.s["dve_delta"], g.so_far("dve_delta"))
    dve.tensor_tensor_scan(g.cum.rearrange("p a b -> p (a b)"), g.tab("keep"),
                                      g.lnw.rearrange("p a b -> p (a b)"), 0.0, ALU.mult, ALU.add).then_inc(g.s["dve_delta"], 1)
    g.count("dve_delta", "cum")
    dve.wait_ge(g.s["dve_delta"], g.so_far("dve_delta"))
    dve.tensor_tensor(g.lnw[:, :, :], g.cum[:, :, :], g.lnw[:, :, :], ALU.subtract).then_inc(g.s["dve_delta"], 1)
    g.count("dve_delta", "cum before")
    for j in range(4):
        dve.tensor_scalar(g.w4[:, j, :], g.rw_a[:, j, :], 1.0, g.v("rw_ka_0_2", j), ALU.subtract, ALU.mult).then_inc(g.s["dve_delta"], 1)
        g.count("dve_delta")
    dve.wait_ge(g.s["dve_delta"], g.so_far("dve_delta"))
    dve.scalar_tensor_tensor(k, g.w4[:, :, :], 1.0, k, ALU.add, ALU.mult).then_inc(g.s["dve_delta"], 1)
    g.count("dve_delta")
    dve.wait_ge(g.s["dve_delta"], g.so_far("dve_delta"))
    split = lambda x: x.rearrange("p j (t c) -> p j t c", t=2)
    dve.wait_ge(g.s["act_delta"], g.at("exp before"))
    dve.scalar_tensor_tensor(g.w4[:, :, :], g.rw_kk[:, :, :], -1.0, g.w4b[:, :, :], ALU.mult, ALU.mult).then_inc(g.s["dve_delta"], 1)
    g.count("dve_delta")
    dve.wait_ge(g.s["dve_delta"], g.so_far("dve_delta"))
    dve.tensor_copy(g.ar[:, :, :, 0, :], split(g.w4[:, :, :])).then_inc(g.s["dve_delta"], 1)
    g.count("dve_delta", "A~")
    dve.wait_ge(g.s["act_delta"], g.at("exp minus"))
    dve.tensor_tensor(g.bt[:, :, :], g.rw_kk[:, :, :], g.rw_a[:, :, :], ALU.mult).then_inc(g.s["dve_delta"], 1)
    g.count("dve_delta")
    dve.wait_ge(g.s["dve_delta"], g.so_far("dve_delta"))
    dve.tensor_tensor(g.bt[:, :, :], g.bt[:, :, :], g.w4c[:, :, :], ALU.mult).then_inc(g.s["dve_delta"], 1)
    g.count("dve_delta", "B~")
    dve.tensor_tensor(g.kt[:, :, :], k, g.w4c[:, :, :], ALU.mult).then_inc(g.s["dve_delta"], 1)
    g.count("dve_delta", "K~")
    dve.wait_ge(g.s["act_delta"], g.at("exp cum"))
    dve.tensor_tensor(g.w4[:, :, :], r, g.cum[:, :, :], ALU.mult).then_inc(g.s["dve_delta"], 1)
    g.count("dve_delta")
    dve.wait_ge(g.s["dve_delta"], g.so_far("dve_delta"))
    dve.tensor_copy(g.ar[:, :, :, 1, :], split(g.w4[:, :, :])).then_inc(g.s["dve_delta"], 1)
    g.count("dve_delta", "R~")
    ends = g.cum.rearrange("p j (n c) -> p j n c", c=CH)[:, :, :, CH - 1]
    dve.tensor_copy(g.lend[:, :, :], ends).then_inc(g.s["dve_delta"], 1)
    g.count("dve_delta", "chunk ends")
    dve.memset(g.states[:, 0, :], 0.0).then_inc(g.s["dve_delta"], 1)
    g.count("dve_delta", ("state", 0))


def delta_in_act(g, act):
    act.wait_ge(g.s["dve_delta"], g.at("shifted", 12))
    act.wait_ge(g.s["dve_delta"], g.at("shifted", 13))
    x = g.prj[:, 12:14, 1:257]
    act.activation(x[0:64, 0, :], x[0:64, 0, :], ACT.Tanh).then_inc(g.s["act_delta"], 1)
    g.count("act_delta", "tanh w")
    act.activation(x[:, 1, :], x[:, 1, :], ACT.Sigmoid).then_inc(g.s["act_delta"], 1)
    g.count("act_delta", "sig g")
    for j in range(4):
        for i, (dst, bias, mark) in enumerate(((g.lnw, "rw_w0_0_2", "sig w"), (g.rw_a, "rw_a0_0_2", "rw a"))):
            act.wait_ge(g.s["pe_delta"], g.at("mm", "lora", j, i))
            act.activation(dst[:, j, :], g.bank(("lora", j, i))[:, 0:L], ACT.Sigmoid, bias=g.v(bias, j)).then_inc(g.s["act_delta"], 1)
            g.count("act_delta", (mark, j))
            g.also("act_delta", ("free", ("lora", j, i)))
    for j in range(2):
        act.wait_ge(g.s["pe_delta"], g.at("mm", "gate", j))
        act.activation(g.rw_g[:, 2 * j:2 * j + 2, :].rearrange("p a b -> p (a b)"),
                                  g.bank(("gate", j))[:, :], ACT.Copy).then_inc(g.s["act_delta"], 1)
        g.count("act_delta", ("free", ("gate", j)))
    g.also("act_delta", "gates")
    act.wait_ge(g.s["dve_delta"], g.at("kk", 3))
    act.activation(g.w4[:, :, :], g.rw_kk[:, :, :], ACT.Square).then_inc(g.s["act_delta"], 1)
    g.count("act_delta", "kk sq")
    for i in range(2):
        act.wait_ge(g.s["pe_delta"], g.at("mm", "kk", i))
        act.activation(g.w4b[:, 2 * i:2 * i + 2, :].rearrange("p a b -> p (a b)"), g.bank(("kk", i))[:, :],
                                  ACT.Sqrt).then_inc(g.s["act_delta"], 1)
        g.count("act_delta", ("free", ("kk", i)))
        g.also("act_delta", ("kk norm", i))
    act.wait_ge(g.s["dve_delta"], g.at("cum before"))
    act.activation(g.w4b[:, :, :], g.lnw[:, :, :], ACT.Exp).then_inc(g.s["act_delta"], 1)
    g.count("act_delta", "exp before")
    act.activation(g.w4c[:, :, :], g.cum[:, :, :], ACT.Exp, scale=-1.0).then_inc(g.s["act_delta"], 1)
    g.count("act_delta", "exp minus")
    act.wait_ge(g.s["act_delta"], g.so_far("act_delta"))
    act.activation(g.cum[:, :, :], g.cum[:, :, :], ACT.Exp).then_inc(g.s["act_delta"], 1)
    g.count("act_delta", "exp cum")


def delta_in_pe(g, pe):
    n, w = g.next_weights()
    pe.wait_ge(g.slab_in[n % RING], 16 * (n // RING + 1))
    g.lora_slab = n
    g.lora = w
    wa2 = w[:, 0:512]
    pe.wait_ge(g.s["act_delta"], g.at("tanh w"))
    pe.wait_ge(g.s["dve_delta"], g.at("shifted", 12))
    x = g.prj[:, 12:14, 1:257]
    for j in range(4):
        for i, r in enumerate((slice(0, 64), slice(64, 128))):
            pe.wait_ge(*g.bank_free())
            ps = g.open(("lora", j, i))
            mm(pe, ps[:, 0:L], wa2[r, P * j:P * j + P], x[r, 0, :]).then_inc(g.s["pe_delta"], 1)
            g.count("pe_delta", ("mm", "lora", j, i))
    pe.wait_ge(g.s["act_delta"], g.at("sig g"))
    for j in range(2):
        pe.wait_ge(*g.bank_free())
        ps = g.open(("gate", j))
        for i in range(2):
            a = 512 + P * (2 * j + i)
            last = mm(pe, ps[:, L * i:L * i + L], w[:, a:a + P], x[:, 1, :])
        last.then_inc(g.s["pe_delta"], 1)
        g.count("pe_delta", ("mm", "gate", j))
    pe.wait_ge(g.s["act_delta"], g.at("kk sq"))
    for i in range(2):
        pe.wait_ge(*g.bank_free())
        ps = g.open(("kk", i))
        mm(pe, ps[:, :], g.tab("headones"), g.w4[:, 2 * i:2 * i + 2, :].rearrange("p a b -> p (a b)")).then_inc(g.s["pe_delta"], 1)
        g.count("pe_delta", ("mm", "kk", i))


def rows_of(h):
    return slice(HD * (h % 2), HD * (h % 2) + HD)


def delta_pe(g, pe, tt):
    pe.wait_ge(g.s["dve_delta"], g.at("A~"))
    pe.wait_ge(g.s["dve_delta"], g.at("B~"))
    pe.wait_ge(g.s["dve_delta"], g.at("K~"))
    pe.wait_ge(g.s["dve_delta"], g.at("R~"))
    pe.wait_ge(g.s["dve_delta"], g.at("chunk ends"))
    c = slice(P * tt, P * tt + P)
    src = [g.ar[:, :, tt, 0, :], g.bt[:, :, c], g.kt[:, :, c], g.prj[:, 8:12, 1 + P * tt:1 + P * tt + P]]
    for n, s in enumerate(src):
        pe.wait_ge(*g.bank_free())
        ps = g.open(("tok", tt, n))
        for j in range(4):
            last = pe.transpose(ps[:, P * j:P * j + P], s[:, j, :], g.tab("ident"))
        last.then_inc(g.s["pe_delta"], 1)
        g.count("pe_delta", ("mm", "tok", tt, n))
    for h in range(8):
        r, j = rows_of(h), h // 2
        pe.wait_ge(*g.bank_free())
        ps = g.open(("mp", tt, h))
        both = g.ar[r, j, tt, :, :].rearrange("p w c -> p (w c)")
        mm(pe, ps[:, 0:256], g.bt[r, j, c], both)
        mm(pe, ps[:, 256:512], g.kt[r, j, c], both).then_inc(g.s["pe_delta"], 1)
        g.count("pe_delta", ("mm", "mp", tt, h))
    for odd in range(2):
        pe.wait_ge(*g.bank_free())
        ps = g.open(("low", tt, odd))
        for j in range(4):
            r = rows_of(odd)
            last = mm(pe, ps[:, P * j:P * j + P], g.ar[r, j, tt, 0, :], g.bt[r, j, c])
        last.then_inc(g.s["pe_delta"], 1)
        g.count("pe_delta", ("mm", "low", tt, odd))
    for lv in range(5):
        pe.wait_ge(g.s["dve_delta"], g.at("F", tt, lv, 0))
        pe.wait_ge(g.s["dve_delta"], g.at("F", tt, lv, 1))
        pe.wait_ge(g.s["dve_delta"], g.at("powers", tt, lv, 0))
        pe.wait_ge(g.s["dve_delta"], g.at("powers", tt, lv, 1))
        pe.wait_ge(*g.moment(("lows", tt, lv, 0)))
        pe.wait_ge(*g.moment(("lows", tt, lv, 1)))
        for odd in range(2):
            heads = [2 * j + odd for j in range(4)]
            if lv < 4:
                pe.wait_ge(*g.bank_free())
                ps = g.open(("D", tt, lv, odd))
                for j, h in enumerate(heads):
                    last = mm(pe, ps[:, P * j:P * j + P], g.mp[:, h, 0, :], g.dm[:, h, :])
                last.then_inc(g.s["pe_delta"], 1)
                g.count("pe_delta", ("mm", "D", tt, lv, odd))
            if lv < 3:
                pe.wait_ge(*g.bank_free())
                ps = g.open(("U", tt, lv, odd))
                for j, h in enumerate(heads):
                    last = mm(pe, ps[:, P * j:P * j + P], g.dm[:, h, :], g.mp[:, h, 0, :])
                last.then_inc(g.s["pe_delta"], 1)
                g.count("pe_delta", ("mm", "U", tt, lv, odd))
            if lv > 0:
                pe.wait_ge(*g.bank_free())
                ps = g.open(("Fp", tt, lv, odd))
                for j, h in enumerate(heads):
                    last = mm(pe, ps[:, P * j:P * j + P], g.dm[:, h, :], g.fm[:, h, :])
                last.then_inc(g.s["pe_delta"], 1)
                g.count("pe_delta", ("mm", "Fp", tt, lv, odd))
            g.also("pe_delta", ("read", tt, lv, odd))
    pe.wait_ge(g.s["dve_delta"], g.at("F", tt, 5, 0))
    pe.wait_ge(g.s["dve_delta"], g.at("F", tt, 5, 1))
    pe.wait_ge(*g.bank_free())
    ps = g.open(("NV", tt))
    for h in range(8):
        last = mm(pe, ps[:, HD * h:HD * h + HD], g.mp[:, h, 2, :], g.tok[:, 3, HD * h:HD * h + HD])
    last.then_inc(g.s["pe_delta"], 1)
    g.count("pe_delta", ("mm", "NV", tt))
    pe.wait_ge(*g.bank_free())
    ps = g.open(("WT", tt))
    for h in range(8):
        last = mm(pe, ps[rows_of(h), P * (h // 2):P * (h // 2) + P], g.tok[:, 0, HD * h:HD * h + HD], g.fm[:, h, :])
    last.then_inc(g.s["pe_delta"], 1)
    g.count("pe_delta", ("mm", "WT", tt))
    pe.wait_ge(g.s["act_delta"], g.at("nv", tt))
    pe.wait_ge(*g.bank_free())
    ps = g.open(("Z", tt))
    for h in range(8):
        last = mm(pe, ps[:, HD * h:HD * h + HD], g.fm[:, h, :], g.nv[:, HD * h:HD * h + HD])
    last.then_inc(g.s["pe_delta"], 1)
    g.count("pe_delta", ("mm", "Z", tt))
    pe.wait_ge(g.s["act_delta"], g.at("wt", tt))
    for cc in range(4):
        n = 4 * tt + cc
        q = slice(CH * cc, CH * cc + CH)
        pe.wait_ge(g.s["dve_delta"], g.at("state", n))
        for odd in range(2):
            pe.wait_ge(*g.bank_free())
            ps = g.open(("u", n, odd))
            for j in range(4):
                last = mm(pe, ps[q, HD * j:HD * j + HD], g.wt[rows_of(odd), j, q],
                          g.states[rows_of(odd), n % 5, HD * j:HD * j + HD])
            last.then_inc(g.s["pe_delta"], 1)
            g.count("pe_delta", ("mm", "u", n, odd))
        pe.wait_ge(*g.bank_free())
        ps = g.open(("s", n))
        pe.wait_ge(g.s["dve_delta"], g.at("U row", n))
        for h in range(8):
            o = ps[rows_of(h), HD * (h // 2):HD * (h // 2) + HD]
            v = slice(HD * h, HD * h + HD)
            mm(pe, o, g.tok[q, 2, v], g.tok[q, 3, v], True, False)
            last = mm(pe, o, g.tok[q, 1, v], g.u[q, v], False, True)
        last.then_inc(g.s["pe_delta"], 1)
        g.count("pe_delta", ("mm", "s", n))
    for odd in range(2):
        r = rows_of(odd)
        pe.wait_ge(*g.bank_free())
        ps = g.open(("y", tt, odd))
        for j in range(4):
            h = 2 * j + odd
            v, o = slice(HD * h, HD * h + HD), slice(P * j, P * j + P)
            mm(pe, ps[r, o], g.u[:, v], g.mp[:, h, 1, :], True, False)
            mm(pe, ps[r, o], g.tok[:, 3, v], g.mp[:, h, 3, :], False, False)
            for cc in range(4):
                o = slice(P * j + CH * cc, P * j + CH * cc + CH)
                last = mm(pe, ps[r, o], g.states[r, (4 * tt + cc) % 5, HD * j:HD * j + HD],
                          g.ar[r, j, tt, 1, CH * cc:CH * cc + CH], False, cc == 3)
        last.then_inc(g.s["pe_delta"], 1)
        g.count("pe_delta", ("mm", "y", tt, odd))


def delta_act(g, act, tt):
    for n in range(4):
        act.wait_ge(g.s["pe_delta"], g.at("mm", "tok", tt, n))
        if tt:
            act.wait_ge(g.s["pe_delta"], g.at("mm", "y", tt - 1, 1))
        act.activation(g.tok[:, n, :], g.bank(("tok", tt, n))[:, :], ACT.Copy).then_inc(g.s["act_delta"], 1)
        g.count("act_delta", ("free", ("tok", tt, n)))
    g.also("act_delta", ("toks", tt))
    for lv in range(4):
        act.wait_ge(g.s["pe_delta"], g.at("read", tt, lv, 1))
        for odd in range(2):
            act.activation(heads_of(g.dm, odd), four(g.bank(("D", tt, lv, odd))), ACT.Copy).then_inc(g.s["act_delta"], 1)
            g.count("act_delta", ("free", ("D", tt, lv, odd)))
            g.also("act_delta", ("lows", tt, lv + 1, odd))
    for key, dst, mark in (("NV", g.nv, "nv"), ("WT", g.wt.rearrange("p a b -> p (a b)"), "wt"), ("Z", g.z, "z")):
        act.wait_ge(g.s["pe_delta"], g.at("mm", key, tt))
        act.activation(dst, g.bank((key, tt))[:, :], ACT.Copy).then_inc(g.s["act_delta"], 1)
        g.count("act_delta", ("free", (key, tt)))
        g.also("act_delta", (mark, tt))
    for odd in range(2):
        r = rows_of(odd)
        act.wait_ge(g.s["pe_delta"], g.at("mm", "y", tt, odd))
        act.activation(g.y[r, :, P * tt:P * tt + P], four(g.bank(("y", tt, odd)))[r], ACT.Copy).then_inc(g.s["act_delta"], 1)
        g.count("act_delta", ("free", ("y", tt, odd)))
    g.also("act_delta", ("y done", tt))


def four(ps):
    return ps[:, :].rearrange("p (a b) -> p a b", a=4)


def heads_of(m, odd):
    return m.rearrange("p (j o) c -> p j o c", o=2)[:, :, odd, :]


def delta_dve(g, dve, tt):
    masks = g.tab("chunk_masks")
    if tt:
        dve.wait_ge(g.s["pe_delta"], g.at("mm", "y", tt - 1, 1))
    for h in range(8):
        dve.wait_ge(g.s["pe_delta"], g.at("mm", "mp", tt, h))
        dve.tensor_tensor(g.mp[:, h, :, :].rearrange("p w c -> p (w c)"), g.bank(("mp", tt, h))[:, :], masks,
                                     ALU.mult).then_inc(g.s["dve_delta"], 1)
        g.count("dve_delta", ("free", ("mp", tt, h)))
    ups = g.mp[:, :, 0, :]
    for odd in range(2):
        dve.wait_ge(g.s["pe_delta"], g.at("mm", "low", tt, odd))
        dve.tensor_tensor(heads_of(g.dm, odd), four(g.bank(("low", tt, odd))), four(g.tab("strict_low")),
                                     ALU.mult).then_inc(g.s["dve_delta"], 1)
        g.count("dve_delta", ("free", ("low", tt, odd)))
        g.also("dve_delta", ("lows", tt, 0, odd))
        g.also("dve_delta", ("powers", tt, 0, odd))
    dve.wait_ge(g.s["dve_delta"], g.so_far("dve_delta"))
    ident = g.tab("ident").unsqueeze(1).broadcast_to((P, 8, P))
    dve.tensor_tensor(g.fm[:, :, :], ups, ident, ALU.add).then_inc(g.s["dve_delta"], 1)
    g.count("dve_delta", ("F", tt, 0, 0))
    g.also("dve_delta", ("F", tt, 0, 1))
    g.also("dve_delta", ("F", tt, 1, 0))
    g.also("dve_delta", ("F", tt, 1, 1))
    for lv in range(5):
        for odd in range(2):
            if lv < 3:
                dve.wait_ge(g.s["pe_delta"], g.at("read", tt, lv, 1))
                dve.tensor_copy(heads_of(ups, odd), four(g.bank(("U", tt, lv, odd)))).then_inc(g.s["dve_delta"], 1)
                g.count("dve_delta", ("free", ("U", tt, lv, odd)))
            g.also("dve_delta", ("powers", tt, lv + 1, odd))
            if lv > 0:
                dve.wait_ge(g.s["pe_delta"], g.at("mm", "Fp", tt, lv, odd))
                f = heads_of(g.fm, odd)
                dve.tensor_tensor(f, four(g.bank(("Fp", tt, lv, odd))), f, ALU.add).then_inc(g.s["dve_delta"], 1)
                g.count("dve_delta", ("free", ("Fp", tt, lv, odd)))
                g.also("dve_delta", ("F", tt, lv + 1, odd))
    dve.wait_ge(g.s["act_delta"], g.at("z", tt))
    for cc in range(4):
        n = 4 * tt + cc
        q = slice(CH * cc, CH * cc + CH)
        for odd in range(2):
            dve.wait_ge(g.s["pe_delta"], g.at("mm", "u", n, odd))
            alt = lambda x: x.rearrange("p (j o v) -> p j o v", o=2, v=HD)[:, :, odd, :]
            dve.tensor_tensor(alt(g.u[q, :]), g.bank(("u", n, odd))[q, 0:L].rearrange("p (j v) -> p j v", v=HD),
                                         alt(g.z[q, :]), ALU.add).then_inc(g.s["dve_delta"], 1)
            g.count("dve_delta", ("free", ("u", n, odd)))
        g.also("dve_delta", ("U row", n))
        dve.wait_ge(g.s["pe_delta"], g.at("mm", "s", n))
        if n >= 4:
            dve.wait_ge(g.s["pe_delta"], g.at("mm", "y", 0, 1))
        now, new = g.states[:, n % 5, :], g.states[:, (n + 1) % 5, :]
        dve.tensor_tensor(new, g.bank(("s", n))[:, 0:L], now, ALU.add).then_inc(g.s["dve_delta"], 1)
        g.count("dve_delta", ("free", ("s", n)))
        dve.wait_ge(g.s["dve_delta"], g.so_far("dve_delta"))
        end = g.lend[:, :, n:n + 1].broadcast_to((P, 4, HD))
        new4 = new.rearrange("p (j v) -> p j v", v=HD)
        dve.tensor_tensor(new4, new4, end, ALU.mult).then_inc(g.s["dve_delta"], 1)
        g.count("dve_delta", ("state", n + 1))
        dve.wait_ge(g.s["dve_delta"], g.so_far("dve_delta"))


def delta_out_dve(g, dve):
    dve.wait_ge(g.s["act_delta"], g.at("y done", 1))
    r, k, v = g.prj[:, 0:4, 1:257], g.prj[:, 4:8, 1:257], g.prj[:, 8:12, 1:257]
    for j in range(4):
        dve.scalar_tensor_tensor(g.w4[:, j, :], r[:, j, :], g.v("rw_rk_0_2", j), k[:, j, :],
                                            ALU.mult, ALU.mult).then_inc(g.s["dve_delta"], 1)
        g.count("dve_delta", ("rkk", j))
    flat = lambda x, i: x[:, 2 * i:2 * i + 2, :].rearrange("p a b -> p (a b)")
    for i in range(2):
        dve.wait_ge(g.s["pe_delta"], g.at("mm", "d mean", i))
        dve.scalar_tensor_tensor(flat(g.y, i), g.bank(("d mean", i))[:, :], -1.0 / HD, flat(g.y, i),
                                            ALU.mult, ALU.add).then_inc(g.s["dve_delta"], 1)
        g.count("dve_delta", ("free", ("d mean", i)))
    for i in range(2):
        dve.wait_ge(g.s["pe_delta"], g.at("mm", "bonus", i))
        b = g.bank(("bonus", i))[:, :].rearrange("p (a b) -> p a b", a=2)
        dve.tensor_tensor(g.w4c[:, 2 * i:2 * i + 2, :], b, v[:, 2 * i:2 * i + 2, :], ALU.mult).then_inc(g.s["dve_delta"], 1)
        g.count("dve_delta", ("free", ("bonus", i)))
    dve.wait_ge(g.s["act_delta"], g.at("free", ("d var", 1)))
    dve.reciprocal(g.w4b[:, :, :], g.w4b[:, :, :]).then_inc(g.s["dve_delta"], 1)
    g.count("dve_delta")
    dve.wait_ge(g.s["dve_delta"], g.so_far("dve_delta"))
    dve.tensor_tensor(g.y[:, :, :], g.y[:, :, :], g.w4b[:, :, :], ALU.mult).then_inc(g.s["dve_delta"], 1)
    g.count("dve_delta", "y normed")
    for j in range(4):
        dve.wait_ge(g.s["act_delta"], g.at("y affine", j))
        dve.tensor_tensor(g.y[:, j, :], g.y[:, j, :], g.w4c[:, j, :], ALU.add).then_inc(g.s["dve_delta"], 1)
        g.count("dve_delta")
    dve.wait_ge(g.s["dve_delta"], g.so_far("dve_delta"))
    dve.tensor_tensor(g.aT[:, 0:4, 0:L], g.y[:, :, :], g.rw_g[:, :, :], ALU.mult).then_inc(g.s["dve_delta"], 1)
    g.count("dve_delta", "y delta")


def delta_out_pe(g, pe):
    flat = lambda x, i: x[:, 2 * i:2 * i + 2, :].rearrange("p a b -> p (a b)")
    pe.wait_ge(g.s["act_delta"], g.at("y done", 1))
    for what, src, key in (("d mean", g.y, ("y done", 1)), ("bonus", g.w4, ("rkk", 3)), ("d var", g.w4b, "d sq")):
        pe.wait_ge(*g.moment(key))
        for i in range(2):
            pe.wait_ge(*g.bank_free())
            ps = g.open((what, i))
            mm(pe, ps[:, :], g.tab("headones"), flat(src, i)).then_inc(g.s["pe_delta"], 1)
            g.count("pe_delta", ("mm", what, i))


def delta_out_act(g, act):
    flat = lambda x, i: x[:, 2 * i:2 * i + 2, :].rearrange("p a b -> p (a b)")
    act.wait_ge(g.s["dve_delta"], g.at("free", ("d mean", 1)))
    act.activation(g.w4b[:, :, :], g.y[:, :, :], ACT.Square).then_inc(g.s["act_delta"], 1)
    g.count("act_delta", "d sq")
    for i in range(2):
        act.wait_ge(g.s["pe_delta"], g.at("mm", "d var", 1))
        act.activation(flat(g.w4b, i), g.bank(("d var", i))[:, :], ACT.Sqrt, bias=g.eps[:, 1:2],
                                  scale=1.0 / HD).then_inc(g.s["act_delta"], 1)
        g.count("act_delta", ("free", ("d var", i)))
    act.wait_ge(g.s["dve_delta"], g.at("y normed"))
    for j in range(4):
        act.activation(g.y[:, j, :], g.y[:, j, :], ACT.Identity, bias=g.v("rw_lnx_b_0_2", j),
                                  scale=g.v("rw_lnx_g_0_2", j)).then_inc(g.s["act_delta"], 1)
        g.count("act_delta", ("y affine", j))


MLA_D, MLA_SCALE = 96, 96 ** -0.5


def mla_act(g, act):
    act.wait_ge(g.s["dve_delta"], g.at("y delta"))
    act.activation(g.w4[:, 0:3, :], g.lat[:, 0:3, :], ACT.Square).then_inc(g.s["act_latent"], 1)
    g.count("act_latent", "lat sq")
    for i, (n, width) in enumerate(((0, 256), (1, 128))):
        act.wait_ge(g.s["pe_latent"], g.at("mm", "lat", i))
        act.activation(g.w4b[:, i, :], g.bank(("lat", i))[:, 0:L], ACT.Sqrt, bias=g.eps[:, 0:1],
                                  scale=1.0 / width).then_inc(g.s["act_latent"], 1)
        g.count("act_latent", ("free", ("lat", i)))
    g.also("act_latent", "lat rms")
    for a in range(4):
        act.wait_ge(g.s["pe_latent"], g.at("mm", "mla q", a))
        act.activation(g.mq[0:96, 2 * a:2 * a + 2, :].rearrange("p a b -> p (a b)"),
                                  g.bank(("mla q", a))[0:96, :], ACT.Copy, scale=MLA_SCALE).then_inc(g.s["act_latent"], 1)
        g.count("act_latent", ("free", ("mla q", a)))
    g.also("act_latent", "mla q raw")
    for a in range(4):
        act.wait_ge(g.s["pe_latent"], g.at("mm", "mla k", a))
        act.activation(g.mk[0:64, 2 * a:2 * a + 2, :].rearrange("p a b -> p (a b)"),
                                  g.bank(("mla k", a))[0:64, :], ACT.Copy).then_inc(g.s["act_latent"], 1)
        g.count("act_latent", ("free", ("mla k", a)))
    for t in range(2):
        act.wait_ge(g.s["pe_latent"], g.at("mm", "mla v", t))
        act.activation(g.mv[:, t, :], g.bank(("mla v", t))[:, :], ACT.Copy).then_inc(g.s["act_latent"], 1)
        g.count("act_latent", ("free", ("mla v", t)))
    act.wait_ge(g.s["dve_latent"], g.at("kpe"))
    act.activation(g.mk[64:96, :, :], g.lat[64:96, 3:4, :].broadcast_to((32, 8, L)), ACT.Copy).then_inc(g.s["act_latent"], 1)
    g.count("act_latent", "mla have")


def mla_pe(g, pe):
    pe.wait_ge(g.s["act_latent"], g.at("lat sq"))
    for i, ts in enumerate(((0, 1), (2,))):
        pe.wait_ge(*g.bank_free())
        ps = g.open(("lat", i))
        for t in ts:
            last = mm(pe, ps[:, 0:L], g.tab("ones"), g.w4[:, t, :], t == ts[0], t == ts[-1])
        last.then_inc(g.s["pe_latent"], 1)
        g.count("pe_latent", ("mm", "lat", i))
    pe.wait_ge(g.s["dve_latent"], g.at("lat normed"))
    wuq = g.lora[:, 1024:2560].rearrange("p (k c) -> p k c", k=2)
    wukv = g.lora[:, 2560:3584].rearrange("p (h w c) -> p h w c", h=8, w=2)
    for a in range(4):
        pe.wait_ge(*g.bank_free())
        ps = g.open(("mla q", a))
        for i in range(2):
            h = 2 * a + i
            for k in range(2):
                last = mm(pe, ps[0:96, L * i:L * i + L], wuq[:, k, 96 * h:96 * h + 96], g.lat[:, k, :], k == 0, k == 1)
        last.then_inc(g.s["pe_latent"], 1)
        g.count("pe_latent", ("mm", "mla q", a))
    for a in range(4):
        pe.wait_ge(*g.bank_free())
        ps = g.open(("mla k", a))
        for i in range(2):
            last = mm(pe, ps[0:64, L * i:L * i + L], wukv[:, 2 * a + i, 0, :], g.lat[:, 2, :])
        last.then_inc(g.s["pe_latent"], 1)
        g.count("pe_latent", ("mm", "mla k", a))
    for t in range(2):
        pe.wait_ge(*g.bank_free())
        ps = g.open(("mla v", t))
        mm(pe, ps[:, :], g.lat[:, 2, P * t:P * t + P], wukv[:, :, 1, :]).then_inc(g.s["pe_latent"], 1)
        g.count("pe_latent", ("mm", "mla v", t))
    g.also("pe_latent", ("used", g.lora_slab))
    swap = g.tab("mla_swap")[64:96, 64:96]
    pe.wait_ge(g.s["act_latent"], g.at("mla q raw"))
    for a in range(4):
        pe.wait_ge(*g.bank_free())
        ps = g.open(("q swap", a))
        mm(pe, ps[64:96, :], swap, g.mq[64:96, 2 * a:2 * a + 2, :].rearrange("p a b -> p (a b)")).then_inc(g.s["pe_latent"], 1)
        g.count("pe_latent", ("mm", "q swap", a))
    pe.wait_ge(*g.bank_free())
    ps = g.open(("k swap",))
    mm(pe, ps[64:96, 0:L], swap, g.lat[64:96, 3, :]).then_inc(g.s["pe_latent"], 1)
    g.count("pe_latent", ("mm", "k swap"))


def mla_dve(g, dve):
    dve.wait_ge(g.s["act_latent"], g.at("lat rms"))
    dve.reciprocal(g.w4b[:, 0:2, :], g.w4b[:, 0:2, :]).then_inc(g.s["dve_latent"], 1)
    g.count("dve_latent")
    dve.wait_ge(g.s["dve_latent"], g.so_far("dve_latent"))
    for t, (n, i) in enumerate((("mla_qnorm_0_2", 0), ("mla_qnorm_0_2", 0), ("mla_kvnorm_0_2", 1))):
        dve.scalar_tensor_tensor(g.lat[:, t, :], g.lat[:, t, :], g.v(n, t % 2), g.w4b[:, i, :],
                                            ALU.mult, ALU.mult).then_inc(g.s["dve_latent"], 1)
        g.count("dve_latent", "lat normed")
    r = slice(64, 96)
    cos, sin = g.tab("mla_cos")[r, :], g.tab("mla_sin")[r, :]
    for a in range(5):
        x = g.mq[r, 2 * a:2 * a + 2, :] if a < 4 else g.lat[r, 3:4, :]
        n = 2 if a < 4 else 1
        key = ("q swap", a) if a < 4 else ("k swap",)
        dve.wait_ge(g.s["pe_latent"], g.at("mm", *key))
        t = g.w4[r, 0:n, :]
        dve.tensor_tensor(t, g.bank(key)[r, 0:L * n].rearrange("p (a b) -> p a b", a=n),
                                     sin.unsqueeze(1).broadcast_to((32, n, L)), ALU.mult).then_inc(g.s["dve_latent"], 1)
        g.count("dve_latent", ("free", key))
        dve.tensor_tensor(x, x, cos.unsqueeze(1).broadcast_to((32, n, L)), ALU.mult).then_inc(g.s["dve_latent"], 1)
        g.count("dve_latent")
        dve.wait_ge(g.s["dve_latent"], g.so_far("dve_latent"))
        dve.tensor_tensor(x, x, t, ALU.add).then_inc(g.s["dve_latent"], 1)
        g.count("dve_latent", ("mla rotated", a))
        dve.wait_ge(g.s["dve_latent"], g.so_far("dve_latent"))
    g.also("dve_latent", "kpe")


def causal_of(g, q, k, v, out, ready, d=None, rows=None):
    def scores(h, t):
        if rows:
            pairs = [(q[0:rows, h, P * t:P * t + P], k[0:rows, h, 0:P * t + P])]
        else:
            pairs = [(q[rows_of(h), h // 2, P * t:P * t + P], k[rows_of(h), h // 2, 0:P * t + P])]
        if d is not None:
            pairs.append((g.tab("row")[:, P * h:P * h + P], d[:, 0:P * t + P]))
        return [(0, pairs)]

    return dict(heads=8, scores=scores, width=lambda t: P * t + P, add=lambda h, t: [(P * t, g.tab("causal"))],
                     values=lambda h, t: v[:, t, HD * h:HD * h + HD], out=out, ready=ready)


def glu_pe(g, pe, key, kt, ready):
    pe.wait_ge(g.s["dve_norm"], g.at(ready))
    for i in range(kt // 2):
        n, w = g.next_weights()
        pe.wait_ge(g.slab_in[n % RING], 16 * (n // RING + 1))
        for j in range(2):
            pe.wait_ge(*g.bank_free())
            ps = g.open(("glu", key, 2 * i + j))
            for ab in range(2):
                for k in range(KD):
                    a = 512 * k + 256 * ab + P * j
                    last = mm(pe, ps[:, L * ab:L * ab + L], w[:, a:a + P], g.aT[:, k, 0:L], k == 0, k == KD - 1)
            last.then_inc(g.s["pe_feedforward"], 1)
            g.count("pe_feedforward", ("mm", "glu", key, 2 * i + j))
        g.also("pe_feedforward", ("used", n))
    for m in range(KD):
        n, w = g.next_weights()
        pe.wait_ge(g.slab_in[n % RING], 16 * (n // RING + 1))
        pe.wait_ge(*g.bank_free())
        ps = g.open(("gd", key, m))
        for k in range(kt):
            if m == 0:
                pe.wait_ge(g.s["dve_feedforward"], g.at("hidden", key, k))
            last = mm(pe, ps[:, 0:L], w[:, P * k:P * k + P], g.hid2[:, k, :], k == 0, k == kt - 1)
        last.then_inc(g.s["pe_feedforward"], 1)
        g.count("pe_feedforward", ("mm", "gd", key, m))
        g.also("pe_feedforward", ("used", n))


def glu_act(g, act, key, kt):
    for t in range(kt):
        act.wait_ge(g.s["pe_feedforward"], g.at("mm", "glu", key, t))
        if t >= 4:
            act.wait_ge(g.s["dve_feedforward"], g.at("hidden", key, t - 4))
        act.activation(g.gate2[:, t % 4, :], g.bank(("glu", key, t))[:, 0:L], ACT.Silu).then_inc(g.s["act_feedforward"], 1)
        g.count("act_feedforward", ("silu", key, t))


def glu_dve(g, dve, key, kt, before=None):
    if before is not None:
        dve.wait_ge(g.s["pe_feedforward"], g.at(before))
    for t in range(kt):
        dve.wait_ge(g.s["act_feedforward"], g.at("silu", key, t))
        dve.tensor_tensor(g.hid2[:, t, :], g.bank(("glu", key, t))[:, L:T2], g.gate2[:, t % 4, :], ALU.mult).then_inc(g.s["dve_feedforward"], 1)
        g.count("dve_feedforward", ("hidden", key, t))
        g.also("dve_feedforward", ("free", ("glu", key, t)))


ODD = ("fq", "fk", "fv", "mq", "mk", "mv")


def odd_proj_pe(g, pe):
    pe.wait_ge(g.s["dve_norm"], g.at("aT", "mix1"))
    for name in ODD:
        n, w = g.next_weights()
        pe.wait_ge(g.slab_in[n % RING], 16 * (n // RING + 1))
        if name[1] == "v":
            for t in range(2):
                pe.wait_ge(*g.bank_free())
                ps = g.open((name, t))
                for k in range(KD):
                    last = mm(pe, ps[:, :], g.aT[:, k, P * t:P * t + P], w[:, 512 * k:512 * k + 512], k == 0, k == KD - 1)
                last.then_inc(g.s["pe_projection"], 1)
                g.count("pe_projection", ("mm", name, t))
        else:
            for i in range(2):
                pe.wait_ge(*g.bank_free())
                ps = g.open((name, i))
                for j in range(2):
                    for k in range(KD):
                        a = 512 * k + P * (2 * i + j)
                        last = mm(pe, ps[:, L * j:L * j + L], w[:, a:a + P], g.aT[:, k, 0:L], k == 0, k == KD - 1)
                last.then_inc(g.s["pe_projection"], 1)
                g.count("pe_projection", ("mm", name, i))
        g.also("pe_projection", ("used", n))
    n, w = g.next_weights()
    pe.wait_ge(g.slab_in[n % RING], 16 * (n // RING + 1))
    pe.wait_ge(*g.bank_free())
    ps = g.open(("forget",))
    for k in range(KD):
        last = mm(pe, ps[0:8, 0:L], w[:, 8 * k:8 * k + 8], g.aT[:, k, 0:L], k == 0, k == KD - 1)
    last.then_inc(g.s["pe_projection"], 1)
    g.count("pe_projection", ("mm", "forget"))
    g.also("pe_projection", ("used", n))
    for name in ("mq", "mk"):
        pe.wait_ge(g.s["act_projection"], g.at("have", name))
        for i in range(2):
            pe.wait_ge(*g.bank_free())
            ps = g.open(("swap", name, i))
            mm(pe, ps[:, :], g.tab("full_swap"), g.q2[name][:, 2 * i:2 * i + 2, :].rearrange("p a b -> p (a b)")).then_inc(g.s["pe_projection"], 1)
            g.count("pe_projection", ("mm", "swap", name, i))


def odd_proj_act(g, act):
    for name in ODD:
        for i in range(2):
            act.wait_ge(g.s["pe_projection"], g.at("mm", name, i))
            dst = g.q2[name][:, i, :] if name[1] == "v" else g.q2[name][:, 2 * i:2 * i + 2, :].rearrange("p a b -> p (a b)")
            act.activation(dst, g.bank((name, i))[:, :], ACT.Copy, scale=HD ** -0.5 if name[1] == "q" else 1.0).then_inc(g.s["act_projection"], 1)
            g.count("act_projection", ("free", (name, i)))
        g.also("act_projection", ("have", name))
    act.wait_ge(g.s["dve_projection"], g.at("minus abs"))
    act.activation(g.lsig[0:8, :], g.oneb[0:8, :], ACT.Exp).then_inc(g.s["act_projection"], 1)
    g.count("act_projection", "exp f")
    act.wait_ge(g.s["act_projection"], g.so_far("act_projection"))
    act.activation(g.lsig[0:8, :], g.lsig[0:8, :], ACT.Ln, bias=1.0).then_inc(g.s["act_projection"], 1)
    g.count("act_projection", "ln f")


def odd_proj_dve(g, dve):
    dve.wait_ge(g.s["dve_norm"], g.at("aT", "mix1"))
    dve.memset(g.negd[:, :], 0.0).then_inc(g.s["dve_projection"], 1)
    g.count("dve_projection")
    f = g.negd[0:8, :]
    dve.wait_ge(g.s["pe_projection"], g.at("mm", "forget"))
    dve.wait_ge(g.s["dve_projection"], g.so_far("dve_projection"))
    dve.tensor_scalar(f, g.bank(("forget",))[0:8, 0:L], g.v("fox_bf_1_2")[0:8, :], None, ALU.add).then_inc(g.s["dve_projection"], 1)
    g.count("dve_projection", ("free", ("forget",)))
    dve.wait_ge(g.s["dve_projection"], g.so_far("dve_projection"))
    dve.scalar_tensor_tensor(g.oneb[0:8, :], f, -1.0, f, ALU.mult, ALU.min).then_inc(g.s["dve_projection"], 1)
    g.count("dve_projection", "minus abs")
    dve.tensor_scalar(f, f, 0.0, None, ALU.min).then_inc(g.s["dve_projection"], 1)
    g.count("dve_projection")
    dve.wait_ge(g.s["act_projection"], g.at("ln f"))
    dve.wait_ge(g.s["dve_projection"], g.so_far("dve_projection"))
    dve.tensor_tensor(g.lsig[0:8, :], g.lsig[0:8, :], f, ALU.subtract).then_inc(g.s["dve_projection"], 1)
    g.count("dve_projection")
    dve.memset(g.oneb[0:8, :], 1.0).then_inc(g.s["dve_projection"], 1)
    g.count("dve_projection")
    dve.wait_ge(g.s["dve_projection"], g.so_far("dve_projection"))
    dve.tensor_tensor_scan(f, g.oneb[0:8, :], g.lsig[0:8, :], 0.0, ALU.mult, ALU.add).then_inc(g.s["dve_projection"], 1)
    g.count("dve_projection", "minus D")
    cos = g.tab("full_cos").unsqueeze(1).broadcast_to((P, 2, L))
    sin = g.tab("full_sin").unsqueeze(1).broadcast_to((P, 2, L))
    for name in ("mq", "mk"):
        for i in range(2):
            x, t = g.q2[name][:, 2 * i:2 * i + 2, :], g.w4[:, 0:2, :]
            dve.wait_ge(g.s["pe_projection"], g.at("mm", "swap", name, i))
            dve.tensor_tensor(t, g.bank(("swap", name, i))[:, :].rearrange("p (a b) -> p a b", a=2), sin,
                                         ALU.mult).then_inc(g.s["dve_projection"], 1)
            g.count("dve_projection", ("free", ("swap", name, i)))
            dve.tensor_tensor(x, x, cos, ALU.mult).then_inc(g.s["dve_projection"], 1)
            g.count("dve_projection")
            dve.wait_ge(g.s["dve_projection"], g.so_far("dve_projection"))
            dve.tensor_tensor(x, x, t, ALU.add).then_inc(g.s["dve_projection"], 1)
            g.count("dve_projection", ("rotated", name))
            dve.wait_ge(g.s["dve_projection"], g.so_far("dve_projection"))


def route_pe(g, pe):
    n, w = g.next_weights()
    pe.wait_ge(g.slab_in[n % RING], 16 * (n // RING + 1))
    pe.wait_ge(g.s["dve_norm"], g.at("aT", "ffn1"))
    for t in range(2):
        pe.wait_ge(*g.bank_free())
        ps = g.open(("logits", t))
        for k in range(KD):
            last = mm(pe, ps[:, 0:8], g.aT[:, k, P * t:P * t + P], w[:, 8 * k:8 * k + 8], k == 0, k == KD - 1)
        last.then_inc(g.s["pe_routing"], 1)
        g.count("pe_routing", ("mm", "logits", t))
    g.also("pe_routing", ("used", n))
    for t in range(2):
        for q in range(2):
            pe.wait_ge(*g.bank_free())
            ps = g.open(("by token", t, q))
            for j in range(4):
                last = pe.transpose(ps[:, P * j:P * j + P], g.aT[:, 4 * q + j, P * t:P * t + P], g.tab("ident"))
            last.then_inc(g.s["pe_routing"], 1)
            g.count("pe_routing", ("mm", "by token", t, q))
    pe.wait_ge(g.s["dve_routing"], g.at("chosen", 1))
    pe.wait_ge(*g.bank_free())
    ps = g.open(("ranks",))
    m0, m1 = g.chosen[:, 0, :], g.chosen[:, 1, :]
    mm(pe, ps[:, 0:8], g.tab("before"), m0)
    mm(pe, ps[:, 8:16], g.tab("ones"), m0, True, False)
    mm(pe, ps[:, 8:16], g.tab("before"), m1, False, True)
    mm(pe, ps[:, 16:24], g.tab("ones"), m0, True, False)
    mm(pe, ps[:, 16:24], g.tab("ones"), m1, False, True).then_inc(g.s["pe_routing"], 1)
    g.count("pe_routing", ("mm", "ranks"))


def route_act(g, act):
    for t in range(2):
        act.wait_ge(g.s["dve_routing"], g.at("gap", t))
        act.activation(g.lg[:, t, 33:34], g.lg[:, t, 32:33], ACT.Exp).then_inc(g.s["act_routing"], 1)
        g.count("act_routing", ("exp gap", t))
    for t in range(2):
        for q in range(2):
            act.wait_ge(g.s["pe_routing"], g.at("mm", "by token", t, q))
            act.activation(g.t_tok[:, t, 512 * q:512 * q + 512], g.bank(("by token", t, q))[:, :],
                           ACT.Copy).then_inc(g.s["act_routing"], 1)
            g.count("act_routing", ("free", ("by token", t, q)))


def route_dve(g, dve):
    sem = g.s["dve_routing"]
    f = lambda t, a, n: g.lg[:, t, a:a + n]
    dve.wait_ge(g.s["dve_norm"], g.at("aT", "ffn1"))
    for t in range(2):
        dve.wait_ge(g.s["pe_routing"], g.at("mm", "logits", t))
        dve.tensor_copy(f(t, 0, 8), g.bank(("logits", t))[:, 0:8]).then_inc(sem, 1)
        g.count("dve_routing", ("free", ("logits", t)))
        dve.wait_ge(sem, g.so_far("dve_routing"))
        dve.max(f(t, 8, 8), f(t, 0, 8)).then_inc(sem, 1)
        g.count("dve_routing")
        dve.wait_ge(sem, g.so_far("dve_routing"))
        dve.max_index(f(t, 16, 8).bitcast(mybir.dt.uint32), f(t, 8, 8), f(t, 0, 8)).then_inc(sem, 1)
        g.count("dve_routing")
        dve.tensor_tensor(f(t, 32, 1), f(t, 9, 1), f(t, 8, 1), ALU.subtract).then_inc(sem, 1)
        g.count("dve_routing", ("gap", t))
        dve.wait_ge(sem, g.so_far("dve_routing"))
        dve.tensor_copy(f(t, 24, 8), f(t, 16, 8).bitcast(mybir.dt.uint32)).then_inc(sem, 1)
        g.count("dve_routing")
        dve.wait_ge(g.s["act_routing"], g.at("exp gap", t))
        dve.tensor_scalar(f(t, 34, 1), f(t, 33, 1), 1.0, None, ALU.add).then_inc(sem, 1)
        g.count("dve_routing")
        dve.wait_ge(sem, g.so_far("dve_routing"))
        dve.reciprocal(f(t, 35, 1), f(t, 34, 1)).then_inc(sem, 1)
        g.count("dve_routing")
        dve.wait_ge(sem, g.so_far("dve_routing"))
        dve.tensor_tensor(f(t, 36, 1), f(t, 35, 1), f(t, 33, 1), ALU.mult).then_inc(sem, 1)
        g.count("dve_routing")
        dve.wait_ge(sem, g.so_far("dve_routing"))
        for n, a in ((0, 40), (1, 48)):
            dve.tensor_scalar(f(t, a, 8), g.tab("expert_no"), f(t, 24 + n, 1), f(t, 35 + n, 1), ALU.is_equal,
                              ALU.mult).then_inc(sem, 1)
            g.count("dve_routing")
            dve.tensor_scalar(f(t, a + 16, 8), g.tab("expert_no"), f(t, 24 + n, 1), None, ALU.is_equal).then_inc(sem, 1)
            g.count("dve_routing")
        dve.wait_ge(sem, g.so_far("dve_routing"))
        dve.tensor_tensor(g.rt[:, 0:NE, 2 + t], f(t, 40, 8), f(t, 48, 8), ALU.add).then_inc(sem, 1)
        g.count("dve_routing")
        dve.tensor_tensor(g.chosen[:, t, :], f(t, 56, 8), f(t, 64, 8), ALU.add).then_inc(sem, 1)
        g.count("dve_routing", ("chosen", t))
    dve.wait_ge(g.s["pe_routing"], g.at("mm", "ranks"))
    dve.wait_ge(sem, g.so_far("dve_routing"))
    ps = g.bank(("ranks",))
    for t in range(2):
        dve.scalar_tensor_tensor(f(t, 40, 8), ps[:, 8 * t:8 * t + 8], 1.0, g.chosen[:, t, :], ALU.add,
                                 ALU.mult).then_inc(sem, 1)
        g.count("dve_routing")
    dve.tensor_reduce(f(0, 32, 1), ps[:, 16:24], AX.X, ALU.max).then_inc(sem, 1)
    g.count("dve_routing", ("free", ("ranks",)))
    dve.wait_ge(sem, g.so_far("dve_routing"))
    for t in range(2):
        dve.tensor_scalar(g.rt[:, 0:NE, t], f(t, 40, 8), -1.0, None, ALU.add).then_inc(sem, 1)
        g.count("dve_routing")
    dve.tensor_scalar(g.rounds[:, :], f(0, 32, 1), float(SLOTS), 1.0, ALU.is_gt, ALU.add).then_inc(sem, 1)
    g.count("dve_routing", "rounds")
    dve.wait_ge(sem, g.so_far("dve_routing"))
    dve.tensor_scalar(g.rt[:, NE, 0:2], g.rt[:, 0, 0:2], -float(SLOTS), None, ALU.add).then_inc(sem, 1)
    g.count("dve_routing")
    dve.tensor_copy(g.rt[:, NE, 2:4], g.rt[:, 0, 2:4]).then_inc(sem, 1)
    g.count("dve_routing", "routed")
    dve.wait_ge(sem, g.so_far("dve_routing"))


GU = FE // FC


def rounds_of(g, e):
    return e.value_load(g.rounds[0:1, 0:1], min_val=1, max_val=2)


def experts_pe(g, pe):
    s = g.s
    base = g.next_slab
    pe.wait_ge(s["dve_routing"], g.at("routed"))
    pe.wait_ge(s["act_routing"], g.at("free", ("by token", 1, 1)))
    rounds = rounds_of(g, pe)
    pe.sem_inc(s["pe_experts"], g.per("pe_experts"))
    A, V, Q = g.per("act_experts"), g.per("dve_experts"), g.per("pe_experts")

    def first():
        pe.wait_ge(s["dve_first"], 1)

    for q in range(2):
        if q == 0:
            first()
        for j in range(4):
            k = 4 * q + j
            for t in range(2):
                last = mm(pe, g.psum[4 + q][:, P * j:P * j + P], g.t_tok[:, t, P * k:P * k + P], g.perm[:, t, :], t == 0, t == 1)
        last.then_inc(s["pe_first"], 1)
    g.enter("pe_experts")
    with pe.Fori(0, rounds) as r, pe.Fori(0, NE) as e:
        it = r * NE + e

        def slab(i):
            n = base + i
            pe.wait_ge(g.slab_in[n % RING], 16 * (n // RING + 1) + it * (16 * ES // RING))
            return g.ring[:, n % RING, :]

        def transposes(q):
            pe.wait_ge(s["dve_experts"], g.at("hidden", q + 1) + it * V)
            if q >= 2:
                pe.wait_ge(s["act_experts"], g.at("hT", q - 2) + it * A)
            for j in range(4):
                k = 4 * q + j
                last = pe.transpose(g.psum[4 + q % 2][:, P * j:P * j + P], g.hb[:, P * k:P * k + P], g.tab("ident"))
            last.then_inc(s["pe_experts"], 1)
            g.count("pe_experts", ("turned", q))

        pe.wait_ge(s["act_experts"], g.at("xg", 1) - A + it * A)
        for i in range(GU):
            for n, (what, bank) in enumerate((("gate", i % 2), ("up", 2 + i % 2))):
                w = slab(2 * i + n)
                if i >= 2:
                    pe.wait_ge(s["dve_experts"], g.at("hidden", i - 2) + it * V)
                else:
                    pe.wait_ge(s["dve_experts"], g.at("added", bank) - V + it * V)
                for k in range(KD):
                    last = mm(pe, g.psum[bank][:, 0:FC], g.xg[:, k, :], w[:, FC * k:FC * k + FC], k == 0, k == KD - 1)
                last.then_inc(s["pe_experts"], 1)
                g.count("pe_experts", (what, i))
            if i >= 2:
                transposes(i - 2)
        transposes(GU - 2)
        pe.wait_ge(s["dve_experts"], g.at("weighted") + it * V)
        pe.wait_ge(s["act_experts"], g.at("hT", GU - 3) + it * A)
        for t in range(2):
            last = pe.transpose(g.psum[5][:, P * t:P * t + P], g.pw[:, t, :], g.tab("ident"))
        last.then_inc(s["pe_experts"], 1)
        g.count("pe_experts", "weighted turned")
        for half in range(2):
            for q in range(4):
                w = slab(2 * GU + 4 * half + q)
                if half == 0:
                    pe.wait_ge(s["act_experts"], g.at("hT", min(GU - 2, (7 * q + 6) // 4)) + it * A)
                for k in range(7):
                    last = mm(pe, g.psum[6 + half][:, :], g.hT2[:, 7 * q + k, :], w[:, 512 * k:512 * k + 512],
                              q == 0 and k == 0, q == 3 and k == 6)
                last.then_inc(s["pe_experts"], 1)
                g.count("pe_experts", ("down", half, q))
            if half == 0:
                pe.wait_ge(s["dve_experts"], g.at("slots") + it * V)
                pe.wait_ge(s["act_experts"], g.at("pwt") + it * A)
                for q in range(2):
                    for j in range(4):
                        k = 4 * q + j
                        for t in range(2):
                            last = mm(pe, g.psum[4 + q][:, P * j:P * j + P], g.t_tok[:, t, P * k:P * k + P],
                                      g.perm[:, t, :], t == 0, t == 1)
                    last.then_inc(s["pe_experts"], 1)
                    g.count("pe_experts", ("gathered", q))
        for m in range(4):
            pe.wait_ge(s["act_experts"], g.at("y", m // 2) + it * A)
            for j in range(2):
                c = 256 * m + P * j
                last = mm(pe, g.psum[m][:, L * j:L * j + L], g.yb[:, c:c + P], g.pwt[:, :])
            last.then_inc(s["pe_experts"], 1)
            g.count("pe_experts", ("scattered", m))
    g.leave()
    g.users = {}


def experts_act(g, act):
    s = g.s
    act.wait_ge(s["dve_routing"], g.at("routed"))
    rounds = rounds_of(g, act)
    A, V, Q = g.per("act_experts"), g.per("dve_experts"), g.per("pe_experts")
    for q in range(2):
        act.wait_ge(s["pe_first"], q + 1)
        act.activation(g.xg[:, 4 * q:4 * q + 4, :].rearrange("p a b -> p (a b)"), g.psum[4 + q][:, :],
                       ACT.Copy).then_inc(s["act_first"], 1)
    act.wait_ge(s["act_first"], 2)
    act.sem_inc(s["act_experts"], A)
    g.enter("act_experts")
    with act.Fori(0, rounds) as r, act.Fori(0, NE) as e:
        it = r * NE + e

        def turn(q):
            act.wait_ge(s["pe_experts"], g.at("turned", q) + it * Q)
            act.activation(g.hT2[:, 4 * q:4 * q + 4, :].rearrange("p a b -> p (a b)"), g.psum[4 + q % 2][:, :],
                           ACT.Copy).then_inc(s["act_experts"], 1)
            g.count("act_experts", ("hT", q))

        for i in range(GU):
            act.wait_ge(s["pe_experts"], g.at("gate", i) + it * Q)
            if i >= 2:
                act.wait_ge(s["dve_experts"], g.at("hidden", i - 2) + it * V)
            act.activation(g.sg[:, i % 2, :], g.psum[i % 2][:, 0:FC], ACT.Silu).then_inc(s["act_experts"], 1)
            g.count("act_experts", ("silu", i))
            if i >= 2:
                turn(i - 2)
        turn(GU - 2)
        act.wait_ge(s["pe_experts"], g.at("weighted turned") + it * Q)
        act.activation(g.pwt[:, :], g.psum[5][:, 0:L], ACT.Copy).then_inc(s["act_experts"], 1)
        g.count("act_experts", "pwt")
        act.wait_ge(s["pe_experts"], g.at("down", 0, 3) + it * Q)
        act.activation(g.yb[:, 0:512], g.psum[6][:, :], ACT.Copy).then_inc(s["act_experts"], 1)
        g.count("act_experts", ("y", 0))
        for q in range(2):
            act.wait_ge(s["pe_experts"], g.at("gathered", q) + it * Q)
            act.activation(g.xg[:, 4 * q:4 * q + 4, :].rearrange("p a b -> p (a b)"), g.psum[4 + q][:, :],
                           ACT.Copy).then_inc(s["act_experts"], 1)
            g.count("act_experts", ("xg", q))
        act.wait_ge(s["pe_experts"], g.at("down", 1, 3) + it * Q)
        act.activation(g.yb[:, 512:1024], g.psum[7][:, :], ACT.Copy).then_inc(s["act_experts"], 1)
        g.count("act_experts", ("y", 1))
    g.leave()


def experts_dve(g, dve):
    s = g.s
    rounds = rounds_of(g, dve)
    A, V, Q = g.per("act_experts"), g.per("dve_experts"), g.per("pe_experts")
    dve.tensor_copy(g.cur[:, :], g.rt_flat[:, 0:4]).then_inc(s["dve_round"], 1)
    dve.wait_ge(s["dve_round"], 1)
    for t in range(2):
        last = dve.tensor_scalar(g.perm[:, t, :], g.tab("slot_no"), g.cur[:, t:t + 1], None, ALU.is_equal)
    last.then_inc(s["dve_first"], 1)
    dve.wait_ge(s["dve_first"], 1)
    dve.sem_inc(s["dve_experts"], V)
    g.enter("dve_experts")
    with dve.Fori(0, rounds) as r:
        with dve.Fori(0, NE) as e:
            it = r * NE + e
            dve.wait_ge(s["pe_experts"], g.at("weighted turned") - Q + it * Q)
            for t in range(2):
                last = dve.tensor_scalar(g.pw[:, t, :], g.tab("slot_no"), g.cur[:, t:t + 1], g.cur[:, 2 + t:3 + t],
                                         ALU.is_equal, ALU.mult)
            last.then_inc(s["dve_experts"], 1)
            g.count("dve_experts", "weighted")
            dve.wait_ge(s["dve_experts"], g.so_far("dve_experts") + it * V)
            dve.tensor_copy(g.cur[:, :], g.rt_flat[:, bass.ds(4 * e + 4, 4)]).then_inc(s["dve_experts"], 1)
            g.count("dve_experts")
            dve.wait_ge(s["dve_experts"], g.so_far("dve_experts") + it * V)
            dve.wait_ge(s["pe_experts"], g.at("gate", 0) + it * Q)
            for t in range(2):
                last = dve.tensor_scalar(g.perm[:, t, :], g.tab("slot_no"), g.cur[:, t:t + 1], None, ALU.is_equal)
            last.then_inc(s["dve_experts"], 1)
            g.count("dve_experts", "slots")
            for i in range(GU):
                dve.wait_ge(s["pe_experts"], g.at("up", i) + it * Q)
                dve.wait_ge(s["act_experts"], g.at("silu", i) + it * A)
                dve.tensor_tensor(g.hb[:, FC * i:FC * i + FC], g.psum[2 + i % 2][:, 0:FC], g.sg[:, i % 2, :],
                                  ALU.mult).then_inc(s["dve_experts"], 1)
                g.count("dve_experts", ("hidden", i))
            for m in range(4):
                dve.wait_ge(s["pe_experts"], g.at("scattered", m) + it * Q)
                h = g.hT[:, 2 * m:2 * m + 2, 0:L]
                dve.tensor_tensor(h, g.psum[m][:, :].rearrange("p (a b) -> p a b", a=2), h,
                                  ALU.add).then_inc(s["dve_experts"], 1)
                g.count("dve_experts", ("added", m))
        dve.tensor_scalar(g.rt[:, :, 0:2], g.rt[:, :, 0:2], -float(SLOTS), None, ALU.add).then_inc(s["dve_round"], 1)
        dve.wait_ge(s["dve_round"], r + 2)
    g.leave()
    dve.tensor_copy(g.cur[:, :], g.rt_flat[:, 0:4]).then_inc(s["dve_over"], 1)
    g.count("dve_over", "experts over")


def experts_sp(g, sp):
    s = g.s
    base = next(n for n, x in enumerate(g.slabs) if x[0] == "moe_wg_1_2")
    Q = g.per("pe_experts")
    width = slab_width(g.slabs[base])
    for n in range(base, base + RING):
        sp.wait_ge(*g.moment(("used", n - RING)))
        sp.dma_start(g.ring[:, n % RING, 0:width], g.io["stream"][n, :, 0:width]).then_inc(g.slab_in[n % RING], 16)
    sp.wait_ge(s["dve_routing"], g.at("rounds"))
    rounds = rounds_of(g, sp)

    def ahead(it, e, i):
        n = base + i
        if i < RING:
            sp.wait_ge(s["pe_experts"], g.at(*g.use_of(ES + i - RING)) - Q + it * Q)
        else:
            sp.wait_ge(s["pe_experts"], g.at(*g.use_of(i - RING)) + it * Q)
        src = g.io["stream"][bass.ds(e * ES + n, 1), :, 0:width].rearrange("a p n -> p (a n)")
        sp.dma_start(g.ring[:, n % RING, 0:width], src).then_inc(g.slab_in[n % RING], 16)

    with sp.Fori(0, rounds) as r:
        with sp.If(r > 0):
            for i in range(RING):
                ahead(r * NE, 0, i)
        sp.end_ifs()
        for i in range(RING, ES):
            ahead(r * NE, 0, i)
        with sp.Fori(1, NE) as e:
            for i in range(ES):
                ahead(r * NE + e, e, i)


def store_pe(g, pe):
    pe.wait_ge(g.s["dve_norm"], g.at("aT", "last"))
    for t in range(2):
        for q in range(2):
            pe.wait_ge(*g.bank_free())
            ps = g.open(("out", t, q))
            for j in range(4):
                last = pe.transpose(ps[:, P * j:P * j + P], g.aT[:, 4 * q + j, P * t:P * t + P], g.tab("ident"))
            last.then_inc(g.s["pe_result"], 1)
            g.count("pe_result", ("mm", "out", t, q))


def store_act(g, act):
    for t in range(2):
        for q in range(2):
            act.wait_ge(g.s["pe_result"], g.at("mm", "out", t, q))
            act.activation(g.outs[:, t, 512 * q:512 * q + 512], g.bank(("out", t, q))[:, :], ACT.Copy).then_inc(g.s["act_result"], 1)
            g.count("act_result", ("stored", t))
        act.wait_ge(g.s["act_result"], g.so_far("act_result"))
        act.dma_start(g.io["out"][P * t:P * t + P, :], g.outs[:, t, :]).then_inc(g.out_sem, 16)
    act.wait_ge(g.out_sem, 32)


def plain_norm(g, kind, e, key, gain, ready):
    if kind == "act":
        norm_act(g, e, key, g.hT, L, None, None, [ready])
    if kind == "pe":
        norm_pe(g, e, key, L)
    if kind == "dve":
        norm_dve(g, e, key, g.hT, L, lambda k, s: g.v(gain, k), None)


def second_block(g, kind, e):
    def only(k, f, *a):
        if kind == k:
            f(g, e, *a)
    g.tab_at = packed(tables_b())[1]
    if kind == "act":
        e.wait_ge(g.s["dve_norm"], g.at("aT", ("final", 1)))
        e.dma_start(g.tabs[:, 0:g.io["tab_b"].shape[1]], g.io["tab_b"]).then_inc(g.const_in["tab_b"], 16)
        g.const_issued.append("tab_b")
    if kind in ("pe", "dve"):
        e.wait_ge(g.const_in["tab_b"], 16)
    plain_norm(g, kind, e, "mix0", "norm_mix_0_2", ("aT", ("final", 1)))
    only("pe", even_proj_pe)
    only("act", even_proj_act)
    g.check(kind, "eproj", 0)
    only("dve", delta_in_dve)
    only("act", delta_in_act)
    only("pe", delta_in_pe)
    g.check(kind, "din", 0)
    for t in range(2):
        only("pe", delta_pe, t)
        only("act", delta_act, t)
        only("dve", delta_dve, t)
    only("dve", delta_out_dve)
    only("act", delta_out_act)
    only("pe", delta_out_pe)
    g.check(kind, "delta", 0)
    only("act", mla_act)
    only("pe", mla_pe)
    only("dve", mla_dve)
    a = causal_of(g, g.mq, g.mk, g.mv, lambda p: g.aT[:, 4 + p, 0:L], ["mla have", ("mla rotated", 4)], rows=96)
    only("pe", attn_pe, "mla", a)
    only("act", attn_act, "mla", a)
    only("dve", attn_dve, "mla", a)
    g.check(kind, "mla", 0)
    only("pe", out_pe, "e", L, ["y delta", ("attended", "mla")])
    only("dve", add_dve, "wo", "e", L, None)
    plain_norm(g, kind, e, "ffn0", "norm_ffn_0_2", ("h", "wo", "e"))
    only("pe", glu_pe, "e", KF, ("aT", "ffn0"))
    only("act", glu_act, "e", KF)
    only("dve", glu_dve, "e", KF)
    only("dve", add_dve, "gd", "e", L, None)
    g.check(kind, "even", 0)
    plain_norm(g, kind, e, "mix1", "norm_mix_1_2", ("h", "gd", "e"))
    only("pe", odd_proj_pe)
    only("act", odd_proj_act)
    only("dve", odd_proj_dve)
    q = g.q2
    for name, a in (("fox", causal_of(g, q["fq"], q["fk"], q["fv"], lambda p: g.aT[:, p, 0:L],
                                      [("have", "fv"), "minus D"], d=g.negd)),
                    ("moba", causal_of(g, q["mq"], q["mk"], q["mv"], lambda p: g.aT[:, 4 + p, 0:L],
                                       [("have", "mv"), ("rotated", "mk")]))):
        only("pe", attn_pe, name, a)
        only("act", attn_act, name, a)
        only("dve", attn_dve, name, a)
    g.check(kind, "oattn", 0)
    only("pe", out_pe, "o", L, [("attended", "fox"), ("attended", "moba")])
    only("dve", add_dve, "wo", "o", L, None)
    plain_norm(g, kind, e, "ffn1", "norm_ffn_1_2", ("h", "wo", "o"))
    only("pe", route_pe)
    only("act", route_act)
    only("dve", route_dve)
    g.check(kind, "route", 0)
    only("pe", experts_pe)
    only("act", experts_act)
    only("dve", experts_dve)
    plain_norm(g, kind, e, "last", "final_norm_2", "experts over")
    only("pe", store_pe)
    only("act", store_act)


class Stop(Exception):
    pass


def first_block(g, kind, e):
    def only(k, f, *a):
        if kind == k:
            f(g, e, *a)
    if kind == "act":
        consts_act(g, e)
        silu_act(g, e)
        e.wait_ge(g.const_in["h0"], 16)
    for l in range(2):
        T = T2 if l == 0 else L
        only("pe", mod_pe, l)
        only("dve", mod_dve, l)
        n1 = ("n1", l)
        if kind == "act":
            ready = [("gain", l, 0)] + ([("h", "dn", 0)] if l else [])
            norm_act(g, e, n1, g.hT, T2, lambda k, s: g.gain[:, l, 0, k, s:s + 1], lambda k, s: g.mod[:, l, k, s:s + 1], ready)
        if kind == "pe":
            e.wait_ge(g.const_in["tab_a"], 16)
            norm_pe(g, e, n1, T2)
        only("dve", norm_dve, n1, g.hT, T2, None, True)
        only("act", bias_act, l)
        only("pe", proj_pe, l)
        only("act", proj_act, l)
        only("dve", proj_dve, l)
        g.check(kind, "proj", l)
        only("pe", pool_pe, l)
        only("act", pool_act, l)
        only("dve", bias_dve, l)
        for name, a in [("na", na_of(g, l))] + ([("ctx", ctx_attn_of(g, l))] if l == 0 else []):
            only("pe", attn_pe, (name, l), a)
            only("act", attn_act, (name, l), a)
            only("dve", attn_dve, (name, l), a)
        g.check(kind, "attn", l)
        only("act", ret_act, l)
        only("pool", ret_pool, l)
        only("pe", ret_pe, l)
        only("dve", ret_dve, l)
        g.check(kind, "ret", l)
        only("pe", out_pe, l, T, [("y ret", l), ("y pool", l), ("attended", ("ctx" if l == 0 else "na", l))])
        only("dve", add_dve, "wo", l, T, lambda m, s: g.mod[:, l, 16 + m, s:s + 1])
        g.check(kind, "wo", l)
        n2 = ("n2", l)
        if kind == "act":
            norm_act(g, e, n2, g.hT, T, lambda k, s: g.gain[:, l, 1, k, s:s + 1],
                     lambda k, s: g.mod[:, l, 24 + k, s:s + 1], [("h", "wo", l)])
        only("pe", norm_pe, n2, T)
        only("dve", norm_dve, n2, g.hT, T, None, True)
        only("pe", ffn1_pe, l, T)
        only("act", ffn1_act, l, T)
        only("dve", ffn1_dve, l, T)
        only("dve", add_dve, "dn", l, T, lambda m, s: g.mod[:, l, 40 + m, s:s + 1])
        g.check(kind, "ffn", l)
    key = ("final", 1)
    if kind == "act":
        norm_act(g, e, key, g.hT, L, None, None, [("h", "dn", 1)])
    only("pe", norm_pe, key, L)
    if kind == "dve":
        norm_dve(g, e, key, g.hT, L, lambda k, s: g.v("final_g", k), None, dst=g.hT)
    g.check(kind, "final1", 0)


def build(nc, io, at, stop=None):
    g = Program(nc, io, at, stop)

    def check(kind, name, l):
        if stop == (name, l):
            raise Stop()

    g.check = check
    with ExitStack() as ctx:
        g.ctx = ctx
        g.slabs = slabs()
        g.next_slab = 0
        g.const_issued, g.biases = [], 0
        g.vec_at, nv = vector_places()
        g.hT, g.aT = g.sb("hT", KD, T2), g.sb("aT", KD, T2)
        g.ring = g.sb("ring", RING, SLOT)
        g.vec = g.sb("vectors", nv)
        na, nb = io["tab_a"].shape[1], io["tab_b"].shape[1]
        g.tabs = g.sb("tables", max(na, nb))
        g.tab_at = packed(tables_a())[1]
        g.pool_w = g.sb("pool_w", 2, 4, 64)
        g.cs, g.mod, g.gain = g.sb("silu_c", KD, 2), g.sb("modulation", 2, 48, 2), g.sb("gain", 2, 2, KD, 2)
        g.cend = g.sb("chunk_ends", 4, 8)
        g.rstd, g.eps = g.sb("rstd", T2), g.sb("eps", 4)
        g.nmax, g.rsum, g.rinv = g.sb("nmax", 4), g.sb("rsum", 4), g.sb("rinv", 4)
        big = g.sb("activations", 14976)
        tmp = g.sb("scratch", 4608)
        g.big, g.tmp = big, tmp

        def part(t, at_, *shape):
            n = int(np.prod(shape))
            v = t[:, at_:at_ + n]
            if len(shape) == 2:
                return v.rearrange("p (a b) -> p a b", a=shape[0])
            if len(shape) == 3:
                return v.rearrange("p (a b c) -> p a b c", a=shape[0], b=shape[1])
            return v

        g.part = part
        g.m1 = {n: part(big, 1536 * i, 3, 512) for i, n in enumerate(("naq", "nak", "rq", "rk", "gate"))}
        g.m1["nav"], g.m1["rv"] = part(big, 7680, 4, 384), part(big, 9216, 4, 384)
        g.m1["pool"] = part(big, 10752, 4, 256)
        g.bias, g.bias_flat = part(big, 11776, 12, 256), big[:, 11776:14848]
        g.hid = part(big, 0, KF, 512)
        g.probs, g.probsT = part(tmp, 0, 3, 512), part(tmp, 1536, 3, 512)
        g.banded = part(tmp, 3072, 2, 512)
        g.ret_e, g.ret_f, g.ret_a = part(tmp, 0, 4, 384), tmp[:, 1536:3072].rearrange("p (a b c) -> p a b c", a=2, b=2), part(tmp, 3072, 3, 512)
        g.conv = part(tmp, 0, 2, 2, 512)
        second_places(g)
        g.rounds = ctx.enter_context(nc.sbuf_tensor("rounds", [P, 1], mybir.dt.int32))
        g.s = {n: ctx.enter_context(nc.semaphore(n)) for n in SEMAPHORES}
        g.counts = {n: 0 for n in SEMAPHORES}
        g.psum = [ctx.enter_context(nc.psum_tensor(f"bank{i}", [P, 512], F32)) for i in range(8)]
        g.slab_in = [ctx.enter_context(nc.semaphore(f"slab_in_slot{i}")) for i in range(RING)]
        g.const_in = {n: ctx.enter_context(nc.semaphore(f"{n}_in")) for n in ("vec", "h0", "tab_a", "tab_b", "pool_w")}
        g.bias_in, g.out_sem = ctx.enter_context(nc.semaphore("bias_in")), ctx.enter_context(nc.semaphore("out_stored"))
        block = ctx.enter_context(nc.Block())

        def run(kind, e):
            g.tab_at = packed(tables_a())[1]
            try:
                first_block(g, kind, e)
                second_block(g, kind, e)
            except Stop:
                pass

        @block.tensor
        def _(pe):
            run("pe", pe)
            g.used_slabs = g.next_slab

        @block.scalar
        def _(act):
            run("act", act)

        @block.vector
        def _(dve):
            dve.memset(g.eps[:, 0:1], EPS).then_inc(g.s["dve_start"], 1)
            g.count("dve_start")
            dve.memset(g.eps[:, 1:2], 64e-5).then_inc(g.s["dve_start"], 1)
            g.count("dve_start", "eps")
            run("dve", dve)

        @block.gpsimd
        def _(pool):
            run("pool", pool)

        @block.sync
        def _(sp):
            if g.stop:
                g.slabs = g.slabs[:g.used_slabs]
            loads_sp(g, sp)
            if not g.stop:
                experts_sp(g, sp)
            for name in g.const_issued:
                sp.wait_ge(g.const_in[name], 16)
            sp.wait_ge(g.bias_in, 16 * g.biases)
    return g


def kernel(**inputs):
    import numpy as _np
    import concourse.bacc as _bacc
    from concourse.bass_utils import run_bass_kernel_spmd as _run

    arrays = {f"in_{k}": v for k, v in lay_out({k: _np.asarray(v) for k, v in inputs.items()}).items()}

    def program(at):
        nc = _bacc.Bacc("TRN2", target_bir_lowering=False, num_devices=1)
        io = {k[3:]: nc.dram_tensor(k, v.shape, F32, kind="ExternalInput").ap() for k, v in arrays.items()}
        io["out"] = nc.dram_tensor("out", (L, D), F32, kind="ExternalOutput").ap()
        return nc, build(nc, io, at)

    _, counted = program({})
    _, counted = program(counted.now)
    nc, _ = program(counted.now)
    got = _run(nc, [arrays], core_ids=[0]).results[0]["out"]
    return got.reshape(1, L, D)
```

```python
from contextlib import ExitStack

import numpy as np

import concourse.bass as bass
from concourse import mybir

F32 = mybir.dt.float32
F32R = mybir.dt.float32r
ALU = mybir.AluOpType
ACT = mybir.ActivationFunctionType
AX = mybir.AxisListType

P = 128
D = 1024
KD = D // P
L = 256
T2 = 2 * L
HD = 64
GRID_W, NA_KW, NA_KH = 64, 16, 8
POOL_WINDOWS = (2, 4, 8, 16)
NAH = RETH = 6
FF = 2816
KF = FF // P
NE, FE = 8, 3584
KE = FE // P
FC = 448
ES = 2 * FE // FC + 8
SLOTS = P
CH = 32
EPS = 1e-6
SLOT = 4096
RING = 3
EXPERT_RING = 4
NEG = -1e30


def tables_a():
    p = np.arange(P)
    out = {}
    out["ident"] = np.eye(P)
    out["ones"] = np.ones((P, P))
    out["headones"] = (p[:, None] // HD == p[None, :] // HD) * 1.0
    c = p % HD
    half, within = c // 32, c % 32
    inv = (10000.0 ** (-np.arange(16, dtype=np.float32) / 16)).astype(np.float32)
    t = np.arange(L)
    pos = np.where(half[:, None] == 0, (t // GRID_W)[None, :], (t % GRID_W)[None, :]).astype(np.float32)
    ang = pos * inv[within % 16][:, None]
    out["rot_cos"] = np.cos(ang)
    out["rot_sin"] = np.where((within < 16)[:, None], -np.sin(ang), np.sin(ang))
    out["rot_swap"] = (p[:, None] == (p ^ 16)[None, :]) * 1.0
    qc = p % GRID_W
    kc = np.arange(L) % GRID_W
    ws = np.clip(qc - NA_KW // 2, 0, GRID_W - NA_KW)
    ok = (kc[None, :] >= ws[:, None]) & (kc[None, :] < ws[:, None] + NA_KW)
    out["na_mask"] = np.where(ok, 0.0, NEG)
    m = np.zeros((L, 4, L))
    for g, w in enumerate(POOL_WINDOWS):
        lo, hi = np.clip(t - w // 2, 0, L), np.clip(t - w // 2 + w, 0, L)
        inside = (t[:, None] >= lo[None, :]) & (t[:, None] < hi[None, :])
        m[:, g, :] = inside / (hi - lo)[None, :] - np.eye(L)
    out["pool"] = m.reshape(2, P, 4, L).transpose(1, 0, 2, 3).reshape(P, -1)
    d = np.arange(3 * P)[None, :] - P - p[:, None]
    out["d_fwd"] = np.maximum(d, 0)
    out["d_bwd"] = np.maximum(-d, 0)
    out["m_fwd"] = (d >= 0) * 1.0
    out["m_bwd"] = (d <= 0) * 1.0
    out["d_cf"] = L + d
    out["d_cb"] = L - d
    return out


def tables_b():
    p = np.arange(P)
    t = np.arange(L)
    out = {}
    out["ident"] = np.eye(P)
    out["ones"] = np.ones((P, P))
    out["before"] = (p[:, None] < p[None, :]) * 1.0
    out["slot_no"] = np.broadcast_to(np.arange(128.0), (P, P))
    out["expert_no"] = np.broadcast_to(np.arange(8.0), (P, 8))
    out["headones"] = (p[:, None] // HD == p[None, :] // HD) * 1.0
    out["causal"] = np.where(p[None, :] <= p[:, None], 0.0, NEG)
    same = p[:, None] // CH == p[None, :] // CH
    strict, incl = (same & (p[:, None] < p[None, :])) * 1.0, (same & (p[:, None] <= p[None, :])) * 1.0
    out["chunk_masks"] = np.stack([strict, incl, strict, incl], 1).reshape(P, -1)
    out["strict_low"] = np.stack([strict.T] * 4, 1).reshape(P, -1)
    out["keep"] = np.broadcast_to(np.arange(4 * L) % CH != 0, (P, 4 * L)) * 1.0
    i16 = (10000.0 ** (-np.arange(0, 32, 2, dtype=np.float32) / 32)).astype(np.float32)
    a = t.astype(np.float32)[None, :] * i16[(p % 32) % 16][:, None]
    rows = (p >= 64) & (p < 96)
    out["mla_cos"] = np.where(rows[:, None], np.cos(a), 1.0)
    out["mla_sin"] = np.where(rows[:, None], np.where((p % 32 < 16)[:, None], -np.sin(a), np.sin(a)), 0.0)
    out["mla_swap"] = ((p[:, None] == (p ^ 16)[None, :]) & rows[:, None]) * 1.0
    i32 = (10000.0 ** (-np.arange(0, 64, 2, dtype=np.float32) / 64)).astype(np.float32)
    a = t.astype(np.float32)[None, :] * i32[(p % 64) % 32][:, None]
    out["full_cos"] = np.cos(a)
    out["full_sin"] = np.where((p % 64 < 32)[:, None], -np.sin(a), np.sin(a))
    out["full_swap"] = (p[:, None] == (p ^ 32)[None, :]) * 1.0
    out["row"] = ((p[:, None, None] == np.arange(8)[None, :, None]) * np.ones((1, 1, P))).reshape(P, -1)
    return out


def packed(tables):
    at, parts, n = {}, [], 0
    for name, v in tables.items():
        v = np.ascontiguousarray(v, np.float32)
        at[name] = (n, v.shape[1])
        parts.append(v)
        n += v.shape[1]
    return np.concatenate(parts, 1), at


VECTORS = [
    ("c", 1, D), ("c_ctx", 1, D), ("b_mod", 2, 6 * D), ("norm1_g", 2, D), ("norm2_g", 2, D), ("pool_scale", 2, 256),
    ("ret_gn_g", 2, 384), ("conv_w", 6, 2 * FF), ("conv_b", 2, 2 * FF), ("final_g", 1, D), ("norm_mix_0_2", 1, D),
    ("shift_mu_0_2", 1, 1792), ("rw_w0_0_2", 1, 512), ("rw_a0_0_2", 1, 512), ("rw_kk_0_2", 1, 512),
    ("rw_ka_0_2", 1, 512), ("rw_rk_0_2", 1, 512), ("rw_lnx_g_0_2", 1, 512), ("rw_lnx_b_0_2", 1, 512),
    ("mla_qnorm_0_2", 1, 256), ("mla_kvnorm_0_2", 1, 128), ("norm_ffn_0_2", 1, D), ("norm_mix_1_2", 1, D),
    ("norm_ffn_1_2", 1, D), ("final_norm_2", 1, D),
]
SPREAD = [("ret_decay_fwd", 12), ("ret_decay_bwd", 12)]


def vector_places():
    at, n = {}, 0
    for name, rows, width in VECTORS:
        at[name] = n
        n += rows * width // P
    for name, width in SPREAD:
        at[name] = n
        n += width
    at["fox_bf_1_2"] = n
    return at, n + 1


def slabs():
    out = []

    def cols(w, layer, lists, kt=KD):
        for c in lists:
            out.append((w, layer, kt, c))

    def r(a, n):
        return [(a, n)]

    for l in range(2):
        cols("w_mod", l, [r(512 * i, 512) for i in range(12)])
        cols("w_in", l, [r(0, 256)] + [r(256 + 384 * i, 384) for i in range(7)])
        cols("w_out", l, [r(512 * i, 512) for i in range(2)])
        cols("w_up", l, [[(256 * i, 256), (FF + 256 * i, 256)] for i in range(KF // 2)])
        cols("w_down", l, [r(P * i, P) for i in range(KD)], KF)
    cols("w_in_0_2", None, [r(512 * i, 512) for i in range(4)] + [r(2048, 160)])
    out.append(("lora", None, 0, None))
    cols("w_out_0_2", None, [r(512 * i, 512) for i in range(2)])
    for i in range(KF // 2):
        out.append(("ffn_gu", None, KD, [(256 * i, 256)]))
    cols("ffn_wd_0_2", None, [r(P * i, P) for i in range(KD)], KF)
    cols("w_in_1_2", None, [r(512 * i, 512) for i in range(3)] + [r(1544 + 512 * i, 512) for i in range(3)] + [r(1536, 8)])
    cols("w_out_1_2", None, [r(512 * i, 512) for i in range(2)])
    cols("router_1_2", None, [r(0, 8)])
    for e in range(NE):
        for i in range(FE // FC):
            out.append(("moe_wg_1_2", e, KD, [(FC * i, FC)]))
            out.append(("moe_wu_1_2", e, KD, [(FC * i, FC)]))
        for half in range(2):
            for q in range(4):
                out.append(("moe_down", e, KE // 4, (half, q)))
    out += [("moe_wg_1_2", 0, KD, [(0, FC)]), ("moe_wu_1_2", 0, KD, [(0, FC)])]
    return out




def is_split(s):
    name, layer, kt, lists = s
    if name in ("w_in_0_2", "w_in_1_2"):
        return lists[0][1] == 512
    return name in ("w_in", "w_up", "ffn_gu", "ffn_wd_0_2") or (name, layer) == ("w_down", 1)


def slab_width(s):
    name, _, kt, lists = s
    if name == "moe_down":
        return kt * 512
    if name == "lora":
        return 3584
    n = kt * sum(n for _, n in lists)
    return 2 * n if name == "ffn_gu" else n


def lay_out(x):
    every = slabs()
    stream = np.zeros((len(every), P, SLOT), np.float32)
    for n, (name, layer, kt, lists) in enumerate(every):
        if name == "lora":
            lo = stream[n]
            lo[0:64, 0:512] = x["rw_w2_0_2"]
            lo[64:128, 0:512] = x["rw_a2_0_2"]
            lo[:, 512:1024] = x["rw_g2_0_2"]
            lo[:, 1024:2560] = x["mla_wuq_0_2"].reshape(2, P, 768).transpose(1, 0, 2).reshape(P, -1)
            lo[:, 2560:3584] = x["mla_wukv_0_2"]
            continue
        if name == "moe_down":
            half, q = lists
            w = x["moe_wd_1_2"][layer, kt * P * q:kt * P * (q + 1), 512 * half:512 * half + 512]
            stream[n, :, :kt * 512] = w.reshape(kt, P, 512).transpose(1, 0, 2).reshape(P, -1)
            continue
        if name == "ffn_gu":
            ws = [x["ffn_wg_0_2"], x["ffn_wu_0_2"]]
        else:
            ws = [x[name] if layer is None else x[name][layer]]
        parts = [w[:, a:a + m] for w in ws for a, m in lists]
        m = sum(w.shape[1] for w in parts)
        v = stream[n, :, :kt * m].reshape(P, kt, m)
        at = 0
        for w in parts:
            v[:, :, at:at + w.shape[1]] = w.reshape(kt, P, -1).transpose(1, 0, 2)
            at += w.shape[1]
    at, n = vector_places()
    vec = np.zeros((P, n), np.float32)
    for name, rows, width in VECTORS:
        k = rows * width // P
        vec[:, at[name]:at[name] + k] = np.ascontiguousarray(x[name]).reshape(k, P).T
    for name, width in SPREAD:
        vec[:, at[name]:at[name] + width] = np.ascontiguousarray(x[name]).reshape(1, width)
    vec[0:8, at["fox_bf_1_2"]] = x["fox_bf_1_2"]
    tok = np.concatenate([x["x"][0], x["ctx"][0]], 0)
    hT = np.ascontiguousarray(tok.reshape(T2, KD, P).transpose(2, 1, 0))
    pw = np.zeros((P, 2, 4, 64), np.float32)
    pw[0:64] = x["pool_w"].transpose(2, 0, 1, 3)
    pw[64:128] = pw[0:64]
    q = np.arange(L)
    dr = (q[None, :] // GRID_W) - (q[:, None] // GRID_W) + NA_KH - 1
    dc = np.clip((q[None, :] % GRID_W) - (q[:, None] % GRID_W) + NA_KW - 1, 0, 2 * NA_KW - 2)
    rpb = np.ascontiguousarray(x["na_rpb"][:, :, dr, dc].reshape(2, NAH, 2, P, L).transpose(0, 3, 1, 2, 4))
    return {"stream": stream, "vec": vec, "h0": hT, "pool_w": pw, "rpb": rpb.reshape(2, P, NAH * 2 * L),
            "tab_a": packed(tables_a())[0], "tab_b": packed(tables_b())[0]}


SEMAPHORES = (
    "act_attention", "dve_attention", "pe_attention", "act_delta", "dve_delta", "pe_delta", "act_experts",
    "dve_experts", "pe_experts", "act_feedforward", "dve_feedforward", "pe_feedforward", "act_first", "dve_first",
    "pe_first", "act_latent", "dve_latent", "pe_latent", "act_modulation", "dve_modulation", "pe_modulation",
    "act_norm", "dve_norm", "pe_norm", "dve_over", "act_pooling", "pe_pooling", "act_projection", "dve_projection",
    "pe_projection", "dve_residual", "pe_residual", "act_result", "pe_result", "act_retention", "dve_retention",
    "pe_retention", "pool_retention", "dve_round", "act_routing", "dve_routing", "pe_routing",
    "act_split", "dve_split", "act_pieces", "dve_pieces", "pe_pieces", "dve_start",
)


class Program:

    def __init__(self, nc, io, earlier, stop=None):
        self.nc, self.io, self.earlier, self.now = nc, io, earlier, {}
        self.stop = stop
        self.bank_of, self.users = {}, {}
        self.turn = {"short": 0, "long": 0}

    def count(self, sem, key=None):
        self.counts[sem] += 1
        if key is not None:
            self.also(sem, key)

    def also(self, sem, key):
        self.now[key] = (sem, self.counts[sem])

    def at(self, *key):
        return self.earlier[key if len(key) > 1 else key[0]][1] if self.earlier else 1

    def moment(self, key):
        name, value = self.earlier[key] if self.earlier else ("dve_start", 1)
        return self.s[name], value

    def per(self, sem):
        return self.earlier.get(("per", sem), 1)

    def enter(self, sem):
        self.counts[sem] += self.per(sem)
        self.entered = (sem, self.counts[sem])

    def leave(self):
        sem, start = self.entered
        self.now[("per", sem)] = self.counts[sem] - start

    def use_of(self, i):
        if i < 2 * FE // FC:
            return (("gate", "up")[i % 2], i // 2)
        return ("down", (i - 2 * FE // FC) // 4, (i - 2 * FE // FC) % 4)

    def so_far(self, sem):
        return self.counts[sem]

    def sb_both(self, name, *shape):
        with self.nc.sbuf_tensor(name + "_rounded", [P, *shape], F32R) as rounded:
            ROUNDED[name] = rounded
        return self.sb(name, *shape)

    def sb(self, name, *shape):
        return self.ctx.enter_context(self.nc.sbuf_tensor(name, [P, *shape], F32))

    def next_bank(self, kind):
        banks = range(0, 6) if kind == "short" else range(6, 8)
        return banks[self.turn[kind] % len(banks)]

    def bank_free(self, kind="short"):
        b = self.next_bank(kind)
        return self.moment(("free", self.users[b]) if b in self.users else "eps")

    def open(self, key, kind="short"):
        b = self.next_bank(kind)
        self.turn[kind] += 1
        self.users[b] = key
        self.bank_of[key] = b
        self.now[("bank", key)] = b
        return self.psum[b]

    def bank(self, key):
        return self.psum[self.earlier.get(("bank", key), 0)]

    def next_weights(self):
        n = self.next_slab
        self.next_slab += 1
        return n, self.ring[:, n % RING, :]

    def v(self, name, i=0):
        a = self.vec_at[name] + i
        return self.vec[:, a:a + 1]

    def tab(self, name):
        a, n = self.tab_at[name]
        return self.tabs[:, a:a + n]


ROUNDED = {}


def exact(ap):
    return bass.AP(tensor=ROUNDED[ap.tensor.name], offset=ap.offset, ap=ap.ap)


def rounded(ap):
    return exact(ap).bitcast(F32)


def mm3(pe, out, upper, lower, w_upper, w_lower, start, stop):
    pe.matmul(out, exact(upper), exact(w_upper), start=start, stop=False)
    pe.matmul(out, exact(upper), exact(w_lower), start=False, stop=False)
    return pe.matmul(out, exact(lower), exact(w_upper), start=False, stop=stop)


def mm(pe, out, lhsT, rhs, start=True, stop=True):
    return pe.matmul(out, lhsT, rhs, start=start, stop=stop)


def loads_sp(g, sp):
    for n, s in enumerate(g.slabs):
        if s[0] == "moe_wg_1_2":
            break
        if n >= RING:
            sp.wait_ge(*g.moment(("used", n - RING)))
        w = slab_width(s)
        sp.dma_start(g.ring[:, n % RING, 0:w], g.io["stream"][n, :, 0:w]).then_inc(g.slab_in[n % RING], 16)


def consts_act(g, act):
    for name, dst in (("vec", g.vec[:, :]), ("h0", g.hT[:, :, :]), ("tab_a", g.tabs[:, 0:g.io["tab_a"].shape[1]]),
                      ("pool_w", g.pool_w[:, :, :, :])):
        act.dma_start(dst, g.io[name]).then_inc(g.const_in[name], 16)
        g.const_issued.append(name)


def piece(g, p):
    n = g.slab_of[p]
    w = slab_width(g.slabs[n]) // 2
    h = p - g.piece_of[n]
    return g.ring[:, n % RING, w * h:w * h + w], g.piece_upper[p % 2][:, 0:w]


def upper_act(g, act, count):
    for p in range(g.uppers, min(g.uppers + count, len(g.slab_of))):
        n = g.slab_of[p]
        w, upper = piece(g, p)
        act.wait_ge(g.slab_in[n % RING], 16 * (n // RING + 1))
        if p >= 2:
            act.wait_ge(*g.moment(("piece used", p - 2)))
        act.activation(exact(upper), w, ACT.Copy).then_inc(g.s["act_pieces"], 1)
        g.count("act_pieces", ("upper", p))
    g.uppers += count


def lower_dve(g, dve, count):
    for p in range(g.lowers, min(g.lowers + count, len(g.slab_of))):
        w, upper = piece(g, p)
        dve.wait_ge(g.s["act_pieces"], g.at("upper", p))
        dve.tensor_tensor(exact(w), w, rounded(upper), ALU.subtract).then_inc(g.s["dve_pieces"], 1)
        g.count("dve_pieces", ("piece", p))
    g.lowers += count


def products(g, pe, slab, kt, outs, stage, x_ready=None):
    n, _ = g.next_weights()
    cols = slab_width(slab) // kt
    banks = {}
    for h in range(2):
        p = g.piece_of[n] + h
        wl, wu = piece(g, p)
        pe.wait_ge(g.s["dve_pieces"], g.at("piece", p))
        for i, (group, at, (a, m), tokens, moment) in enumerate(outs):
            if h == 0:
                pe.wait_ge(*g.bank_free())
                banks[i] = g.open(group)
            for k in range(kt // 2):
                kk = kt // 2 * h + k
                if i == 0 and x_ready is not None:
                    pe.wait_ge(*g.moment((*x_ready, kk)))
                xu, xl = g.x(kk)
                c = slice(cols * k + a, cols * k + a + m)
                first, last_k = kk == 0, kk == kt - 1
                if tokens is None:
                    last = mm3(pe, banks[i][:, at], wu[:, c], wl[:, c], xu, xl, first, last_k)
                else:
                    t = slice(P * tokens, P * tokens + P)
                    last = mm3(pe, banks[i][:, at], xu[:, t], xl[:, t], wu[:, c], wl[:, c], first, last_k)
            if h == 1:
                last.then_inc(g.s["pe_" + stage], 1)
                g.count("pe_" + stage, moment)
        if h == 0:
            last.then_inc(g.s["pe_pieces"], 1)
            g.count("pe_pieces", ("piece used", p))
        else:
            g.now[("piece used", p)] = ("pe_" + stage, g.counts["pe_" + stage])
    g.also("pe_" + stage, ("used", n))


def silu_act(g, act):
    act.wait_ge(g.const_in["vec"], 16)
    for i, n in enumerate(("c", "c_ctx")):
        a = g.vec_at[n]
        act.activation(g.cs[:, :, i], g.vec[:, a:a + KD], ACT.Silu).then_inc(g.s["act_modulation"], 1)
        g.count("act_modulation", ("silu_c", i))


def mod_pe(g, pe, l):
    pe.wait_ge(g.s["act_modulation"], g.at("silu_c", 0))
    pe.wait_ge(g.s["act_modulation"], g.at("silu_c", 1))
    pe.wait_ge(g.const_in["tab_a"], 16)
    for i in range(13):
        if i < 12:
            n, w = g.next_weights()
            pe.wait_ge(g.slab_in[n % RING], 16 * (n // RING + 1))
            pe.wait_ge(*g.bank_free())
            ps = g.open(("mod rows", l, i))
            for k in range(KD):
                last = mm(pe, ps[0:2, :], g.cs[:, k, :], w[:, 512 * k:512 * k + 512], k == 0, k == KD - 1)
            last.then_inc(g.s["pe_modulation"], 1)
            g.count("pe_modulation", ("used", n))
            g.also("pe_modulation", ("mm", "mod rows", l, i))
        if i >= 1:
            pe.wait_ge(g.s["act_modulation"], g.at("free", ("mod rows", l, i - 1)))
            pe.wait_ge(*g.bank_free())
            ps = g.open(("mod", l, i - 1))
            for j in range(4):
                last = pe.transpose(ps[:, 2 * j:2 * j + 2], g.mod_rows[0:2, (i - 1) % 2, P * j:P * j + P],
                                    g.tab("ident")[0:2, 0:2])
            last.then_inc(g.s["pe_modulation"], 1)
            g.count("pe_modulation", ("mm", "mod", l, i - 1))


def mod_act(g, act, l):
    for i in range(12):
        act.wait_ge(g.s["pe_modulation"], g.at("mm", "mod rows", l, i))
        if i >= 2:
            act.wait_ge(g.s["pe_modulation"], g.at("mm", "mod", l, i - 2))
        act.activation(g.mod_rows[0:2, i % 2, :], g.bank(("mod rows", l, i))[0:2, :], ACT.Copy).then_inc(g.s["act_modulation"], 1)
        g.count("act_modulation", ("free", ("mod rows", l, i)))


def mod_dve(g, dve, l):
    dve.wait_ge(g.const_in["vec"], 16)
    a = g.vec_at["b_mod"] + 48 * l
    for i in range(12):
        dve.wait_ge(g.s["pe_modulation"], g.at("mm", "mod", l, i))
        ps = g.bank(("mod", l, i))[:, 0:8].rearrange("p (c s) -> p c s", s=2)
        b = g.vec[:, a + 4 * i:a + 4 * i + 4].unsqueeze(2).broadcast_to((P, 4, 2))
        dve.tensor_tensor(g.mod[:, l, 4 * i:4 * i + 4, :], ps, b, ALU.add).then_inc(g.s["dve_modulation"], 1)
        g.count("dve_modulation", ("free", ("mod", l, i)))
    dve.wait_ge(g.s["dve_modulation"], g.so_far("dve_modulation"))
    for n, (name, c) in enumerate((("norm1_g", 8), ("norm2_g", 32))):
        a = g.vec_at[name] + KD * l
        gain = g.vec[:, a:a + KD].unsqueeze(2).broadcast_to((P, KD, 2))
        dve.scalar_tensor_tensor(g.gain[:, l, n, :, :], g.mod[:, l, c:c + KD, :], 1.0, gain,
                                            ALU.add, ALU.mult).then_inc(g.s["dve_modulation"], 1)
        g.count("dve_modulation", ("gain", l, n))


def norm_act(g, act, key, src, T, scales, shifts, ready, upper=None):
    for moment in ready:
        act.wait_ge(*g.moment(moment))
    for k in range(KD):
        act.activation(g.aT[:, k, 0:T], src[:, k, 0:T], ACT.Square).then_inc(g.s["act_norm"], 1)
        g.count("act_norm", ("square", key, k))
    act.wait_ge(g.s["pe_norm"], g.at("mm", "sumsq", key))
    act.activation(g.rstd[:, 0:T], g.bank(("sumsq", key))[:, 0:T], ACT.Sqrt, bias=g.eps[:, 0:1],
                              scale=1.0 / D).then_inc(g.s["act_norm"], 1)
    g.count("act_norm", ("free", ("sumsq", key)))
    if upper is not None:
        upper_act(g, act, 2)
        if shifts is None:
            for k in range(KD):
                act.wait_ge(g.s["dve_norm"], g.at("normed", key, k))
                act.activation(exact(upper(k)), g.aT[:, k, 0:T], ACT.Copy).then_inc(g.s["act_norm"], 1)
                g.count("act_norm", ("upper x", key, k))
    if shifts is not None:
        for k in range(KD):
            act.wait_ge(g.s["dve_norm"], g.at("normed", key, k))
            for s in range(T // L):
                c = slice(L * s, L * s + L)
                act.activation(g.aT[:, k, c], g.aT[:, k, c], ACT.Identity, bias=shifts(k, s),
                                          scale=scales(k, s)).then_inc(g.s["act_norm"], 1)
                g.count("act_norm", ("aT", key))
            g.also("act_norm", ("shifted x", key, k))


def norm_pe(g, pe, key, T):
    pe.wait_ge(*g.bank_free())
    ps = g.open(("sumsq", key))
    for k in range(KD):
        pe.wait_ge(g.s["act_norm"], g.at("square", key, k))
        last = mm(pe, ps[:, 0:T], g.tab("ones"), g.aT[:, k, 0:T], k == 0, k == KD - 1)
    last.then_inc(g.s["pe_norm"], 1)
    g.count("pe_norm", ("mm", "sumsq", key))


def norm_dve(g, dve, key, src, T, scales, shifts, dst=None, upper=None):
    dve.wait_ge(g.s["act_norm"], g.at("free", ("sumsq", key)))
    dve.reciprocal(g.rstd[:, 0:T], g.rstd[:, 0:T]).then_inc(g.s["dve_norm"], 1)
    g.count("dve_norm")
    dve.wait_ge(g.s["dve_norm"], g.so_far("dve_norm"))
    dst = g.aT if dst is None else dst
    for k in range(KD):
        if shifts is not None:
            dve.tensor_tensor(dst[:, k, 0:T], src[:, k, 0:T], g.rstd[:, 0:T], ALU.mult).then_inc(g.s["dve_norm"], 1)
            g.count("dve_norm", ("normed", key, k))
        else:
            dve.scalar_tensor_tensor(dst[:, k, 0:T], src[:, k, 0:T], scales(k, 0), g.rstd[:, 0:T],
                                                ALU.mult, ALU.mult).then_inc(g.s["dve_norm"], 1)
            g.count("dve_norm", ("normed", key, k))
            g.also("dve_norm", ("aT", key))
    if upper is None:
        return
    lower_dve(g, dve, 1)
    for k in range(KD):
        x = g.aT[:, k, 0:T]
        if shifts is not None:
            dve.wait_ge(g.s["act_norm"], g.at("shifted x", key, k))
            dve.tensor_copy(exact(upper(k)), x).then_inc(g.s["dve_norm"], 1)
            g.count("dve_norm")
            dve.wait_ge(g.s["dve_norm"], g.so_far("dve_norm"))
        else:
            dve.wait_ge(g.s["act_norm"], g.at("upper x", key, k))
        dve.tensor_tensor(exact(x), x, rounded(upper(k)), ALU.subtract).then_inc(g.s["dve_norm"], 1)
        g.count("dve_norm", ("x", key, k))
    lower_dve(g, dve, 1)


def units_of(heads, qts=2):
    return [(h, q) for h in range(heads) for q in range(qts)]


def attn_pe(g, pe, name, a):
    for moment in a["ready"]:
        pe.wait_ge(*g.moment(moment))
    us = units_of(a["heads"])
    n = len(us)
    for i in range(n + 3):
        if i < n:
            h, q = us[i]
            pe.wait_ge(*g.bank_free())
            ps = g.open(("S", name, i))
            for col, pairs in a["scores"](h, q):
                for m, (x, y) in enumerate(pairs):
                    w = y.shape[-1]
                    last = mm(pe, ps[:, col:col + w], x, y, m == 0, m == len(pairs) - 1)
            last.then_inc(g.s["pe_attention"], 1)
            g.count("pe_attention", ("mm", "S", name, i))
        if 2 <= i < n + 2:
            j = i - 2
            pe.wait_ge(g.s["dve_attention"], g.at("P", name, j))
            pe.wait_ge(*g.bank_free())
            ps = g.open(("T", name, j))
            for t in range(a["width"](us[j][1]) // P):
                last = pe.transpose(ps[:, P * t:P * t + P], g.probs[:, j % 3, P * t:P * t + P], g.tab("ident"))
            last.then_inc(g.s["pe_attention"], 1)
            g.count("pe_attention", ("mm", "T", name, j))
        if i >= 3:
            j = i - 3
            h, q = us[j]
            pair = ("O", name, h // 2)
            if h % 2 == 0 and q == 0:
                pe.wait_ge(*g.bank_free("long"))
                g.open(pair, "long")
            ps = g.psum[g.bank_of[pair]]
            pe.wait_ge(g.s["act_attention"], g.at("PT", name, j))
            nt = a["width"](q) // P
            r = slice(HD * (h % 2), HD * (h % 2) + HD)
            for t in range(nt):
                last = mm(pe, ps[r, P * q:P * q + P], a["values"](h, t), g.probsT[:, j % 3, P * t:P * t + P],
                          t == 0, t == nt - 1)
            last.then_inc(g.s["pe_attention"], 1)
            g.count("pe_attention", ("mm", "PV", name, j))


def attn_dve(g, dve, name, a):
    us = units_of(a["heads"])
    n = len(us)
    for i in range(n + 1):
        if i < n:
            h, q = us[i]
            ps = g.bank(("S", name, i))
            dve.wait_ge(g.s["pe_attention"], g.at("mm", "S", name, i))
            for col, extra in a["add"](h, q):
                w = extra.shape[-1]
                dve.tensor_tensor(ps[:, col:col + w], ps[:, col:col + w], extra, ALU.add).then_inc(g.s["dve_attention"], 1)
                g.count("dve_attention")
                dve.wait_ge(g.s["dve_attention"], g.so_far("dve_attention"))
            dve.tensor_reduce(g.nmax[:, i % 4:i % 4 + 1], ps[:, 0:a["width"](q)], AX.X, ALU.max,
                                         negate=True).then_inc(g.s["dve_attention"], 1)
            g.count("dve_attention", ("nmax", name, i))
        if i >= 1:
            j = i - 1
            w = a["width"](us[j][1])
            dve.wait_ge(g.s["act_attention"], g.at("exp", name, j))
            dve.reciprocal(g.rinv[:, j % 4:j % 4 + 1], g.rsum[:, j % 4:j % 4 + 1]).then_inc(g.s["dve_attention"], 1)
            g.count("dve_attention")
            dve.wait_ge(g.s["dve_attention"], g.so_far("dve_attention"))
            dve.tensor_scalar(g.probs[:, j % 3, 0:w], g.probs[:, j % 3, 0:w], g.rinv[:, j % 4:j % 4 + 1],
                                         None, ALU.mult).then_inc(g.s["dve_attention"], 1)
            g.count("dve_attention", ("P", name, j))


def attn_act(g, act, name, a):
    us = units_of(a["heads"])
    n = len(us)
    for i in range(n + 3):
        if i < n:
            w = a["width"](us[i][1])
            act.wait_ge(g.s["dve_attention"], g.at("nmax", name, i))
            if i >= 3:
                act.wait_ge(g.s["pe_attention"], g.at("mm", "T", name, i - 3))
            act.activation(g.probs[:, i % 3, 0:w], g.bank(("S", name, i))[:, 0:w], ACT.Exp,
                                      bias=g.nmax[:, i % 4:i % 4 + 1], accum_out=g.rsum[:, i % 4:i % 4 + 1]).then_inc(g.s["act_attention"], 1)
            g.count("act_attention", ("exp", name, i))
            g.also("act_attention", ("free", ("S", name, i)))
        if 2 <= i < n + 2:
            j = i - 2
            w = a["width"](us[j][1])
            act.wait_ge(g.s["pe_attention"], g.at("mm", "T", name, j))
            if j >= 3:
                act.wait_ge(g.s["pe_attention"], g.at("mm", "PV", name, j - 3))
            act.activation(g.probsT[:, j % 3, 0:w], g.bank(("T", name, j))[:, 0:w], ACT.Copy).then_inc(g.s["act_attention"], 1)
            g.count("act_attention", ("PT", name, j))
            g.also("act_attention", ("free", ("T", name, j)))
        if i >= 3:
            j = i - 3
            h, q = us[j]
            if h % 2 and q == 1:
                act.wait_ge(g.s["pe_attention"], g.at("mm", "PV", name, j))
                act.activation(a["out"](h // 2), g.bank(("O", name, h // 2))[:, 0:L], ACT.Copy).then_inc(g.s["act_attention"], 1)
                g.count("act_attention", ("free", ("O", name, h // 2)))
    g.also("act_attention", ("attended", name))




T_BLOCKS = ("naq", "nak", "rq", "rk", "gate")
IN_ORDER = ("naq", "nak", "nav", "rq", "rk", "rv", "gate")


def proj_T(l, name):
    return T2 if l == 0 or name in ("nak", "rk", "nav", "rv") else L


def proj_pe(g, pe, l):
    g.x = lambda k: (g.n1_upper(k), g.aT[:, k, :])
    slab = g.slabs[g.next_slab]
    products(g, pe, slab, KD, [(("pool", l, t), slice(0, 256), (0, 256), t, ("mm", "pool", l, t))
                               for t in range(proj_T(l, "pool") // P)], "projection", ("x", ("n1", l)))
    for name in IN_ORDER:
        T = proj_T(l, name)
        if name in T_BLOCKS:
            outs = [((name, l, j), slice(0, T), (P * j, P), None, ("mm", name, l, j)) for j in range(3)]
            g.x = lambda k, T=T: (g.n1_upper(k)[:, 0:T], g.aT[:, k, 0:T])
        else:
            outs = [((name, l, t), slice(0, 384), (0, 384), t, ("mm", name, l, t)) for t in range(T // P)]
            g.x = lambda k: (g.n1_upper(k), g.aT[:, k, :])
        products(g, pe, g.slabs[g.next_slab], KD, outs, "projection")
    for name in ("rq", "rk"):
        for j in range(3):
            pe.wait_ge(*g.moment(("raw", name, l, j)))
            pe.wait_ge(*g.bank_free())
            ps = g.open(("swap", name, l, j))
            mm(pe, ps[:, 0:L], g.tab("rot_swap"), g.m1[name][:, j, 0:L]).then_inc(g.s["pe_projection"], 1)
            g.count("pe_projection", ("mm", "swap", name, l, j))


def proj_act(g, act, l):
    upper_act(g, act, 1)
    for t in range(proj_T(l, "pool") // P):
        act.wait_ge(g.s["pe_projection"], g.at("mm", "pool", l, t))
        act.activation(g.m1["pool"][:, t, :], g.bank(("pool", l, t))[:, 0:256], ACT.Copy).then_inc(g.s["act_projection"], 1)
        g.count("act_projection", ("free", ("pool", l, t)))
    g.also("act_projection", ("have", "pool", l))
    for name in IN_ORDER:
        upper_act(g, act, 1 if name == "gate" else 2)
        if name in ("nak", "rk"):
            continue
        T = proj_T(l, name)
        for j in range(3 if name in T_BLOCKS else T // P):
            act.wait_ge(g.s["pe_projection"], g.at("mm", name, l, j))
            n = T if name in T_BLOCKS else 384
            f, scale = (ACT.Silu, 1.0) if name == "gate" else (ACT.Copy, HD ** -0.5 if name == "naq" else 1.0)
            act.activation(g.m1[name][:, j, 0:n], g.bank((name, l, j))[:, 0:n], f, scale=scale).then_inc(g.s["act_projection"], 1)
            g.count("act_projection", ("free", (name, l, j)))
            g.also("act_projection", ("raw", name, l, j))
        g.also("act_projection", ("have", name, l))


def proj_dve(g, dve, l):
    dve.wait_ge(g.const_in["tab_a"], 16)
    lower_dve(g, dve, 1)
    for name in IN_ORDER:
        lower_dve(g, dve, 1 if name == "gate" else 2)
        if name not in ("nak", "rk"):
            continue
        for j in range(3):
            dve.wait_ge(g.s["pe_projection"], g.at("mm", name, l, j))
            s = HD ** -0.5 if name == "rk" else 1.0
            dve.tensor_scalar(g.m1[name][:, j, :], g.bank((name, l, j))[:, :], s, None, ALU.mult).then_inc(g.s["dve_projection"], 1)
            g.count("dve_projection", ("free", (name, l, j)))
            g.also("dve_projection", ("raw", name, l, j))
        g.also("dve_projection", ("have", name, l))
    for name in ("rq", "rk"):
        for j in range(3):
            x = g.m1[name][:, j, 0:L]
            dve.wait_ge(g.s["pe_projection"], g.at("mm", "swap", name, l, j))
            dve.tensor_tensor(g.tmp[:, 0:L], g.bank(("swap", name, l, j))[:, 0:L], g.tab("rot_sin"), ALU.mult).then_inc(g.s["dve_projection"], 1)
            g.count("dve_projection", ("free", ("swap", name, l, j)))
            dve.tensor_tensor(x, x, g.tab("rot_cos"), ALU.mult).then_inc(g.s["dve_projection"], 1)
            g.count("dve_projection")
            dve.wait_ge(g.s["dve_projection"], g.so_far("dve_projection"))
            dve.tensor_tensor(x, x, g.tmp[:, 0:L], ALU.add).then_inc(g.s["dve_projection"], 1)
            g.count("dve_projection", ("rotated", name, l, j))
            dve.wait_ge(g.s["dve_projection"], g.so_far("dve_projection"))


def pool_pe(g, pe, l):
    pe.wait_ge(g.const_in["tab_a"], 16)
    pe.wait_ge(g.const_in["pool_w"], 16)
    pe.wait_ge(g.s["act_projection"], g.at("have", "pool", l))
    segs = proj_T(l, "pool") // L
    band = g.tab("pool").rearrange("p (s g t) -> p s g t", s=2, g=4)
    for s in range(segs):
        pe.wait_ge(*g.bank_free())
        ps = g.open(("band", l, s))
        for q in range(4):
            r = slice(HD * (q % 2), HD * (q % 2) + HD)
            for t in range(2):
                last = mm(pe, ps[r, L * (q // 2):L * (q // 2) + L], g.m1["pool"][:, 2 * s + t, HD * q:HD * q + HD],
                          band[:, t, q, :], t == 0, t == 1)
        last.then_inc(g.s["pe_pooling"], 1)
        g.count("pe_pooling", ("mm", "band", l, s))
    for s in range(segs):
        pe.wait_ge(g.s["act_pooling"], g.at("banded", l, s))
        for odd in range(2):
            pe.wait_ge(*g.bank_free())
            ps = g.open(("pooled", l, s, odd))
            r = slice(HD * odd, HD * odd + HD)
            for q in (odd, 2 + odd):
                c = slice(L * (q // 2), L * (q // 2) + L)
                last = mm(pe, ps[r, c], g.pool_w[r, l, q, :], g.banded[r, s, c])
            last.then_inc(g.s["pe_pooling"], 1)
            g.count("pe_pooling", ("mm", "pooled", l, s, odd))


def pool_act(g, act, l):
    segs = proj_T(l, "pool") // L
    for s in range(segs):
        act.wait_ge(g.s["pe_pooling"], g.at("mm", "band", l, s))
        act.activation(g.banded[:, s, :], g.bank(("band", l, s))[:, :], ACT.Copy).then_inc(g.s["act_pooling"], 1)
        g.count("act_pooling", ("banded", l, s))
        g.also("act_pooling", ("free", ("band", l, s)))
    for s in range(segs):
        for odd in range(2):
            act.wait_ge(g.s["pe_pooling"], g.at("mm", "pooled", l, s, odd))
            r = slice(HD * odd, HD * odd + HD)
            for j in range(2):
                act.activation(g.aT[r, j, L * s:L * s + L], g.bank(("pooled", l, s, odd))[r, L * j:L * j + L],
                                          ACT.Copy, scale=g.v("pool_scale", 2 * l + j)[r, :]).then_inc(g.s["act_pooling"], 1)
                g.count("act_pooling", ("free", ("pooled", l, s, odd)))
    g.also("act_pooling", ("y pool", l))


def na_of(g, l):
    m = g.m1

    def half(h):
        return slice(HD * (h % 2), HD * (h % 2) + HD)

    def scores(h, q):
        x = m["naq"][half(h), h // 2, P * q:P * q + P]
        k = m["nak"]
        return [(0, [(x, k[half(h), h // 2, 0:L])]), (L, [(x, k[half(h), h // 2, L:T2])])]

    return dict(heads=NAH, scores=scores, width=lambda q: T2, out=lambda p: g.aT[:, 2 + p, 0:L],
                     add=lambda h, q: [(0, g.bias[:, 2 * h + q, :])], ready=[("have", "naq", l), ("have", "nak", l),
                     ("have", "nav", l)], values=lambda h, t: m["nav"][:, t, HD * h:HD * h + HD])


def ctx_attn_of(g, l):
    m = g.m1

    def half(h):
        return slice(HD * (h % 2), HD * (h % 2) + HD)

    def scores(h, q):
        return [(0, [(m["naq"][half(h), h // 2, L + P * q:L + P * q + P], m["nak"][half(h), h // 2, L:T2])])]

    return dict(heads=NAH, scores=scores, width=lambda q: L, out=lambda p: g.aT[:, 2 + p, L:T2],
                     add=lambda h, q: [], ready=[("have", "naq", l)],
                     values=lambda h, t: m["nav"][:, 2 + t, HD * h:HD * h + HD])


def bias_act(g, act, l):
    if l:
        act.wait_ge(g.s["dve_retention"], g.at("y ret", l - 1))
    act.dma_start(g.bias_flat, g.io["rpb"][l]).then_inc(g.bias_in, 16)
    g.biases += 1


def bias_dve(g, dve, l):
    dve.wait_ge(g.bias_in, 16 * (l + 1))
    m = g.tab("na_mask").unsqueeze(1).broadcast_to((P, 2 * NAH, L))
    dve.tensor_tensor(g.bias[:, :, :], g.bias[:, :, :], m, ALU.add).then_inc(g.s["dve_attention"], 1)
    g.count("dve_attention")
    dve.wait_ge(g.s["dve_attention"], g.so_far("dve_attention"))


def shifted(g, table):
    v = table.rearrange("p (a b) -> p a b", a=3)[:, 0:2, :]
    ap = [list(x) for x in v.ap]
    assert ap[-2] == [P, 2] or tuple(ap[-2]) == (P, 2), ap
    ap[-1] = [1, L]
    return bass.AP(v.tensor, v.offset, ap)


def ret_act(g, act, l):
    for h in range(RETH):
        e = g.ret_e
        for n, (table, lg) in enumerate((("d_fwd", "ret_decay_fwd"), ("d_bwd", "ret_decay_bwd"),
                                         ("d_cf", "ret_decay_fwd"), ("d_cb", "ret_decay_bwd"))):
            if h and n % 2 == 0:
                act.wait_ge(g.s["pool_retention"], g.at("decays" if n else "inner decays", l, h - 1))
            act.activation(e[:, n, :], g.tab(table), ACT.Exp, scale=g.v(lg, RETH * l + h)).then_inc(g.s["act_retention"], 1)
            g.count("act_retention", ("powers", l, h))
        if h >= 2 and h % 2 == 0:
            ret_out(g, act, l, h // 2 - 1)
    ret_out(g, act, l, RETH // 2 - 1)
    T = T2 if l == 0 else L
    for j in range(3):
        act.wait_ge(g.s["dve_retention"], g.at("centred", l, j))
        act.activation(g.m1["nak"][:, j, 0:T], g.m1["naq"][:, j, 0:T], ACT.Square).then_inc(g.s["act_retention"], 1)
        g.count("act_retention", ("gn sq", l, j))
    for j in range(3):
        act.wait_ge(g.s["pe_retention"], g.at("mm", "gn var", l, j))
        act.activation(g.m1["nak"][:, j, 0:T], g.bank(("gn var", l, j))[:, 0:T], ACT.Sqrt,
                                  bias=g.eps[:, 0:1], scale=1.0 / HD).then_inc(g.s["act_retention"], 1)
        g.count("act_retention", ("free", ("gn var", l, j)))


def ret_out(g, act, l, j):
    T = T2 if l == 0 else L
    act.wait_ge(g.s["pe_retention"], g.at("mm", "ro", l, j))
    act.activation(g.m1["naq"][:, j, 0:T], g.bank(("ro", l, j))[:, 0:T], ACT.Copy).then_inc(g.s["act_retention"], 1)
    g.count("act_retention", ("free", ("ro", l, j)))


def ret_pool(g, pool, l):
    pool.wait_ge(g.const_in["tab_a"], 16)
    for h in range(RETH):
        e, f = g.ret_e, g.ret_f[:, h % 2]
        pool.wait_ge(g.s["act_retention"], g.at("powers", l, h))
        pool.tensor_tensor(e[:, 0, :], e[:, 0, :], g.tab("m_fwd"), ALU.mult).then_inc(g.s["pool_retention"], 1)
        g.count("pool_retention")
        pool.tensor_tensor(e[:, 1, :], e[:, 1, :], g.tab("m_bwd"), ALU.mult).then_inc(g.s["pool_retention"], 1)
        g.count("pool_retention")
        pool.wait_ge(g.s["pool_retention"], g.so_far("pool_retention"))
        if h >= 2:
            pool.wait_ge(g.s["dve_retention"], g.at("decayed", l, h - 2))
        elif l:
            pool.wait_ge(g.s["dve_retention"], g.at("decayed", l - 1, RETH - 2 + h))
        pool.tensor_tensor(f[:, 0, :], e[:, 0, :], e[:, 1, :], ALU.add).then_inc(g.s["pool_retention"], 1)
        g.count("pool_retention", ("inner decays", l, h))
        pool.tensor_tensor(f[:, 1, :], e[:, 2, :], e[:, 3, :], ALU.add).then_inc(g.s["pool_retention"], 1)
        g.count("pool_retention", ("decays", l, h))


def ret_parts(l):
    return [(0, 0, 0), (0, L, 1)] + ([(L, L, 0)] if l == 0 else [])


def ret_pe(g, pe, l):
    pe.wait_ge(g.s["dve_projection"], g.at("rotated", "rk", l, 2))
    pe.wait_ge(g.s["act_projection"], g.at("have", "rv", l))
    pe.wait_ge(g.s["act_projection"], g.at("have", "gate", l))
    parts = ret_parts(l)
    n = RETH * len(parts)
    m = g.m1

    def scores(i):
        h, (q0, k0, _) = i // len(parts), parts[i % len(parts)]
        r = slice(HD * (h % 2), HD * (h % 2) + HD)
        pe.wait_ge(*g.bank_free())
        ps = g.open(("rs", l, i))
        for s in range(2):
            kt = k0 + P * (1 - s)
            last = mm(pe, ps[:, L * s:L * s + L], m["rk"][r, h // 2, kt:kt + P], m["rq"][r, h // 2, q0:q0 + L])
        last.then_inc(g.s["pe_retention"], 1)
        g.count("pe_retention", ("mm", "rs", l, i))

    def outputs(i):
        h, p = i // len(parts), i % len(parts)
        q0, k0, _ = parts[p]
        r = slice(HD * (h % 2), HD * (h % 2) + HD)
        if h % 2 == 0 and p == 0:
            pe.wait_ge(*g.bank_free("long"))
            g.open(("ro", l, h // 2), "long")
        ps = g.psum[g.bank_of[("ro", l, h // 2)]]
        pe.wait_ge(g.s["dve_retention"], g.at("weighted", l, i))
        for s in range(2):
            first = s == 0 and (q0, k0) != (0, L)
            stop = s == 1 and (q0, k0) != (0, 0)
            last = mm(pe, ps[r, q0:q0 + L], m["rv"][:, k0 // P + 1 - s, HD * h:HD * h + HD],
                      g.ret_a[:, i % 3, L * s:L * s + L], first, stop)
        last.then_inc(g.s["pe_retention"], 1)
        g.count("pe_retention", ("mm", "ro unit", l, i))
        if h % 2 and p == len(parts) - 1:
            g.also("pe_retention", ("mm", "ro", l, h // 2))

    for i in range(n + 2):
        if i < n:
            scores(i)
        if i >= 2:
            outputs(i - 2)
    T = T2 if l == 0 else L
    for what, src in (("gn mean", "naq"), ("gn var", "nak")):
        for j in range(3):
            pe.wait_ge(g.s["act_retention"], g.at(("free", ("ro", l, j)) if what == "gn mean" else ("gn sq", l, j)))
            pe.wait_ge(*g.bank_free())
            ps = g.open((what, l, j))
            mm(pe, ps[:, 0:T], g.tab("headones"), m[src][:, j, 0:T]).then_inc(g.s["pe_retention"], 1)
            g.count("pe_retention", ("mm", what, l, j))


def ret_dve(g, dve, l):
    parts = ret_parts(l)
    for i in range(RETH * len(parts)):
        h, (_, _, table) = i // len(parts), parts[i % len(parts)]
        dve.wait_ge(g.s["pe_retention"], g.at("mm", "rs", l, i))
        dve.wait_ge(g.s["pool_retention"], g.at("decays", l, h))
        if i >= 3:
            dve.wait_ge(g.s["pe_retention"], g.at("mm", "ro unit", l, i - 3))
        dve.tensor_tensor(g.ret_a[:, i % 3, :].rearrange("p (s t) -> p s t", s=2),
                                     g.bank(("rs", l, i))[:, :].rearrange("p (s t) -> p s t", s=2),
                                     shifted(g, g.ret_f[:, h % 2, table, :]), ALU.mult).then_inc(g.s["dve_retention"], 1)
        g.count("dve_retention", ("weighted", l, i))
        g.also("dve_retention", ("free", ("rs", l, i)))
        g.also("dve_retention", ("decayed", l, h))
    T = T2 if l == 0 else L
    y, r = g.m1["naq"], g.m1["nak"]
    for j in range(3):
        dve.wait_ge(g.s["pe_retention"], g.at("mm", "gn mean", l, j))
        dve.scalar_tensor_tensor(y[:, j, 0:T], g.bank(("gn mean", l, j))[:, 0:T], -1.0 / HD, y[:, j, 0:T],
                                            ALU.mult, ALU.add).then_inc(g.s["dve_retention"], 1)
        g.count("dve_retention", ("centred", l, j))
        g.also("dve_retention", ("free", ("gn mean", l, j)))
    for j in range(3):
        dve.wait_ge(g.s["act_retention"], g.at("free", ("gn var", l, j)))
        dve.reciprocal(r[:, j, 0:T], r[:, j, 0:T]).then_inc(g.s["dve_retention"], 1)
        g.count("dve_retention")
        dve.wait_ge(g.s["dve_retention"], g.so_far("dve_retention"))
        dve.tensor_tensor(y[:, j, 0:T], y[:, j, 0:T], r[:, j, 0:T], ALU.mult).then_inc(g.s["dve_retention"], 1)
        g.count("dve_retention")
        dve.wait_ge(g.s["dve_retention"], g.so_far("dve_retention"))
        dve.scalar_tensor_tensor(g.aT[:, 5 + j, 0:T], y[:, j, 0:T], g.v("ret_gn_g", 3 * l + j),
                                            g.m1["gate"][:, j, 0:T], ALU.mult, ALU.mult).then_inc(g.s["dve_retention"], 1)
        g.count("dve_retention", ("y ret", l))
        dve.wait_ge(g.s["dve_retention"], g.so_far("dve_retention"))


def out_pe(g, pe, key, T, ready):
    for moment in ready:
        pe.wait_ge(*g.moment(moment))
    for i in range(2):
        n, w = g.next_weights()
        pe.wait_ge(g.slab_in[n % RING], 16 * (n // RING + 1))
        for j in range(4):
            pe.wait_ge(*g.bank_free())
            ps = g.open(("wo", key, 4 * i + j))
            for k in range(KD):
                a = 512 * k + P * j
                last = mm(pe, ps[:, 0:T], w[:, a:a + P], g.aT[:, k, 0:T], k == 0, k == KD - 1)
            last.then_inc(g.s["pe_residual"], 1)
            g.count("pe_residual", ("mm", "wo", key, 4 * i + j))
        g.also("pe_residual", ("used", n))


def add_dve(g, dve, what, key, T, gate, split=False):
    for m in range(KD):
        if split and m < KD - 1:
            lower_dve(g, dve, 1)
        dve.wait_ge(*g.moment(("mm", what, key, m)))
        ps = g.bank((what, key, m))
        if gate is None:
            dve.tensor_tensor(g.hT[:, m, 0:T], ps[:, 0:T], g.hT[:, m, 0:T], ALU.add).then_inc(g.s["dve_residual"], 1)
            g.count("dve_residual", ("free", (what, key, m)))
        else:
            for s in range(T // L):
                c = slice(L * s, L * s + L)
                dve.scalar_tensor_tensor(g.hT[:, m, c], ps[:, c], gate(m, s), g.hT[:, m, c],
                                                    ALU.mult, ALU.add).then_inc(g.s["dve_residual"], 1)
                g.count("dve_residual", ("free", (what, key, m)))
        if split and m < KD - 1:
            lower_dve(g, dve, 1)
    g.also("dve_residual", ("h", what, key))


def ffn1_pe(g, pe, l, T):
    g.x = lambda k: (g.n2_upper(l, k), g.aT[:, k, 0:T])
    for i in range(KF // 2):
        outs = [(("up", l, 2 * i + j, ab), slice(0, T), (256 * ab + P * j, P), None, ("mm", "up", l, 2 * i + j, ab))
                for j in range(2) for ab in range(2)]
        products(g, pe, g.slabs[g.next_slab], KD, outs, "feedforward", ("x", ("n2", l)) if i == 0 else None)
    if l == 1:
        g.x = lambda k: (g.hid[:, k, L:T2], g.hid[:, k, 0:L])
        for m in range(KD):
            products(g, pe, g.slabs[g.next_slab], KF, [(("dn", l, m), slice(0, T), (0, P), None, ("mm", "dn", l, m))],
                     "feedforward", ("hidden", l) if m == 0 else None)
        return
    for m in range(KD):
        n, w = g.next_weights()
        pe.wait_ge(g.slab_in[n % RING], 16 * (n // RING + 1))
        pe.wait_ge(*g.bank_free())
        ps = g.open(("dn", l, m))
        for k in range(KF):
            if m == 0:
                pe.wait_ge(g.s["dve_feedforward"], g.at("hidden", l, k))
            last = mm(pe, ps[:, 0:T], w[:, P * k:P * k + P], g.hid[:, k, 0:T], k == 0, k == KF - 1)
        last.then_inc(g.s["pe_feedforward"], 1)
        g.count("pe_feedforward", ("mm", "dn", l, m))
        g.also("pe_feedforward", ("used", n))


def ffn1_act(g, act, l, T):
    last = KF // 2 - 1

    def upper_hidden(t):
        act.wait_ge(g.s["dve_feedforward"], g.at("hidden f32", l, t))
        act.activation(exact(g.hid[:, t, L:T2]), g.hid[:, t, 0:L], ACT.Copy).then_inc(g.s["act_feedforward"], 1)
        g.count("act_feedforward", ("upper hidden", l, t))

    for t in range(KF + 1):
        if t < KF and t % 2 == 0 and (l == 1 or t // 2 < last):
            upper_act(g, act, 1)
        if t < KF:
            for ab in range(2):
                act.wait_ge(g.s["pe_feedforward"], g.at("mm", "up", l, t, ab))
                if t >= 2:
                    act.wait_ge(g.s["dve_feedforward"], g.at("hidden f32", l, t - 2))
                c = t + KF * ab
                act.activation(g.conv[:, t % 2, ab, 0:T], g.bank(("up", l, t, ab))[:, 0:T], ACT.Identity,
                                          bias=g.v("conv_b", 2 * KF * l + c),
                                          scale=g.v("conv_w", 2 * KF * (3 * l + 1) + c)).then_inc(g.s["act_feedforward"], 1)
                g.count("act_feedforward", ("middle", l, t, ab))
        if t >= 1:
            act.wait_ge(g.s["dve_feedforward"], g.at("conv", l, t - 1, 0))
            act.activation(g.conv[:, (t - 1) % 2, 0, 0:T], g.conv[:, (t - 1) % 2, 0, 0:T], ACT.Silu).then_inc(g.s["act_feedforward"], 1)
            g.count("act_feedforward", ("silu", l, t - 1))
        if l == 1 and t >= 2:
            upper_hidden(t - 2)
        if t < KF and t % 2 == 1 and (l == 1 or t // 2 < last):
            upper_act(g, act, 1)
    if l == 1:
        upper_hidden(KF - 1)
        upper_act(g, act, 2 * KD - 2)


def ffn1_dve(g, dve, l, T):
    last = KF // 2 - 1

    def lower_hidden(t):
        dve.wait_ge(g.s["act_feedforward"], g.at("upper hidden", l, t))
        x = g.hid[:, t, 0:L]
        dve.tensor_tensor(exact(x), x, rounded(g.hid[:, t, L:T2]), ALU.subtract).then_inc(g.s["dve_feedforward"], 1)
        g.count("dve_feedforward", ("hidden", l, t))

    for t in range(KF + 1):
        if t < KF and t % 2 == 0 and (l == 1 or t // 2 < last):
            lower_dve(g, dve, 1)
        if t < KF:
            for ab in range(2):
                c = t + KF * ab
                ps = g.bank(("up", l, t, ab))[:, 0:T].rearrange("p (s t) -> p s t", t=L)
                u = g.conv[:, t % 2, ab, 0:T].rearrange("p (s t) -> p s t", t=L)
                dve.wait_ge(g.s["act_feedforward"], g.at("middle", l, t, ab))
                dve.scalar_tensor_tensor(u[:, :, 1:L], ps[:, :, 0:L - 1], g.v("conv_w", 2 * KF * 3 * l + c),
                                                    u[:, :, 1:L], ALU.mult, ALU.add).then_inc(g.s["dve_feedforward"], 1)
                g.count("dve_feedforward")
                dve.wait_ge(g.s["dve_feedforward"], g.so_far("dve_feedforward"))
                dve.scalar_tensor_tensor(u[:, :, 0:L - 1], ps[:, :, 1:L],
                                                    g.v("conv_w", 2 * KF * (3 * l + 2) + c), u[:, :, 0:L - 1],
                                                    ALU.mult, ALU.add).then_inc(g.s["dve_feedforward"], 1)
                g.count("dve_feedforward", ("conv", l, t, ab))
                g.also("dve_feedforward", ("free", ("up", l, t, ab)))
        if t >= 1:
            dve.wait_ge(g.s["act_feedforward"], g.at("silu", l, t - 1))
            dve.wait_ge(g.s["dve_feedforward"], g.so_far("dve_feedforward"))
            b = (t - 1) % 2
            dve.tensor_tensor(g.hid[:, t - 1, 0:T], g.conv[:, b, 0, 0:T], g.conv[:, b, 1, 0:T], ALU.mult).then_inc(g.s["dve_feedforward"], 1)
            g.count("dve_feedforward", ("hidden f32", l, t - 1))
            if l == 0:
                g.also("dve_feedforward", ("hidden", l, t - 1))
        if l == 1 and t >= 2:
            lower_hidden(t - 2)
        if t < KF and t % 2 == 1 and (l == 1 or t // 2 < last):
            lower_dve(g, dve, 1)
    if l == 1:
        lower_hidden(KF - 1)


SHIFTED = 14
LN_DECAY = -float(np.exp(-0.5))


def second_places(g):
    b, t = g.big, g.tmp
    g.prj = b[:, 0:SHIFTED * 257].rearrange("p (a b) -> p a b", a=SHIFTED)
    g.lat = g.part(b, 3600, 4, L)
    g.tok = g.part(b, 4624, 4, 512)
    g.lnw, g.cum = g.part(b, 4624, 4, L), g.part(b, 5648, 4, L)
    g.rw_a, g.rw_kk = g.part(b, 6672, 4, L), g.part(b, 7696, 4, L)
    g.nv, g.z, g.wt, g.u = b[:, 6672:7184], b[:, 7184:7696], g.part(b, 7696, 4, P), b[:, 8208:8720]
    g.rw_g = g.part(b, 8720, 4, L)
    g.bt, g.kt = g.part(b, 9744, 4, L), g.part(b, 10768, 4, L)
    g.ar = b[:, 11792:13840].rearrange("p (j t w c) -> p j t w c", j=4, t=2, w=2)
    g.y = g.part(b, 13840, 4, L)
    g.lend = g.cend
    g.mp = g.aT[:, :, :].rearrange("p h (w c) -> p h w c", w=4)
    g.dm, g.fm = g.part(t, 0, 8, P), g.part(t, 1024, 8, P)
    g.states = g.part(t, 2048, 5, L)
    g.w4 = g.part(t, 3328, 4, L)
    g.w4b = g.part(t, 0, 4, L)
    g.w4c = g.part(t, 1024, 4, L)
    g.d14 = g.part(t, 0, SHIFTED, L)
    g.mq, g.mk, g.mv = g.part(b, 9744, 8, L), g.part(b, 11792, 8, L), g.part(b, 13840, 2, 512)
    g.hid2, g.hid2_upper = g.part(b, 0, KF, L), g.part(b, KF * L, KF, L)
    g.gate2 = g.part(t, 0, 4, L)
    g.q2 = {n: g.part(b, 1024 * i, 4, L) for i, n in enumerate(("fq", "fk", "mq", "mk"))}
    g.q2.update({n: g.part(b, 4096 + 1024 * i, 2, 512) for i, n in enumerate(("fv", "mv"))})
    g.negd, g.lsig = b[:, 6144:6400], b[:, 6400:6656]
    g.oneb = b[:, 6656:6912]
    g.t_tok, g.hb, g.hT2 = g.part(b, 0, 2, D), b[:, 2048:3840], g.part(b, 3840, 2, KE, P)
    g.xg, g.sg, g.yb = g.part(b, 11008, 2, KD, P), g.part(b, 13056, 2, FC), b[:, 13952:14976]
    g.perm, g.pw, g.pwt = g.part(t, 0, 2, P), g.part(t, 256, 2, P), t[:, 512:768]
    g.rt_flat, g.cur = t[:, 768:804], t[:, 804:808]
    g.rt = g.rt_flat.rearrange("p (e c) -> p e c", c=4)
    g.lg, g.chosen = g.part(t, 808, 2, 80), g.part(t, 968, 2, 8)
    w = KD * FC
    g.upper = (t[:, 1024:1024 + w], g.aT[:, :, :].rearrange("p a b -> p (a b)")[:, 0:w], g.tabs[:, 2048:2048 + w])
    g.outs = g.part(b, 0, 2, D)


def even_proj_pe(g, pe):
    g.x = lambda k: (g.half_upper(k), g.aT[:, k, 0:L])
    for i in range(4):
        outs = [(("e", 4 * i + j), slice(0, L), (P * j, P), None, ("mm", "e", 4 * i + j)) for j in range(4)]
        products(g, pe, g.slabs[g.next_slab], KD, outs, "projection", ("x", "mix0") if i == 0 else None)
    n, w = g.next_weights()
    pe.wait_ge(g.slab_in[n % RING], 16 * (n // RING + 1))
    for t, m in ((16, P), (17, 32)):
        pe.wait_ge(*g.bank_free())
        ps = g.open(("e", t))
        out = ps[0:P, 0:L] if m == P else ps[64:96, 0:L]
        for k in range(KD):
            a = 160 * k + P * (t - 16)
            mm(pe, out, w[:, a:a + m], rounded(g.half_upper(k)), k == 0, False)
            last = mm(pe, out, w[:, a:a + m], rounded(g.aT[:, k, 0:L]), False, k == KD - 1)
        last.then_inc(g.s["pe_projection"], 1)
        g.count("pe_projection", ("mm", "e", t))
    g.also("pe_projection", ("used", n))


def even_proj_act(g, act):
    for t in range(18):
        if t % 4 == 0 and t < 12:
            upper_act(g, act, 1)
        act.wait_ge(g.s["pe_projection"], g.at("mm", "e", t))
        r = slice(0, P) if t < 17 else slice(64, 96)
        dst = g.prj[:, t, 1:257] if t < SHIFTED else g.lat[r, t - SHIFTED, :]
        act.activation(dst, g.bank(("e", t))[r, 0:L], ACT.Copy).then_inc(g.s["act_projection"], 1)
        g.count("act_projection", ("free", ("e", t)))
        if t % 4 == 3 and t < 12:
            upper_act(g, act, 1)
    g.also("act_projection", ("projected", 0))


def delta_in_dve(g, dve):
    lower_dve(g, dve, 6)
    dve.wait_ge(g.s["dve_norm"], g.at("aT", "mix0"))
    dve.memset(g.prj[:, :, 0:1], 0.0).then_inc(g.s["dve_delta"], 1)
    g.count("dve_delta")
    dve.wait_ge(g.s["dve_delta"], g.so_far("dve_delta"))
    dve.wait_ge(g.s["act_projection"], g.at("projected", 0))
    dve.tensor_tensor(g.d14[:, :, :], g.prj[:, :, 0:L], g.prj[:, :, 1:257], ALU.subtract).then_inc(g.s["dve_delta"], 1)
    g.count("dve_delta")
    dve.wait_ge(g.s["dve_delta"], g.so_far("dve_delta"))
    for t in [12, 13] + list(range(12)):
        dve.scalar_tensor_tensor(g.prj[:, t, 1:257], g.d14[:, t, :], g.v("shift_mu_0_2", t),
                                            g.prj[:, t, 1:257], ALU.mult, ALU.add).then_inc(g.s["dve_delta"], 1)
        g.count("dve_delta", ("shifted", t))
    r, k = g.prj[:, 0:4, 1:257], g.prj[:, 4:8, 1:257]
    dve.wait_ge(g.s["dve_delta"], g.so_far("dve_delta"))
    for j in range(4):
        dve.tensor_scalar(g.rw_kk[:, j, :], k[:, j, :], g.v("rw_kk_0_2", j), None, ALU.mult).then_inc(g.s["dve_delta"], 1)
        g.count("dve_delta", ("kk", j))
    dve.wait_ge(g.s["act_delta"], g.at("kk norm", 1))
    dve.tensor_scalar(g.w4b[:, :, :], g.w4b[:, :, :], 1e-12, None, ALU.max).then_inc(g.s["dve_delta"], 1)
    g.count("dve_delta")
    dve.wait_ge(g.s["dve_delta"], g.so_far("dve_delta"))
    dve.reciprocal(g.w4b[:, :, :], g.w4b[:, :, :]).then_inc(g.s["dve_delta"], 1)
    g.count("dve_delta")
    dve.wait_ge(g.s["dve_delta"], g.so_far("dve_delta"))
    dve.tensor_tensor(g.rw_kk[:, :, :], g.rw_kk[:, :, :], g.w4b[:, :, :], ALU.mult).then_inc(g.s["dve_delta"], 1)
    g.count("dve_delta")
    dve.wait_ge(g.s["act_delta"], g.at("sig w", 3))
    dve.wait_ge(g.s["act_delta"], g.at("rw a", 3))
    dve.tensor_scalar(g.lnw[:, :, :], g.lnw[:, :, :], LN_DECAY, None, ALU.mult).then_inc(g.s["dve_delta"], 1)
    g.count("dve_delta")
    dve.wait_ge(g.s["dve_delta"], g.so_far("dve_delta"))
    dve.tensor_tensor_scan(g.cum.rearrange("p a b -> p (a b)"), g.tab("keep"),
                                      g.lnw.rearrange("p a b -> p (a b)"), 0.0, ALU.mult, ALU.add).then_inc(g.s["dve_delta"], 1)
    g.count("dve_delta", "cum")
    dve.wait_ge(g.s["dve_delta"], g.so_far("dve_delta"))
    dve.tensor_tensor(g.lnw[:, :, :], g.cum[:, :, :], g.lnw[:, :, :], ALU.subtract).then_inc(g.s["dve_delta"], 1)
    g.count("dve_delta", "cum before")
    for j in range(4):
        dve.tensor_scalar(g.w4[:, j, :], g.rw_a[:, j, :], 1.0, g.v("rw_ka_0_2", j), ALU.subtract, ALU.mult).then_inc(g.s["dve_delta"], 1)
        g.count("dve_delta")
    dve.wait_ge(g.s["dve_delta"], g.so_far("dve_delta"))
    dve.scalar_tensor_tensor(k, g.w4[:, :, :], 1.0, k, ALU.add, ALU.mult).then_inc(g.s["dve_delta"], 1)
    g.count("dve_delta")
    dve.wait_ge(g.s["dve_delta"], g.so_far("dve_delta"))
    split = lambda x: x.rearrange("p j (t c) -> p j t c", t=2)
    dve.wait_ge(g.s["act_delta"], g.at("exp before"))
    dve.scalar_tensor_tensor(g.w4[:, :, :], g.rw_kk[:, :, :], -1.0, g.w4b[:, :, :], ALU.mult, ALU.mult).then_inc(g.s["dve_delta"], 1)
    g.count("dve_delta")
    dve.wait_ge(g.s["dve_delta"], g.so_far("dve_delta"))
    dve.tensor_copy(g.ar[:, :, :, 0, :], split(g.w4[:, :, :])).then_inc(g.s["dve_delta"], 1)
    g.count("dve_delta", "A~")
    dve.wait_ge(g.s["act_delta"], g.at("exp minus"))
    dve.tensor_tensor(g.bt[:, :, :], g.rw_kk[:, :, :], g.rw_a[:, :, :], ALU.mult).then_inc(g.s["dve_delta"], 1)
    g.count("dve_delta")
    dve.wait_ge(g.s["dve_delta"], g.so_far("dve_delta"))
    dve.tensor_tensor(g.bt[:, :, :], g.bt[:, :, :], g.w4c[:, :, :], ALU.mult).then_inc(g.s["dve_delta"], 1)
    g.count("dve_delta", "B~")
    dve.tensor_tensor(g.kt[:, :, :], k, g.w4c[:, :, :], ALU.mult).then_inc(g.s["dve_delta"], 1)
    g.count("dve_delta", "K~")
    dve.wait_ge(g.s["act_delta"], g.at("exp cum"))
    dve.tensor_tensor(g.w4[:, :, :], r, g.cum[:, :, :], ALU.mult).then_inc(g.s["dve_delta"], 1)
    g.count("dve_delta")
    dve.wait_ge(g.s["dve_delta"], g.so_far("dve_delta"))
    dve.tensor_copy(g.ar[:, :, :, 1, :], split(g.w4[:, :, :])).then_inc(g.s["dve_delta"], 1)
    g.count("dve_delta", "R~")
    ends = g.cum.rearrange("p j (n c) -> p j n c", c=CH)[:, :, :, CH - 1]
    dve.tensor_copy(g.lend[:, :, :], ends).then_inc(g.s["dve_delta"], 1)
    g.count("dve_delta", "chunk ends")
    dve.memset(g.states[:, 0, :], 0.0).then_inc(g.s["dve_delta"], 1)
    g.count("dve_delta", ("state", 0))


def delta_in_act(g, act):
    act.wait_ge(g.s["dve_delta"], g.at("shifted", 12))
    act.wait_ge(g.s["dve_delta"], g.at("shifted", 13))
    x = g.prj[:, 12:14, 1:257]
    act.activation(x[0:64, 0, :], x[0:64, 0, :], ACT.Tanh).then_inc(g.s["act_delta"], 1)
    g.count("act_delta", "tanh w")
    act.activation(x[:, 1, :], x[:, 1, :], ACT.Sigmoid).then_inc(g.s["act_delta"], 1)
    g.count("act_delta", "sig g")
    for j in range(4):
        for i, (dst, bias, mark) in enumerate(((g.lnw, "rw_w0_0_2", "sig w"), (g.rw_a, "rw_a0_0_2", "rw a"))):
            act.wait_ge(g.s["pe_delta"], g.at("mm", "lora", j, i))
            act.activation(dst[:, j, :], g.bank(("lora", j, i))[:, 0:L], ACT.Sigmoid, bias=g.v(bias, j)).then_inc(g.s["act_delta"], 1)
            g.count("act_delta", (mark, j))
            g.also("act_delta", ("free", ("lora", j, i)))
    for j in range(2):
        act.wait_ge(g.s["pe_delta"], g.at("mm", "gate", j))
        act.activation(g.rw_g[:, 2 * j:2 * j + 2, :].rearrange("p a b -> p (a b)"),
                                  g.bank(("gate", j))[:, :], ACT.Copy).then_inc(g.s["act_delta"], 1)
        g.count("act_delta", ("free", ("gate", j)))
    g.also("act_delta", "gates")
    act.wait_ge(g.s["dve_delta"], g.at("kk", 3))
    act.activation(g.w4[:, :, :], g.rw_kk[:, :, :], ACT.Square).then_inc(g.s["act_delta"], 1)
    g.count("act_delta", "kk sq")
    for i in range(2):
        act.wait_ge(g.s["pe_delta"], g.at("mm", "kk", i))
        act.activation(g.w4b[:, 2 * i:2 * i + 2, :].rearrange("p a b -> p (a b)"), g.bank(("kk", i))[:, :],
                                  ACT.Sqrt).then_inc(g.s["act_delta"], 1)
        g.count("act_delta", ("free", ("kk", i)))
        g.also("act_delta", ("kk norm", i))
    act.wait_ge(g.s["dve_delta"], g.at("cum before"))
    act.activation(g.w4b[:, :, :], g.lnw[:, :, :], ACT.Exp).then_inc(g.s["act_delta"], 1)
    g.count("act_delta", "exp before")
    act.activation(g.w4c[:, :, :], g.cum[:, :, :], ACT.Exp, scale=-1.0).then_inc(g.s["act_delta"], 1)
    g.count("act_delta", "exp minus")
    act.wait_ge(g.s["act_delta"], g.so_far("act_delta"))
    act.activation(g.cum[:, :, :], g.cum[:, :, :], ACT.Exp).then_inc(g.s["act_delta"], 1)
    g.count("act_delta", "exp cum")


def delta_in_pe(g, pe):
    n, w = g.next_weights()
    pe.wait_ge(g.slab_in[n % RING], 16 * (n // RING + 1))
    g.lora_slab = n
    g.lora = w
    wa2 = w[:, 0:512]
    pe.wait_ge(g.s["act_delta"], g.at("tanh w"))
    pe.wait_ge(g.s["dve_delta"], g.at("shifted", 12))
    x = g.prj[:, 12:14, 1:257]
    for j in range(4):
        for i, r in enumerate((slice(0, 64), slice(64, 128))):
            pe.wait_ge(*g.bank_free())
            ps = g.open(("lora", j, i))
            mm(pe, ps[:, 0:L], wa2[r, P * j:P * j + P], x[r, 0, :]).then_inc(g.s["pe_delta"], 1)
            g.count("pe_delta", ("mm", "lora", j, i))
    pe.wait_ge(g.s["act_delta"], g.at("sig g"))
    for j in range(2):
        pe.wait_ge(*g.bank_free())
        ps = g.open(("gate", j))
        for i in range(2):
            a = 512 + P * (2 * j + i)
            last = mm(pe, ps[:, L * i:L * i + L], w[:, a:a + P], x[:, 1, :])
        last.then_inc(g.s["pe_delta"], 1)
        g.count("pe_delta", ("mm", "gate", j))
    pe.wait_ge(g.s["act_delta"], g.at("kk sq"))
    for i in range(2):
        pe.wait_ge(*g.bank_free())
        ps = g.open(("kk", i))
        mm(pe, ps[:, :], g.tab("headones"), g.w4[:, 2 * i:2 * i + 2, :].rearrange("p a b -> p (a b)")).then_inc(g.s["pe_delta"], 1)
        g.count("pe_delta", ("mm", "kk", i))


def rows_of(h):
    return slice(HD * (h % 2), HD * (h % 2) + HD)


def delta_pe(g, pe, tt):
    pe.wait_ge(g.s["dve_delta"], g.at("A~"))
    pe.wait_ge(g.s["dve_delta"], g.at("B~"))
    pe.wait_ge(g.s["dve_delta"], g.at("K~"))
    pe.wait_ge(g.s["dve_delta"], g.at("R~"))
    pe.wait_ge(g.s["dve_delta"], g.at("chunk ends"))
    c = slice(P * tt, P * tt + P)
    src = [g.ar[:, :, tt, 0, :], g.bt[:, :, c], g.kt[:, :, c], g.prj[:, 8:12, 1 + P * tt:1 + P * tt + P]]
    for n, s in enumerate(src):
        pe.wait_ge(*g.bank_free())
        ps = g.open(("tok", tt, n))
        for j in range(4):
            last = pe.transpose(ps[:, P * j:P * j + P], s[:, j, :], g.tab("ident"))
        last.then_inc(g.s["pe_delta"], 1)
        g.count("pe_delta", ("mm", "tok", tt, n))
    for h in range(8):
        r, j = rows_of(h), h // 2
        pe.wait_ge(*g.bank_free())
        ps = g.open(("mp", tt, h))
        both = g.ar[r, j, tt, :, :].rearrange("p w c -> p (w c)")
        mm(pe, ps[:, 0:256], g.bt[r, j, c], both)
        mm(pe, ps[:, 256:512], g.kt[r, j, c], both).then_inc(g.s["pe_delta"], 1)
        g.count("pe_delta", ("mm", "mp", tt, h))
    for odd in range(2):
        pe.wait_ge(*g.bank_free())
        ps = g.open(("low", tt, odd))
        for j in range(4):
            r = rows_of(odd)
            last = mm(pe, ps[:, P * j:P * j + P], g.ar[r, j, tt, 0, :], g.bt[r, j, c])
        last.then_inc(g.s["pe_delta"], 1)
        g.count("pe_delta", ("mm", "low", tt, odd))
    for lv in range(5):
        pe.wait_ge(g.s["dve_delta"], g.at("F", tt, lv, 0))
        pe.wait_ge(g.s["dve_delta"], g.at("F", tt, lv, 1))
        pe.wait_ge(g.s["dve_delta"], g.at("powers", tt, lv, 0))
        pe.wait_ge(g.s["dve_delta"], g.at("powers", tt, lv, 1))
        pe.wait_ge(*g.moment(("lows", tt, lv, 0)))
        pe.wait_ge(*g.moment(("lows", tt, lv, 1)))
        for odd in range(2):
            heads = [2 * j + odd for j in range(4)]
            if lv < 4:
                pe.wait_ge(*g.bank_free())
                ps = g.open(("D", tt, lv, odd))
                for j, h in enumerate(heads):
                    last = mm(pe, ps[:, P * j:P * j + P], g.mp[:, h, 0, :], g.dm[:, h, :])
                last.then_inc(g.s["pe_delta"], 1)
                g.count("pe_delta", ("mm", "D", tt, lv, odd))
            if lv < 3:
                pe.wait_ge(*g.bank_free())
                ps = g.open(("U", tt, lv, odd))
                for j, h in enumerate(heads):
                    last = mm(pe, ps[:, P * j:P * j + P], g.dm[:, h, :], g.mp[:, h, 0, :])
                last.then_inc(g.s["pe_delta"], 1)
                g.count("pe_delta", ("mm", "U", tt, lv, odd))
            if lv > 0:
                pe.wait_ge(*g.bank_free())
                ps = g.open(("Fp", tt, lv, odd))
                for j, h in enumerate(heads):
                    last = mm(pe, ps[:, P * j:P * j + P], g.dm[:, h, :], g.fm[:, h, :])
                last.then_inc(g.s["pe_delta"], 1)
                g.count("pe_delta", ("mm", "Fp", tt, lv, odd))
            g.also("pe_delta", ("read", tt, lv, odd))
    pe.wait_ge(g.s["dve_delta"], g.at("F", tt, 5, 0))
    pe.wait_ge(g.s["dve_delta"], g.at("F", tt, 5, 1))
    pe.wait_ge(*g.bank_free())
    ps = g.open(("NV", tt))
    for h in range(8):
        last = mm(pe, ps[:, HD * h:HD * h + HD], g.mp[:, h, 2, :], g.tok[:, 3, HD * h:HD * h + HD])
    last.then_inc(g.s["pe_delta"], 1)
    g.count("pe_delta", ("mm", "NV", tt))
    pe.wait_ge(*g.bank_free())
    ps = g.open(("WT", tt))
    for h in range(8):
        last = mm(pe, ps[rows_of(h), P * (h // 2):P * (h // 2) + P], g.tok[:, 0, HD * h:HD * h + HD], g.fm[:, h, :])
    last.then_inc(g.s["pe_delta"], 1)
    g.count("pe_delta", ("mm", "WT", tt))
    pe.wait_ge(g.s["act_delta"], g.at("nv", tt))
    pe.wait_ge(*g.bank_free())
    ps = g.open(("Z", tt))
    for h in range(8):
        last = mm(pe, ps[:, HD * h:HD * h + HD], g.fm[:, h, :], g.nv[:, HD * h:HD * h + HD])
    last.then_inc(g.s["pe_delta"], 1)
    g.count("pe_delta", ("mm", "Z", tt))
    pe.wait_ge(g.s["act_delta"], g.at("wt", tt))
    for cc in range(4):
        n = 4 * tt + cc
        q = slice(CH * cc, CH * cc + CH)
        pe.wait_ge(g.s["dve_delta"], g.at("state", n))
        for odd in range(2):
            pe.wait_ge(*g.bank_free())
            ps = g.open(("u", n, odd))
            for j in range(4):
                last = mm(pe, ps[q, HD * j:HD * j + HD], g.wt[rows_of(odd), j, q],
                          g.states[rows_of(odd), n % 5, HD * j:HD * j + HD])
            last.then_inc(g.s["pe_delta"], 1)
            g.count("pe_delta", ("mm", "u", n, odd))
        pe.wait_ge(*g.bank_free())
        ps = g.open(("s", n))
        pe.wait_ge(g.s["dve_delta"], g.at("U row", n))
        for h in range(8):
            o = ps[rows_of(h), HD * (h // 2):HD * (h // 2) + HD]
            v = slice(HD * h, HD * h + HD)
            mm(pe, o, g.tok[q, 2, v], g.tok[q, 3, v], True, False)
            last = mm(pe, o, g.tok[q, 1, v], g.u[q, v], False, True)
        last.then_inc(g.s["pe_delta"], 1)
        g.count("pe_delta", ("mm", "s", n))
    for odd in range(2):
        r = rows_of(odd)
        pe.wait_ge(*g.bank_free())
        ps = g.open(("y", tt, odd))
        for j in range(4):
            h = 2 * j + odd
            v, o = slice(HD * h, HD * h + HD), slice(P * j, P * j + P)
            mm(pe, ps[r, o], g.u[:, v], g.mp[:, h, 1, :], True, False)
            mm(pe, ps[r, o], g.tok[:, 3, v], g.mp[:, h, 3, :], False, False)
            for cc in range(4):
                o = slice(P * j + CH * cc, P * j + CH * cc + CH)
                last = mm(pe, ps[r, o], g.states[r, (4 * tt + cc) % 5, HD * j:HD * j + HD],
                          g.ar[r, j, tt, 1, CH * cc:CH * cc + CH], False, cc == 3)
        last.then_inc(g.s["pe_delta"], 1)
        g.count("pe_delta", ("mm", "y", tt, odd))


def delta_act(g, act, tt):
    for n in range(4):
        act.wait_ge(g.s["pe_delta"], g.at("mm", "tok", tt, n))
        if tt:
            act.wait_ge(g.s["pe_delta"], g.at("mm", "y", tt - 1, 1))
        act.activation(g.tok[:, n, :], g.bank(("tok", tt, n))[:, :], ACT.Copy).then_inc(g.s["act_delta"], 1)
        g.count("act_delta", ("free", ("tok", tt, n)))
    g.also("act_delta", ("toks", tt))
    for lv in range(4):
        act.wait_ge(g.s["pe_delta"], g.at("read", tt, lv, 1))
        for odd in range(2):
            act.activation(heads_of(g.dm, odd), four(g.bank(("D", tt, lv, odd))), ACT.Copy).then_inc(g.s["act_delta"], 1)
            g.count("act_delta", ("free", ("D", tt, lv, odd)))
            g.also("act_delta", ("lows", tt, lv + 1, odd))
    for key, dst, mark in (("NV", g.nv, "nv"), ("WT", g.wt.rearrange("p a b -> p (a b)"), "wt"), ("Z", g.z, "z")):
        act.wait_ge(g.s["pe_delta"], g.at("mm", key, tt))
        act.activation(dst, g.bank((key, tt))[:, :], ACT.Copy).then_inc(g.s["act_delta"], 1)
        g.count("act_delta", ("free", (key, tt)))
        g.also("act_delta", (mark, tt))
    for odd in range(2):
        r = rows_of(odd)
        act.wait_ge(g.s["pe_delta"], g.at("mm", "y", tt, odd))
        act.activation(g.y[r, :, P * tt:P * tt + P], four(g.bank(("y", tt, odd)))[r], ACT.Copy).then_inc(g.s["act_delta"], 1)
        g.count("act_delta", ("free", ("y", tt, odd)))
    g.also("act_delta", ("y done", tt))


def four(ps):
    return ps[:, :].rearrange("p (a b) -> p a b", a=4)


def heads_of(m, odd):
    return m.rearrange("p (j o) c -> p j o c", o=2)[:, :, odd, :]


def delta_dve(g, dve, tt):
    masks = g.tab("chunk_masks")
    if tt:
        dve.wait_ge(g.s["pe_delta"], g.at("mm", "y", tt - 1, 1))
    for h in range(8):
        dve.wait_ge(g.s["pe_delta"], g.at("mm", "mp", tt, h))
        dve.tensor_tensor(g.mp[:, h, :, :].rearrange("p w c -> p (w c)"), g.bank(("mp", tt, h))[:, :], masks,
                                     ALU.mult).then_inc(g.s["dve_delta"], 1)
        g.count("dve_delta", ("free", ("mp", tt, h)))
    ups = g.mp[:, :, 0, :]
    for odd in range(2):
        dve.wait_ge(g.s["pe_delta"], g.at("mm", "low", tt, odd))
        dve.tensor_tensor(heads_of(g.dm, odd), four(g.bank(("low", tt, odd))), four(g.tab("strict_low")),
                                     ALU.mult).then_inc(g.s["dve_delta"], 1)
        g.count("dve_delta", ("free", ("low", tt, odd)))
        g.also("dve_delta", ("lows", tt, 0, odd))
        g.also("dve_delta", ("powers", tt, 0, odd))
    dve.wait_ge(g.s["dve_delta"], g.so_far("dve_delta"))
    ident = g.tab("ident").unsqueeze(1).broadcast_to((P, 8, P))
    dve.tensor_tensor(g.fm[:, :, :], ups, ident, ALU.add).then_inc(g.s["dve_delta"], 1)
    g.count("dve_delta", ("F", tt, 0, 0))
    g.also("dve_delta", ("F", tt, 0, 1))
    g.also("dve_delta", ("F", tt, 1, 0))
    g.also("dve_delta", ("F", tt, 1, 1))
    for lv in range(5):
        for odd in range(2):
            if lv < 3:
                dve.wait_ge(g.s["pe_delta"], g.at("read", tt, lv, 1))
                dve.tensor_copy(heads_of(ups, odd), four(g.bank(("U", tt, lv, odd)))).then_inc(g.s["dve_delta"], 1)
                g.count("dve_delta", ("free", ("U", tt, lv, odd)))
            g.also("dve_delta", ("powers", tt, lv + 1, odd))
            if lv > 0:
                dve.wait_ge(g.s["pe_delta"], g.at("mm", "Fp", tt, lv, odd))
                f = heads_of(g.fm, odd)
                dve.tensor_tensor(f, four(g.bank(("Fp", tt, lv, odd))), f, ALU.add).then_inc(g.s["dve_delta"], 1)
                g.count("dve_delta", ("free", ("Fp", tt, lv, odd)))
                g.also("dve_delta", ("F", tt, lv + 1, odd))
    dve.wait_ge(g.s["act_delta"], g.at("z", tt))
    for cc in range(4):
        n = 4 * tt + cc
        q = slice(CH * cc, CH * cc + CH)
        for odd in range(2):
            dve.wait_ge(g.s["pe_delta"], g.at("mm", "u", n, odd))
            alt = lambda x: x.rearrange("p (j o v) -> p j o v", o=2, v=HD)[:, :, odd, :]
            dve.tensor_tensor(alt(g.u[q, :]), g.bank(("u", n, odd))[q, 0:L].rearrange("p (j v) -> p j v", v=HD),
                                         alt(g.z[q, :]), ALU.add).then_inc(g.s["dve_delta"], 1)
            g.count("dve_delta", ("free", ("u", n, odd)))
        g.also("dve_delta", ("U row", n))
        dve.wait_ge(g.s["pe_delta"], g.at("mm", "s", n))
        if n >= 4:
            dve.wait_ge(g.s["pe_delta"], g.at("mm", "y", 0, 1))
        now, new = g.states[:, n % 5, :], g.states[:, (n + 1) % 5, :]
        dve.tensor_tensor(new, g.bank(("s", n))[:, 0:L], now, ALU.add).then_inc(g.s["dve_delta"], 1)
        g.count("dve_delta", ("free", ("s", n)))
        dve.wait_ge(g.s["dve_delta"], g.so_far("dve_delta"))
        end = g.lend[:, :, n:n + 1].broadcast_to((P, 4, HD))
        new4 = new.rearrange("p (j v) -> p j v", v=HD)
        dve.tensor_tensor(new4, new4, end, ALU.mult).then_inc(g.s["dve_delta"], 1)
        g.count("dve_delta", ("state", n + 1))
        dve.wait_ge(g.s["dve_delta"], g.so_far("dve_delta"))


def delta_out_dve(g, dve):
    dve.wait_ge(g.s["act_delta"], g.at("y done", 1))
    r, k, v = g.prj[:, 0:4, 1:257], g.prj[:, 4:8, 1:257], g.prj[:, 8:12, 1:257]
    for j in range(4):
        dve.scalar_tensor_tensor(g.w4[:, j, :], r[:, j, :], g.v("rw_rk_0_2", j), k[:, j, :],
                                            ALU.mult, ALU.mult).then_inc(g.s["dve_delta"], 1)
        g.count("dve_delta", ("rkk", j))
    flat = lambda x, i: x[:, 2 * i:2 * i + 2, :].rearrange("p a b -> p (a b)")
    for i in range(2):
        dve.wait_ge(g.s["pe_delta"], g.at("mm", "d mean", i))
        dve.scalar_tensor_tensor(flat(g.y, i), g.bank(("d mean", i))[:, :], -1.0 / HD, flat(g.y, i),
                                            ALU.mult, ALU.add).then_inc(g.s["dve_delta"], 1)
        g.count("dve_delta", ("free", ("d mean", i)))
    for i in range(2):
        dve.wait_ge(g.s["pe_delta"], g.at("mm", "bonus", i))
        b = g.bank(("bonus", i))[:, :].rearrange("p (a b) -> p a b", a=2)
        dve.tensor_tensor(g.w4c[:, 2 * i:2 * i + 2, :], b, v[:, 2 * i:2 * i + 2, :], ALU.mult).then_inc(g.s["dve_delta"], 1)
        g.count("dve_delta", ("free", ("bonus", i)))
    dve.wait_ge(g.s["act_delta"], g.at("free", ("d var", 1)))
    dve.reciprocal(g.w4b[:, :, :], g.w4b[:, :, :]).then_inc(g.s["dve_delta"], 1)
    g.count("dve_delta")
    dve.wait_ge(g.s["dve_delta"], g.so_far("dve_delta"))
    dve.tensor_tensor(g.y[:, :, :], g.y[:, :, :], g.w4b[:, :, :], ALU.mult).then_inc(g.s["dve_delta"], 1)
    g.count("dve_delta", "y normed")
    for j in range(4):
        dve.wait_ge(g.s["act_delta"], g.at("y affine", j))
        dve.tensor_tensor(g.y[:, j, :], g.y[:, j, :], g.w4c[:, j, :], ALU.add).then_inc(g.s["dve_delta"], 1)
        g.count("dve_delta")
    dve.wait_ge(g.s["dve_delta"], g.so_far("dve_delta"))
    dve.tensor_tensor(g.aT[:, 0:4, 0:L], g.y[:, :, :], g.rw_g[:, :, :], ALU.mult).then_inc(g.s["dve_delta"], 1)
    g.count("dve_delta", "y delta")


def delta_out_pe(g, pe):
    flat = lambda x, i: x[:, 2 * i:2 * i + 2, :].rearrange("p a b -> p (a b)")
    pe.wait_ge(g.s["act_delta"], g.at("y done", 1))
    for what, src, key in (("d mean", g.y, ("y done", 1)), ("bonus", g.w4, ("rkk", 3)), ("d var", g.w4b, "d sq")):
        pe.wait_ge(*g.moment(key))
        for i in range(2):
            pe.wait_ge(*g.bank_free())
            ps = g.open((what, i))
            mm(pe, ps[:, :], g.tab("headones"), flat(src, i)).then_inc(g.s["pe_delta"], 1)
            g.count("pe_delta", ("mm", what, i))


def delta_out_act(g, act):
    flat = lambda x, i: x[:, 2 * i:2 * i + 2, :].rearrange("p a b -> p (a b)")
    act.wait_ge(g.s["dve_delta"], g.at("free", ("d mean", 1)))
    act.activation(g.w4b[:, :, :], g.y[:, :, :], ACT.Square).then_inc(g.s["act_delta"], 1)
    g.count("act_delta", "d sq")
    for i in range(2):
        act.wait_ge(g.s["pe_delta"], g.at("mm", "d var", 1))
        act.activation(flat(g.w4b, i), g.bank(("d var", i))[:, :], ACT.Sqrt, bias=g.eps[:, 1:2],
                                  scale=1.0 / HD).then_inc(g.s["act_delta"], 1)
        g.count("act_delta", ("free", ("d var", i)))
    act.wait_ge(g.s["dve_delta"], g.at("y normed"))
    for j in range(4):
        act.activation(g.y[:, j, :], g.y[:, j, :], ACT.Identity, bias=g.v("rw_lnx_b_0_2", j),
                                  scale=g.v("rw_lnx_g_0_2", j)).then_inc(g.s["act_delta"], 1)
        g.count("act_delta", ("y affine", j))


MLA_D, MLA_SCALE = 96, 96 ** -0.5


def mla_act(g, act):
    act.wait_ge(g.s["dve_delta"], g.at("y delta"))
    act.activation(g.w4[:, 0:3, :], g.lat[:, 0:3, :], ACT.Square).then_inc(g.s["act_latent"], 1)
    g.count("act_latent", "lat sq")
    for i, (n, width) in enumerate(((0, 256), (1, 128))):
        act.wait_ge(g.s["pe_latent"], g.at("mm", "lat", i))
        act.activation(g.w4b[:, i, :], g.bank(("lat", i))[:, 0:L], ACT.Sqrt, bias=g.eps[:, 0:1],
                                  scale=1.0 / width).then_inc(g.s["act_latent"], 1)
        g.count("act_latent", ("free", ("lat", i)))
    g.also("act_latent", "lat rms")
    for a in range(4):
        act.wait_ge(g.s["pe_latent"], g.at("mm", "mla q", a))
        act.activation(g.mq[0:96, 2 * a:2 * a + 2, :].rearrange("p a b -> p (a b)"),
                                  g.bank(("mla q", a))[0:96, :], ACT.Copy, scale=MLA_SCALE).then_inc(g.s["act_latent"], 1)
        g.count("act_latent", ("free", ("mla q", a)))
    g.also("act_latent", "mla q raw")
    for a in range(4):
        act.wait_ge(g.s["pe_latent"], g.at("mm", "mla k", a))
        act.activation(g.mk[0:64, 2 * a:2 * a + 2, :].rearrange("p a b -> p (a b)"),
                                  g.bank(("mla k", a))[0:64, :], ACT.Copy).then_inc(g.s["act_latent"], 1)
        g.count("act_latent", ("free", ("mla k", a)))
    for t in range(2):
        act.wait_ge(g.s["pe_latent"], g.at("mm", "mla v", t))
        act.activation(g.mv[:, t, :], g.bank(("mla v", t))[:, :], ACT.Copy).then_inc(g.s["act_latent"], 1)
        g.count("act_latent", ("free", ("mla v", t)))
    act.wait_ge(g.s["dve_latent"], g.at("kpe"))
    act.activation(g.mk[64:96, :, :], g.lat[64:96, 3:4, :].broadcast_to((32, 8, L)), ACT.Copy).then_inc(g.s["act_latent"], 1)
    g.count("act_latent", "mla have")


def mla_pe(g, pe):
    pe.wait_ge(g.s["act_latent"], g.at("lat sq"))
    for i, ts in enumerate(((0, 1), (2,))):
        pe.wait_ge(*g.bank_free())
        ps = g.open(("lat", i))
        for t in ts:
            last = mm(pe, ps[:, 0:L], g.tab("ones"), g.w4[:, t, :], t == ts[0], t == ts[-1])
        last.then_inc(g.s["pe_latent"], 1)
        g.count("pe_latent", ("mm", "lat", i))
    pe.wait_ge(g.s["dve_latent"], g.at("lat normed"))
    wuq = g.lora[:, 1024:2560].rearrange("p (k c) -> p k c", k=2)
    wukv = g.lora[:, 2560:3584].rearrange("p (h w c) -> p h w c", h=8, w=2)
    for a in range(4):
        pe.wait_ge(*g.bank_free())
        ps = g.open(("mla q", a))
        for i in range(2):
            h = 2 * a + i
            for k in range(2):
                last = mm(pe, ps[0:96, L * i:L * i + L], wuq[:, k, 96 * h:96 * h + 96], g.lat[:, k, :], k == 0, k == 1)
        last.then_inc(g.s["pe_latent"], 1)
        g.count("pe_latent", ("mm", "mla q", a))
    for a in range(4):
        pe.wait_ge(*g.bank_free())
        ps = g.open(("mla k", a))
        for i in range(2):
            last = mm(pe, ps[0:64, L * i:L * i + L], wukv[:, 2 * a + i, 0, :], g.lat[:, 2, :])
        last.then_inc(g.s["pe_latent"], 1)
        g.count("pe_latent", ("mm", "mla k", a))
    for t in range(2):
        pe.wait_ge(*g.bank_free())
        ps = g.open(("mla v", t))
        mm(pe, ps[:, :], g.lat[:, 2, P * t:P * t + P], wukv[:, :, 1, :]).then_inc(g.s["pe_latent"], 1)
        g.count("pe_latent", ("mm", "mla v", t))
    g.also("pe_latent", ("used", g.lora_slab))
    swap = g.tab("mla_swap")[64:96, 64:96]
    pe.wait_ge(g.s["act_latent"], g.at("mla q raw"))
    for a in range(4):
        pe.wait_ge(*g.bank_free())
        ps = g.open(("q swap", a))
        mm(pe, ps[64:96, :], swap, g.mq[64:96, 2 * a:2 * a + 2, :].rearrange("p a b -> p (a b)")).then_inc(g.s["pe_latent"], 1)
        g.count("pe_latent", ("mm", "q swap", a))
    pe.wait_ge(*g.bank_free())
    ps = g.open(("k swap",))
    mm(pe, ps[64:96, 0:L], swap, g.lat[64:96, 3, :]).then_inc(g.s["pe_latent"], 1)
    g.count("pe_latent", ("mm", "k swap"))


def mla_dve(g, dve):
    dve.wait_ge(g.s["act_latent"], g.at("lat rms"))
    dve.reciprocal(g.w4b[:, 0:2, :], g.w4b[:, 0:2, :]).then_inc(g.s["dve_latent"], 1)
    g.count("dve_latent")
    dve.wait_ge(g.s["dve_latent"], g.so_far("dve_latent"))
    for t, (n, i) in enumerate((("mla_qnorm_0_2", 0), ("mla_qnorm_0_2", 0), ("mla_kvnorm_0_2", 1))):
        dve.scalar_tensor_tensor(g.lat[:, t, :], g.lat[:, t, :], g.v(n, t % 2), g.w4b[:, i, :],
                                            ALU.mult, ALU.mult).then_inc(g.s["dve_latent"], 1)
        g.count("dve_latent", "lat normed")
    r = slice(64, 96)
    cos, sin = g.tab("mla_cos")[r, :], g.tab("mla_sin")[r, :]
    for a in range(5):
        x = g.mq[r, 2 * a:2 * a + 2, :] if a < 4 else g.lat[r, 3:4, :]
        n = 2 if a < 4 else 1
        key = ("q swap", a) if a < 4 else ("k swap",)
        dve.wait_ge(g.s["pe_latent"], g.at("mm", *key))
        t = g.w4[r, 0:n, :]
        dve.tensor_tensor(t, g.bank(key)[r, 0:L * n].rearrange("p (a b) -> p a b", a=n),
                                     sin.unsqueeze(1).broadcast_to((32, n, L)), ALU.mult).then_inc(g.s["dve_latent"], 1)
        g.count("dve_latent", ("free", key))
        dve.tensor_tensor(x, x, cos.unsqueeze(1).broadcast_to((32, n, L)), ALU.mult).then_inc(g.s["dve_latent"], 1)
        g.count("dve_latent")
        dve.wait_ge(g.s["dve_latent"], g.so_far("dve_latent"))
        dve.tensor_tensor(x, x, t, ALU.add).then_inc(g.s["dve_latent"], 1)
        g.count("dve_latent", ("mla rotated", a))
        dve.wait_ge(g.s["dve_latent"], g.so_far("dve_latent"))
    g.also("dve_latent", "kpe")


def causal_of(g, q, k, v, out, ready, d=None, rows=None):
    def scores(h, t):
        if rows:
            pairs = [(q[0:rows, h, P * t:P * t + P], k[0:rows, h, 0:P * t + P])]
        else:
            pairs = [(q[rows_of(h), h // 2, P * t:P * t + P], k[rows_of(h), h // 2, 0:P * t + P])]
        if d is not None:
            pairs.append((g.tab("row")[:, P * h:P * h + P], d[:, 0:P * t + P]))
        return [(0, pairs)]

    return dict(heads=8, scores=scores, width=lambda t: P * t + P, add=lambda h, t: [(P * t, g.tab("causal"))],
                     values=lambda h, t: v[:, t, HD * h:HD * h + HD], out=out, ready=ready)


def glu_pe(g, pe, key):
    g.x = lambda k: (g.half_upper(k), g.aT[:, k, 0:L])
    for i in range(KF // 2):
        outs = []
        for j in range(2):
            t = 2 * i + j
            outs += [(("gate", key, t), slice(0, L), (P * j, P), None, ("mm", "gate", key, t)),
                     (("up", key, t), slice(0, L), (256 + P * j, P), None, ("mm", "up", key, t))]
        products(g, pe, g.slabs[g.next_slab], KD, outs, "feedforward", ("x", "ffn0") if i == 0 else None)
    g.x = lambda k: (g.hid2_upper[:, k, :], g.hid2[:, k, :])
    for m in range(KD):
        products(g, pe, g.slabs[g.next_slab], KF, [(("gd", key, m), slice(0, L), (0, P), None, ("mm", "gd", key, m))],
                 "feedforward", ("hidden", key) if m == 0 else None)


def glu_act(g, act, key):
    def upper_hidden(t):
        act.wait_ge(g.s["dve_feedforward"], g.at("hidden f32", key, t))
        act.activation(exact(g.hid2_upper[:, t, :]), g.hid2[:, t, :], ACT.Copy).then_inc(g.s["act_feedforward"], 1)
        g.count("act_feedforward", ("upper hidden", key, t))

    for t in range(KF):
        if t % 2 == 0:
            upper_act(g, act, 1)
        act.wait_ge(g.s["pe_feedforward"], g.at("mm", "gate", key, t))
        if t >= 4:
            act.wait_ge(g.s["dve_feedforward"], g.at("hidden f32", key, t - 4))
        act.activation(g.gate2[:, t % 4, :], g.bank(("gate", key, t))[:, 0:L], ACT.Silu).then_inc(g.s["act_feedforward"], 1)
        g.count("act_feedforward", ("silu", key, t))
        g.also("act_feedforward", ("free", ("gate", key, t)))
        if t >= 1:
            upper_hidden(t - 1)
        if t % 2 == 1:
            upper_act(g, act, 1)
    upper_hidden(KF - 1)
    upper_act(g, act, 2 * KD - 2)


def glu_dve(g, dve, key):
    def lower_hidden(t):
        dve.wait_ge(g.s["act_feedforward"], g.at("upper hidden", key, t))
        x = g.hid2[:, t, :]
        dve.tensor_tensor(exact(x), x, rounded(g.hid2_upper[:, t, :]), ALU.subtract).then_inc(g.s["dve_feedforward"], 1)
        g.count("dve_feedforward", ("hidden", key, t))

    for t in range(KF):
        if t % 2 == 0:
            lower_dve(g, dve, 1)
        dve.wait_ge(g.s["act_feedforward"], g.at("silu", key, t))
        dve.wait_ge(g.s["pe_feedforward"], g.at("mm", "up", key, t))
        dve.tensor_tensor(g.hid2[:, t, :], g.bank(("up", key, t))[:, 0:L], g.gate2[:, t % 4, :], ALU.mult).then_inc(g.s["dve_feedforward"], 1)
        g.count("dve_feedforward", ("hidden f32", key, t))
        g.also("dve_feedforward", ("free", ("up", key, t)))
        if t >= 1:
            lower_hidden(t - 1)
        if t % 2 == 1:
            lower_dve(g, dve, 1)
    lower_hidden(KF - 1)


ODD = ("fq", "fk", "fv", "mq", "mk", "mv")


def odd_proj_pe(g, pe):
    g.x = lambda k: (g.half_upper(k), g.aT[:, k, 0:L])
    for name in ODD:
        outs = []
        for i in range(2):
            if name[1] == "v":
                outs.append(((name, i), slice(0, 512), (0, 512), i, ("mm", name, i)))
            else:
                outs += [((name, 2 * i + j), slice(0, L), (P * (2 * i + j), P), None, ("mm", name, 2 * i + j))
                         for j in range(2)]
        products(g, pe, g.slabs[g.next_slab], KD, outs, "projection", ("x", "mix1") if name == ODD[0] else None)
    n, w = g.next_weights()
    pe.wait_ge(g.slab_in[n % RING], 16 * (n // RING + 1))
    pe.wait_ge(*g.bank_free())
    ps = g.open(("forget",))
    for k in range(KD):
        mm(pe, ps[0:8, 0:L], w[:, 8 * k:8 * k + 8], rounded(g.half_upper(k)), k == 0, False)
        last = mm(pe, ps[0:8, 0:L], w[:, 8 * k:8 * k + 8], rounded(g.aT[:, k, 0:L]), False, k == KD - 1)
    last.then_inc(g.s["pe_projection"], 1)
    g.count("pe_projection", ("mm", "forget"))
    g.also("pe_projection", ("used", n))
    for name in ("mq", "mk"):
        pe.wait_ge(g.s["act_projection"], g.at("have", name))
        for i in range(2):
            pe.wait_ge(*g.bank_free())
            ps = g.open(("swap", name, i))
            mm(pe, ps[:, :], g.tab("full_swap"), g.q2[name][:, 2 * i:2 * i + 2, :].rearrange("p a b -> p (a b)")).then_inc(g.s["pe_projection"], 1)
            g.count("pe_projection", ("mm", "swap", name, i))


def odd_proj_act(g, act):
    for name in ODD:
        if name != ODD[-1]:
            upper_act(g, act, 1)
        for i in range(2 if name[1] == "v" else 4):
            act.wait_ge(g.s["pe_projection"], g.at("mm", name, i))
            dst = g.q2[name][:, i, :]
            act.activation(dst, g.bank((name, i))[:, 0:dst.shape[-1]], ACT.Copy, scale=HD ** -0.5 if name[1] == "q" else 1.0).then_inc(g.s["act_projection"], 1)
            g.count("act_projection", ("free", (name, i)))
        g.also("act_projection", ("have", name))
        if name != ODD[-1]:
            upper_act(g, act, 1)
    act.wait_ge(g.s["dve_projection"], g.at("minus abs"))
    act.activation(g.lsig[0:8, :], g.oneb[0:8, :], ACT.Exp).then_inc(g.s["act_projection"], 1)
    g.count("act_projection", "exp f")
    act.wait_ge(g.s["act_projection"], g.so_far("act_projection"))
    act.activation(g.lsig[0:8, :], g.lsig[0:8, :], ACT.Ln, bias=1.0).then_inc(g.s["act_projection"], 1)
    g.count("act_projection", "ln f")


def odd_proj_dve(g, dve):
    lower_dve(g, dve, 2 * len(ODD) - 2)
    dve.wait_ge(g.s["dve_norm"], g.at("aT", "mix1"))
    dve.memset(g.negd[:, :], 0.0).then_inc(g.s["dve_projection"], 1)
    g.count("dve_projection")
    f = g.negd[0:8, :]
    dve.wait_ge(g.s["pe_projection"], g.at("mm", "forget"))
    dve.wait_ge(g.s["dve_projection"], g.so_far("dve_projection"))
    dve.tensor_scalar(f, g.bank(("forget",))[0:8, 0:L], g.v("fox_bf_1_2")[0:8, :], None, ALU.add).then_inc(g.s["dve_projection"], 1)
    g.count("dve_projection", ("free", ("forget",)))
    dve.wait_ge(g.s["dve_projection"], g.so_far("dve_projection"))
    dve.scalar_tensor_tensor(g.oneb[0:8, :], f, -1.0, f, ALU.mult, ALU.min).then_inc(g.s["dve_projection"], 1)
    g.count("dve_projection", "minus abs")
    dve.tensor_scalar(f, f, 0.0, None, ALU.min).then_inc(g.s["dve_projection"], 1)
    g.count("dve_projection")
    dve.wait_ge(g.s["act_projection"], g.at("ln f"))
    dve.wait_ge(g.s["dve_projection"], g.so_far("dve_projection"))
    dve.tensor_tensor(g.lsig[0:8, :], g.lsig[0:8, :], f, ALU.subtract).then_inc(g.s["dve_projection"], 1)
    g.count("dve_projection")
    dve.memset(g.oneb[0:8, :], 1.0).then_inc(g.s["dve_projection"], 1)
    g.count("dve_projection")
    dve.wait_ge(g.s["dve_projection"], g.so_far("dve_projection"))
    dve.tensor_tensor_scan(f, g.oneb[0:8, :], g.lsig[0:8, :], 0.0, ALU.mult, ALU.add).then_inc(g.s["dve_projection"], 1)
    g.count("dve_projection", "minus D")
    cos = g.tab("full_cos").unsqueeze(1).broadcast_to((P, 2, L))
    sin = g.tab("full_sin").unsqueeze(1).broadcast_to((P, 2, L))
    for name in ("mq", "mk"):
        for i in range(2):
            x, t = g.q2[name][:, 2 * i:2 * i + 2, :], g.w4[:, 0:2, :]
            dve.wait_ge(g.s["pe_projection"], g.at("mm", "swap", name, i))
            dve.tensor_tensor(t, g.bank(("swap", name, i))[:, :].rearrange("p (a b) -> p a b", a=2), sin,
                                         ALU.mult).then_inc(g.s["dve_projection"], 1)
            g.count("dve_projection", ("free", ("swap", name, i)))
            dve.tensor_tensor(x, x, cos, ALU.mult).then_inc(g.s["dve_projection"], 1)
            g.count("dve_projection")
            dve.wait_ge(g.s["dve_projection"], g.so_far("dve_projection"))
            dve.tensor_tensor(x, x, t, ALU.add).then_inc(g.s["dve_projection"], 1)
            g.count("dve_projection", ("rotated", name))
            dve.wait_ge(g.s["dve_projection"], g.so_far("dve_projection"))


def route_pe(g, pe):
    n, w = g.next_weights()
    pe.wait_ge(g.slab_in[n % RING], 16 * (n // RING + 1))
    pe.wait_ge(g.s["dve_norm"], g.at("aT", "ffn1"))
    for t in range(2):
        pe.wait_ge(*g.bank_free())
        ps = g.open(("logits", t))
        for k in range(KD):
            last = mm(pe, ps[:, 0:8], g.aT[:, k, P * t:P * t + P], w[:, 8 * k:8 * k + 8], k == 0, k == KD - 1)
        last.then_inc(g.s["pe_routing"], 1)
        g.count("pe_routing", ("mm", "logits", t))
    g.also("pe_routing", ("used", n))
    for t in range(2):
        for q in range(2):
            pe.wait_ge(*g.bank_free())
            ps = g.open(("by token", t, q))
            for j in range(4):
                last = pe.transpose(ps[:, P * j:P * j + P], g.aT[:, 4 * q + j, P * t:P * t + P], g.tab("ident"))
            last.then_inc(g.s["pe_routing"], 1)
            g.count("pe_routing", ("mm", "by token", t, q))
    pe.wait_ge(g.s["dve_routing"], g.at("chosen", 1))
    pe.wait_ge(*g.bank_free())
    ps = g.open(("ranks",))
    m0, m1 = g.chosen[:, 0, :], g.chosen[:, 1, :]
    mm(pe, ps[:, 0:8], g.tab("before"), m0)
    mm(pe, ps[:, 8:16], g.tab("ones"), m0, True, False)
    mm(pe, ps[:, 8:16], g.tab("before"), m1, False, True)
    mm(pe, ps[:, 16:24], g.tab("ones"), m0, True, False)
    mm(pe, ps[:, 16:24], g.tab("ones"), m1, False, True).then_inc(g.s["pe_routing"], 1)
    g.count("pe_routing", ("mm", "ranks"))


def route_act(g, act):
    for t in range(2):
        act.wait_ge(g.s["dve_routing"], g.at("gap", t))
        act.activation(g.lg[:, t, 33:34], g.lg[:, t, 32:33], ACT.Exp).then_inc(g.s["act_routing"], 1)
        g.count("act_routing", ("exp gap", t))
    for t in range(2):
        for q in range(2):
            act.wait_ge(g.s["pe_routing"], g.at("mm", "by token", t, q))
            act.activation(g.t_tok[:, t, 512 * q:512 * q + 512], g.bank(("by token", t, q))[:, :],
                           ACT.Copy).then_inc(g.s["act_routing"], 1)
            g.count("act_routing", ("free", ("by token", t, q)))


def route_dve(g, dve):
    sem = g.s["dve_routing"]
    f = lambda t, a, n: g.lg[:, t, a:a + n]
    dve.wait_ge(g.s["dve_norm"], g.at("aT", "ffn1"))
    for t in range(2):
        dve.wait_ge(g.s["pe_routing"], g.at("mm", "logits", t))
        dve.tensor_copy(f(t, 0, 8), g.bank(("logits", t))[:, 0:8]).then_inc(sem, 1)
        g.count("dve_routing", ("free", ("logits", t)))
        dve.wait_ge(sem, g.so_far("dve_routing"))
        dve.max(f(t, 8, 8), f(t, 0, 8)).then_inc(sem, 1)
        g.count("dve_routing")
        dve.wait_ge(sem, g.so_far("dve_routing"))
        dve.max_index(f(t, 16, 8).bitcast(mybir.dt.uint32), f(t, 8, 8), f(t, 0, 8)).then_inc(sem, 1)
        g.count("dve_routing")
        dve.tensor_tensor(f(t, 32, 1), f(t, 9, 1), f(t, 8, 1), ALU.subtract).then_inc(sem, 1)
        g.count("dve_routing", ("gap", t))
        dve.wait_ge(sem, g.so_far("dve_routing"))
        dve.tensor_copy(f(t, 24, 8), f(t, 16, 8).bitcast(mybir.dt.uint32)).then_inc(sem, 1)
        g.count("dve_routing")
        dve.wait_ge(g.s["act_routing"], g.at("exp gap", t))
        dve.tensor_scalar(f(t, 34, 1), f(t, 33, 1), 1.0, None, ALU.add).then_inc(sem, 1)
        g.count("dve_routing")
        dve.wait_ge(sem, g.so_far("dve_routing"))
        dve.reciprocal(f(t, 35, 1), f(t, 34, 1)).then_inc(sem, 1)
        g.count("dve_routing")
        dve.wait_ge(sem, g.so_far("dve_routing"))
        dve.tensor_tensor(f(t, 36, 1), f(t, 35, 1), f(t, 33, 1), ALU.mult).then_inc(sem, 1)
        g.count("dve_routing")
        dve.wait_ge(sem, g.so_far("dve_routing"))
        for n, a in ((0, 40), (1, 48)):
            dve.tensor_scalar(f(t, a, 8), g.tab("expert_no"), f(t, 24 + n, 1), f(t, 35 + n, 1), ALU.is_equal,
                              ALU.mult).then_inc(sem, 1)
            g.count("dve_routing")
            dve.tensor_scalar(f(t, a + 16, 8), g.tab("expert_no"), f(t, 24 + n, 1), None, ALU.is_equal).then_inc(sem, 1)
            g.count("dve_routing")
        dve.wait_ge(sem, g.so_far("dve_routing"))
        dve.tensor_tensor(g.rt[:, 0:NE, 2 + t], f(t, 40, 8), f(t, 48, 8), ALU.add).then_inc(sem, 1)
        g.count("dve_routing")
        dve.tensor_tensor(g.chosen[:, t, :], f(t, 56, 8), f(t, 64, 8), ALU.add).then_inc(sem, 1)
        g.count("dve_routing", ("chosen", t))
    dve.wait_ge(g.s["pe_routing"], g.at("mm", "ranks"))
    dve.wait_ge(sem, g.so_far("dve_routing"))
    ps = g.bank(("ranks",))
    for t in range(2):
        dve.scalar_tensor_tensor(f(t, 40, 8), ps[:, 8 * t:8 * t + 8], 1.0, g.chosen[:, t, :], ALU.add,
                                 ALU.mult).then_inc(sem, 1)
        g.count("dve_routing")
    dve.tensor_reduce(f(0, 32, 1), ps[:, 16:24], AX.X, ALU.max).then_inc(sem, 1)
    g.count("dve_routing", ("free", ("ranks",)))
    dve.wait_ge(sem, g.so_far("dve_routing"))
    for t in range(2):
        dve.tensor_scalar(g.rt[:, 0:NE, t], f(t, 40, 8), -1.0, None, ALU.add).then_inc(sem, 1)
        g.count("dve_routing")
    dve.tensor_scalar(g.rounds[:, :], f(0, 32, 1), float(SLOTS), 1.0, ALU.is_gt, ALU.add).then_inc(sem, 1)
    g.count("dve_routing", "rounds")
    dve.wait_ge(sem, g.so_far("dve_routing"))
    dve.tensor_scalar(g.rt[:, NE, 0:2], g.rt[:, 0, 0:2], -float(SLOTS), None, ALU.add).then_inc(sem, 1)
    g.count("dve_routing")
    dve.tensor_copy(g.rt[:, NE, 2:4], g.rt[:, 0, 2:4]).then_inc(sem, 1)
    g.count("dve_routing", "routed")
    dve.wait_ge(sem, g.so_far("dve_routing"))


GU = FE // FC
HB = 4 * FC
WS = KD * FC


def halves_of(i):
    m = 4 * (FC if i % ES < 2 * GU else 512)
    return slice(0, m), slice(m, WS)


def rounds_of(g, e):
    return e.value_load(g.rounds[0:1, 0:1], min_val=1, max_val=2)


def experts_pe(g, pe):
    s = g.s
    pe.wait_ge(s["dve_routing"], g.at("routed"))
    pe.wait_ge(s["act_routing"], g.at("free", ("by token", 1, 1)))
    rounds = rounds_of(g, pe)
    pe.sem_inc(s["pe_experts"], g.per("pe_experts"))
    A, V = g.per("act_experts"), g.per("dve_experts")
    for q in range(2):
        pe.wait_ge(s["dve_first"], 1)
        for j in range(4):
            k = 4 * q + j
            for t in range(2):
                last = mm(pe, g.psum[4 + q][:, P * j:P * j + P], g.t_tok[:, t, P * k:P * k + P], g.perm[:, t, :],
                          t == 0, t == 1)
        last.then_inc(s["pe_first"], 1)
    g.enter("pe_experts")
    with pe.Fori(0, rounds) as r, pe.Fori(0, NE) as e:
        it = r * NE + e

        def weights(i):
            return g.upper[i % 3], g.ring[:, i % EXPERT_RING, 0:WS]

        def transposes(q):
            pe.wait_ge(s["dve_experts"], g.at("hidden", q + 1) + it * V)
            if q >= 2:
                pe.wait_ge(s["dve_experts"], g.at("hT lower", q - 2) + it * V)
            for j in range(4):
                c = P * (4 * q + j) % HB
                last = pe.transpose(g.psum[4 + q % 2][:, P * j:P * j + P], g.hb[:, c:c + P], g.tab("ident"))
            last.then_inc(s["pe_experts"], 1)
            g.count("pe_experts", ("turned", q))

        pe.wait_ge(s["dve_experts"], g.at("xg lower", 1) - V + it * V)
        for i in range(GU):
            for n, (what, bank) in enumerate((("gate", i % 2), ("up", 2 + i % 2))):
                wu, wl = weights(2 * i + n)
                if i >= 2:
                    pe.wait_ge(s["dve_experts"], g.at("hidden", i - 2) + it * V)
                else:
                    pe.wait_ge(s["dve_experts"], g.at("added", bank) - V + it * V)
                for k in range(KD):
                    if k % 4 == 0:
                        pe.wait_ge(s["dve_split"], 2 * (2 * i + n) + k // 4 + 1 + it * (2 * ES))
                    c = slice(FC * k, FC * k + FC)
                    last = mm3(pe, g.psum[bank][:, 0:FC], g.xg[:, 0, k, :], g.xg[:, 1, k, :], wu[:, c], wl[:, c],
                               k == 0, k == KD - 1)
                last.then_inc(s["pe_experts"], 1)
                g.count("pe_experts", (what, i))
            if i >= 2:
                transposes(i - 2)
        transposes(GU - 2)
        pe.wait_ge(s["dve_experts"], g.at("weighted") + it * V)
        pe.wait_ge(s["dve_experts"], g.at("hT lower", GU - 3) + it * V)
        for t in range(2):
            last = pe.transpose(g.psum[5][:, P * t:P * t + P], g.pw[:, t, :], g.tab("ident"))
        last.then_inc(s["pe_experts"], 1)
        g.count("pe_experts", "weighted turned")
        for half in range(2):
            for q in range(4):
                wu, wl = weights(2 * GU + 4 * half + q)
                if half == 0:
                    pe.wait_ge(s["dve_experts"], g.at("hT lower", min(GU - 2, (7 * q + 6) // 4)) + it * V)
                for k in range(7):
                    if k % 4 == 0:
                        pe.wait_ge(s["dve_split"], 2 * (2 * GU + 4 * half + q) + k // 4 + 1 + it * (2 * ES))
                    c = slice(512 * k, 512 * k + 512)
                    last = mm3(pe, g.psum[6 + half][:, :], g.hT2[:, 0, 7 * q + k, :], g.hT2[:, 1, 7 * q + k, :],
                               wu[:, c], wl[:, c], q == 0 and k == 0, q == 3 and k == 6)
                last.then_inc(s["pe_experts"], 1)
                g.count("pe_experts", ("down", half, q))
            if half == 0:
                pe.wait_ge(s["dve_experts"], g.at("slots") + it * V)
                pe.wait_ge(s["act_experts"], g.at("pwt") + it * A)
                for q in range(2):
                    for j in range(4):
                        k = 4 * q + j
                        for t in range(2):
                            last = mm(pe, g.psum[4 + q][:, P * j:P * j + P], g.t_tok[:, t, P * k:P * k + P],
                                      g.perm[:, t, :], t == 0, t == 1)
                    last.then_inc(s["pe_experts"], 1)
                    g.count("pe_experts", ("gathered", q))
        for m in range(4):
            pe.wait_ge(s["act_experts"], g.at("y", m // 2) + it * A)
            for j in range(2):
                c = 256 * m + P * j
                last = mm(pe, g.psum[m][:, L * j:L * j + L], g.yb[:, c:c + P], g.pwt[:, :])
            last.then_inc(s["pe_experts"], 1)
            g.count("pe_experts", ("scattered", m))
    g.leave()
    g.users = {}


def experts_act(g, act):
    s = g.s
    act.wait_ge(s["dve_routing"], g.at("routed"))
    rounds = rounds_of(g, act)
    A, V, Q = g.per("act_experts"), g.per("dve_experts"), g.per("pe_experts")
    for q in range(2):
        act.wait_ge(s["pe_first"], q + 1)
        act.activation(exact(g.xg[:, 0, 4 * q:4 * q + 4, :].rearrange("p a b -> p (a b)")), g.psum[4 + q][:, :],
                       ACT.Copy).then_inc(s["act_first"], 1)
    for n in range(2):
        act.wait_ge(g.expert_in[n], 16)
        for c in halves_of(n):
            act.activation(exact(g.upper[n][:, c]), g.ring[:, n, c], ACT.Copy).then_inc(s["act_split"], 1)
    act.sem_inc(s["act_experts"], A)
    g.enter("act_experts")
    with act.Fori(0, rounds) as r, act.Fori(0, NE) as e:
        it = r * NE + e

        def split(i):
            act.wait_ge(g.expert_in[i % EXPERT_RING], 16 * (i // EXPERT_RING + 1) + it * (16 * ES // EXPERT_RING))
            if i >= 3:
                act.wait_ge(s["pe_experts"], g.at(*g.use_of(i - 3)) + it * Q)
            else:
                act.wait_ge(s["pe_experts"], g.at(*g.use_of(ES + i - 3)) - Q + it * Q)
            for c in halves_of(i):
                act.activation(exact(g.upper[i % 3][:, c]), g.ring[:, i % EXPERT_RING, c],
                               ACT.Copy).then_inc(s["act_split"], 1)

        def turn(q):
            act.wait_ge(s["pe_experts"], g.at("turned", q) + it * Q)
            act.activation(exact(g.hT2[:, 0, 4 * q:4 * q + 4, :].rearrange("p a b -> p (a b)")), g.psum[4 + q % 2][:, :],
                           ACT.Copy).then_inc(s["act_experts"], 1)
            g.count("act_experts", ("hT", q))

        for i in range(GU):
            split(2 * i + 2)
            act.wait_ge(s["pe_experts"], g.at("gate", i) + it * Q)
            if i >= 2:
                act.wait_ge(s["dve_experts"], g.at("hidden", i - 2) + it * V)
            act.activation(g.sg[:, i % 2, :], g.psum[i % 2][:, 0:FC], ACT.Silu).then_inc(s["act_experts"], 1)
            g.count("act_experts", ("silu", i))
            split(2 * i + 3)
            if i >= 2:
                turn(i - 2)
        turn(GU - 2)
        act.wait_ge(s["pe_experts"], g.at("weighted turned") + it * Q)
        act.activation(g.pwt[:, :], g.psum[5][:, 0:L], ACT.Copy).then_inc(s["act_experts"], 1)
        g.count("act_experts", "pwt")
        for q in range(4):
            split(2 * GU + 2 + q)
        act.wait_ge(s["pe_experts"], g.at("down", 0, 3) + it * Q)
        act.activation(g.yb[:, 0:512], g.psum[6][:, :], ACT.Copy).then_inc(s["act_experts"], 1)
        g.count("act_experts", ("y", 0))
        for q in range(2):
            act.wait_ge(s["pe_experts"], g.at("gathered", q) + it * Q)
            act.activation(exact(g.xg[:, 0, 4 * q:4 * q + 4, :].rearrange("p a b -> p (a b)")), g.psum[4 + q][:, :],
                           ACT.Copy).then_inc(s["act_experts"], 1)
            g.count("act_experts", ("xg", q))
        for q in range(4):
            split(2 * GU + 6 + q)
        act.wait_ge(s["pe_experts"], g.at("down", 1, 3) + it * Q)
        act.activation(g.yb[:, 512:1024], g.psum[7][:, :], ACT.Copy).then_inc(s["act_experts"], 1)
        g.count("act_experts", ("y", 1))
    g.leave()


def experts_dve(g, dve):
    s = g.s
    rounds = rounds_of(g, dve)
    A, V, Q = g.per("act_experts"), g.per("dve_experts"), g.per("pe_experts")
    dve.tensor_copy(g.cur[:, :], g.rt_flat[:, 0:4]).then_inc(s["dve_round"], 1)
    dve.wait_ge(s["dve_round"], 1)
    for t in range(2):
        last = dve.tensor_scalar(g.perm[:, t, :], g.tab("slot_no"), g.cur[:, t:t + 1], None, ALU.is_equal)
    last.then_inc(s["dve_first"], 1)
    dve.wait_ge(s["dve_first"], 1)

    def lower_tokens(q):
        upper, lower = (g.xg[:, n, 4 * q:4 * q + 4, :].rearrange("p a b -> p (a b)") for n in range(2))
        return dve.tensor_tensor(exact(lower), g.psum[4 + q][:, :], rounded(upper), ALU.subtract)

    for q in range(2):
        dve.wait_ge(s["act_first"], q + 1)
        lower_tokens(q).then_inc(s["dve_first"], 1)
    for n in range(2):
        for h, c in enumerate(halves_of(n)):
            dve.wait_ge(s["act_split"], 2 * n + h + 1)
            w = g.ring[:, n, c]
            dve.tensor_tensor(exact(w), w, rounded(g.upper[n][:, c]), ALU.subtract).then_inc(s["dve_split"], 1)
    dve.wait_ge(s["dve_first"], 3)
    dve.sem_inc(s["dve_experts"], V)
    g.enter("dve_experts")
    with dve.Fori(0, rounds) as r:
        with dve.Fori(0, NE) as e:
            it = r * NE + e

            def split(i):
                for h, c in enumerate(halves_of(i)):
                    dve.wait_ge(s["act_split"], 2 * i + h + 1 + it * (2 * ES))
                    w = g.ring[:, i % EXPERT_RING, c]
                    dve.tensor_tensor(exact(w), w, rounded(g.upper[i % 3][:, c]),
                                      ALU.subtract).then_inc(s["dve_split"], 1)

            def turn(q):
                dve.wait_ge(s["act_experts"], g.at("hT", q) + it * A)
                upper, lower = (g.hT2[:, n, 4 * q:4 * q + 4, :].rearrange("p a b -> p (a b)") for n in range(2))
                dve.tensor_tensor(exact(lower), g.psum[4 + q % 2][:, :], rounded(upper), ALU.subtract).then_inc(s["dve_experts"], 1)
                g.count("dve_experts", ("hT lower", q))

            dve.wait_ge(s["pe_experts"], g.at("weighted turned") - Q + it * Q)
            for t in range(2):
                last = dve.tensor_scalar(g.pw[:, t, :], g.tab("slot_no"), g.cur[:, t:t + 1], g.cur[:, 2 + t:3 + t],
                                         ALU.is_equal, ALU.mult)
            last.then_inc(s["dve_experts"], 1)
            g.count("dve_experts", "weighted")
            dve.wait_ge(s["dve_experts"], g.so_far("dve_experts") + it * V)
            dve.tensor_copy(g.cur[:, :], g.rt_flat[:, bass.ds(4 * e + 4, 4)]).then_inc(s["dve_experts"], 1)
            g.count("dve_experts")
            dve.wait_ge(s["dve_experts"], g.so_far("dve_experts") + it * V)
            dve.wait_ge(s["pe_experts"], g.at("gate", 0) + it * Q)
            for t in range(2):
                last = dve.tensor_scalar(g.perm[:, t, :], g.tab("slot_no"), g.cur[:, t:t + 1], None, ALU.is_equal)
            last.then_inc(s["dve_experts"], 1)
            g.count("dve_experts", "slots")
            for i in range(GU):
                split(2 * i + 2)
                dve.wait_ge(s["pe_experts"], g.at("up", i) + it * Q)
                dve.wait_ge(s["act_experts"], g.at("silu", i) + it * A)
                c = FC * i % HB
                dve.tensor_tensor(g.hb[:, c:c + FC], g.psum[2 + i % 2][:, 0:FC], g.sg[:, i % 2, :],
                                  ALU.mult).then_inc(s["dve_experts"], 1)
                g.count("dve_experts", ("hidden", i))
                split(2 * i + 3)
                if i >= 2:
                    turn(i - 2)
            turn(GU - 2)
            for q in range(4):
                split(2 * GU + 2 + q)
            for q in range(2):
                dve.wait_ge(s["act_experts"], g.at("xg", q) + it * A)
                lower_tokens(q).then_inc(s["dve_experts"], 1)
                g.count("dve_experts", ("xg lower", q))
            for q in range(4):
                split(2 * GU + 6 + q)
            for m in range(4):
                dve.wait_ge(s["pe_experts"], g.at("scattered", m) + it * Q)
                h = g.hT[:, 2 * m:2 * m + 2, 0:L]
                dve.tensor_tensor(h, g.psum[m][:, :].rearrange("p (a b) -> p a b", a=2), h,
                                  ALU.add).then_inc(s["dve_experts"], 1)
                g.count("dve_experts", ("added", m))
        dve.tensor_scalar(g.rt[:, :, 0:2], g.rt[:, :, 0:2], -float(SLOTS), None, ALU.add).then_inc(s["dve_round"], 1)
        dve.wait_ge(s["dve_round"], r + 2)
    g.leave()
    dve.tensor_copy(g.cur[:, :], g.rt_flat[:, 0:4]).then_inc(s["dve_over"], 1)
    g.count("dve_over", "experts over")


def experts_sp(g, sp):
    s = g.s
    base = g.expert_base
    Q = g.per("pe_experts")
    for n in range(2):
        sp.wait_ge(*g.moment(("used", base - 1 - (base - 1 - n) % RING)))
        sp.dma_start(g.ring[:, n, 0:WS], g.io["stream"][base + n, :, 0:WS]).then_inc(g.expert_in[n], 16)
    sp.wait_ge(s["dve_routing"], g.at("rounds"))
    rounds = rounds_of(g, sp)
    with sp.Fori(0, rounds) as r, sp.Fori(0, NE) as e:
        it = r * NE + e
        for i in range(2, ES + 2):
            if i < EXPERT_RING:
                sp.wait_ge(s["pe_experts"], g.at(*g.use_of(ES + i - EXPERT_RING)) - Q + it * Q)
            else:
                sp.wait_ge(s["pe_experts"], g.at(*g.use_of(i - EXPERT_RING)) + it * Q)
            src = g.io["stream"][bass.ds(e * ES + (base + i), 1), :, 0:WS].rearrange("a p n -> p (a n)")
            sp.dma_start(g.ring[:, i % EXPERT_RING, 0:WS], src).then_inc(g.expert_in[i % EXPERT_RING], 16)


def store_pe(g, pe):
    pe.wait_ge(g.s["dve_norm"], g.at("aT", "last"))
    for t in range(2):
        for q in range(2):
            pe.wait_ge(*g.bank_free())
            ps = g.open(("out", t, q))
            for j in range(4):
                last = pe.transpose(ps[:, P * j:P * j + P], g.aT[:, 4 * q + j, P * t:P * t + P], g.tab("ident"))
            last.then_inc(g.s["pe_result"], 1)
            g.count("pe_result", ("mm", "out", t, q))


def store_act(g, act):
    for t in range(2):
        for q in range(2):
            act.wait_ge(g.s["pe_result"], g.at("mm", "out", t, q))
            act.activation(g.outs[:, t, 512 * q:512 * q + 512], g.bank(("out", t, q))[:, :], ACT.Copy).then_inc(g.s["act_result"], 1)
            g.count("act_result", ("stored", t))
        act.wait_ge(g.s["act_result"], g.so_far("act_result"))
        act.dma_start(g.io["out"][P * t:P * t + P, :], g.outs[:, t, :]).then_inc(g.out_sem, 16)
    act.wait_ge(g.out_sem, 32)


def plain_norm(g, kind, e, key, gain, ready, upper=None):
    if kind == "act":
        norm_act(g, e, key, g.hT, L, None, None, [ready], upper)
    if kind == "pe":
        norm_pe(g, e, key, L)
    if kind == "dve":
        norm_dve(g, e, key, g.hT, L, lambda k, s: g.v(gain, k), None, upper=upper)


def second_block(g, kind, e):
    def only(k, f, *a):
        if kind == k:
            f(g, e, *a)
    g.tab_at = packed(tables_b())[1]
    if kind == "act":
        e.wait_ge(g.s["dve_norm"], g.at("aT", ("final", 1)))
        e.dma_start(g.tabs[:, 0:g.io["tab_b"].shape[1]], g.io["tab_b"]).then_inc(g.const_in["tab_b"], 16)
        g.const_issued.append("tab_b")
    if kind in ("pe", "dve"):
        e.wait_ge(g.const_in["tab_b"], 16)
    plain_norm(g, kind, e, "mix0", "norm_mix_0_2", ("aT", ("final", 1)), g.half_upper)
    only("pe", even_proj_pe)
    only("act", even_proj_act)
    g.check(kind, "eproj", 0)
    only("dve", delta_in_dve)
    only("act", delta_in_act)
    only("pe", delta_in_pe)
    g.check(kind, "din", 0)
    for t in range(2):
        only("pe", delta_pe, t)
        only("act", delta_act, t)
        only("dve", delta_dve, t)
    only("dve", delta_out_dve)
    only("act", delta_out_act)
    only("pe", delta_out_pe)
    g.check(kind, "delta", 0)
    only("act", mla_act)
    only("pe", mla_pe)
    only("dve", mla_dve)
    a = causal_of(g, g.mq, g.mk, g.mv, lambda p: g.aT[:, 4 + p, 0:L], ["mla have", ("mla rotated", 4)], rows=96)
    only("pe", attn_pe, "mla", a)
    only("act", attn_act, "mla", a)
    only("dve", attn_dve, "mla", a)
    g.check(kind, "mla", 0)
    only("pe", out_pe, "e", L, ["y delta", ("attended", "mla")])
    only("dve", add_dve, "wo", "e", L, None)
    plain_norm(g, kind, e, "ffn0", "norm_ffn_0_2", ("h", "wo", "e"), g.half_upper)
    only("pe", glu_pe, "e")
    only("act", glu_act, "e")
    only("dve", glu_dve, "e")
    only("dve", add_dve, "gd", "e", L, None, True)
    g.check(kind, "even", 0)
    plain_norm(g, kind, e, "mix1", "norm_mix_1_2", ("h", "gd", "e"), g.half_upper)
    only("pe", odd_proj_pe)
    only("act", odd_proj_act)
    only("dve", odd_proj_dve)
    q = g.q2
    for name, a in (("fox", causal_of(g, q["fq"], q["fk"], q["fv"], lambda p: g.aT[:, p, 0:L],
                                      [("have", "fv"), "minus D"], d=g.negd)),
                    ("moba", causal_of(g, q["mq"], q["mk"], q["mv"], lambda p: g.aT[:, 4 + p, 0:L],
                                       [("have", "mv"), ("rotated", "mk")]))):
        only("pe", attn_pe, name, a)
        only("act", attn_act, name, a)
        only("dve", attn_dve, name, a)
    g.check(kind, "oattn", 0)
    only("pe", out_pe, "o", L, [("attended", "fox"), ("attended", "moba")])
    only("dve", add_dve, "wo", "o", L, None)
    plain_norm(g, kind, e, "ffn1", "norm_ffn_1_2", ("h", "wo", "o"))
    only("pe", route_pe)
    only("act", route_act)
    only("dve", route_dve)
    g.check(kind, "route", 0)
    only("pe", experts_pe)
    only("act", experts_act)
    only("dve", experts_dve)
    plain_norm(g, kind, e, "last", "final_norm_2", "experts over")
    only("pe", store_pe)
    only("act", store_act)


class Stop(Exception):
    pass


def first_block(g, kind, e):
    def only(k, f, *a):
        if kind == k:
            f(g, e, *a)
    if kind == "act":
        consts_act(g, e)
        silu_act(g, e)
        e.wait_ge(g.const_in["h0"], 16)
    for l in range(2):
        T = T2 if l == 0 else L
        only("pe", mod_pe, l)
        only("act", mod_act, l)
        only("dve", mod_dve, l)
        n1 = ("n1", l)
        if kind == "act":
            ready = [("gain", l, 0)] + ([("h", "dn", 0)] if l else [])
            norm_act(g, e, n1, g.hT, T2, lambda k, s: g.gain[:, l, 0, k, s:s + 1], lambda k, s: g.mod[:, l, k, s:s + 1], ready,
                     g.n1_upper)
        if kind == "pe":
            e.wait_ge(g.const_in["tab_a"], 16)
            norm_pe(g, e, n1, T2)
        only("dve", norm_dve, n1, g.hT, T2, None, True, None, g.n1_upper)
        only("act", bias_act, l)
        only("pe", proj_pe, l)
        only("act", proj_act, l)
        only("dve", proj_dve, l)
        g.check(kind, "proj", l)
        only("pe", pool_pe, l)
        only("act", pool_act, l)
        only("dve", bias_dve, l)
        for name, a in [("na", na_of(g, l))] + ([("ctx", ctx_attn_of(g, l))] if l == 0 else []):
            only("pe", attn_pe, (name, l), a)
            only("act", attn_act, (name, l), a)
            only("dve", attn_dve, (name, l), a)
        g.check(kind, "attn", l)
        only("act", ret_act, l)
        only("pool", ret_pool, l)
        only("pe", ret_pe, l)
        only("dve", ret_dve, l)
        g.check(kind, "ret", l)
        only("pe", out_pe, l, T, [("y ret", l), ("y pool", l), ("attended", ("ctx" if l == 0 else "na", l))])
        only("dve", add_dve, "wo", l, T, lambda m, s: g.mod[:, l, 16 + m, s:s + 1])
        g.check(kind, "wo", l)
        n2 = ("n2", l)
        if kind == "act":
            norm_act(g, e, n2, g.hT, T, lambda k, s: g.gain[:, l, 1, k, s:s + 1],
                     lambda k, s: g.mod[:, l, 24 + k, s:s + 1], [("h", "wo", l)], lambda k: g.n2_upper(l, k))
        only("pe", norm_pe, n2, T)
        only("dve", norm_dve, n2, g.hT, T, None, True, None, lambda k: g.n2_upper(l, k))
        only("pe", ffn1_pe, l, T)
        only("act", ffn1_act, l, T)
        only("dve", ffn1_dve, l, T)
        only("dve", add_dve, "dn", l, T, lambda m, s: g.mod[:, l, 40 + m, s:s + 1], l == 1)
        g.check(kind, "ffn", l)
    key = ("final", 1)
    if kind == "act":
        norm_act(g, e, key, g.hT, L, None, None, [("h", "dn", 1)])
    only("pe", norm_pe, key, L)
    if kind == "dve":
        norm_dve(g, e, key, g.hT, L, lambda k, s: g.v("final_g", k), None, dst=g.hT)
    g.check(kind, "final1", 0)


def build(nc, io, at, stop=None):
    g = Program(nc, io, at, stop)

    def check(kind, name, l):
        if stop == (name, l):
            raise Stop()

    g.check = check
    with ExitStack() as ctx:
        g.ctx = ctx
        g.slabs = slabs()
        g.next_slab = 0
        g.piece_of, g.slab_of = {}, []
        for n, x in enumerate(g.slabs):
            if is_split(x):
                g.piece_of[n] = len(g.slab_of)
                g.slab_of += [n, n]
        g.uppers, g.lowers = 0, 0
        g.expert_base = next(n for n, x in enumerate(g.slabs) if x[0] == "moe_wg_1_2")
        g.const_issued, g.biases = [], 0
        g.vec_at, nv = vector_places()
        g.hT, g.aT = g.sb("hT", KD, T2), g.sb_both("aT", KD, T2)
        g.ring = g.sb_both("ring", EXPERT_RING, SLOT)
        g.piece_upper = [g.ring[:, RING, SLOT // 2 * i:SLOT // 2 * i + SLOT // 2] for i in range(2)]
        g.vec = g.sb("vectors", nv)
        na, nb = io["tab_a"].shape[1], io["tab_b"].shape[1]
        g.tabs = g.sb_both("tables", max(na, nb))
        g.tab_at = packed(tables_a())[1]
        g.mod_rows = g.sb("mod_rows", 2, 512)
        g.pool_w = g.sb("pool_w", 2, 4, 64)
        g.cs, g.mod, g.gain = g.sb("silu_c", KD, 2), g.sb("modulation", 2, 48, 2), g.sb("gain", 2, 2, KD, 2)
        g.cend = g.sb("chunk_ends", 4, 8)
        g.rstd, g.eps = g.sb("rstd", T2), g.sb("eps", 4)
        g.nmax, g.rsum, g.rinv = g.sb("nmax", 4), g.sb("rsum", 4), g.sb("rinv", 4)
        big = g.sb_both("activations", 14976)
        tmp = g.sb_both("scratch", 4608)
        g.big, g.tmp = big, tmp

        def part(t, at_, *shape):
            n = int(np.prod(shape))
            v = t[:, at_:at_ + n]
            if len(shape) == 2:
                return v.rearrange("p (a b) -> p a b", a=shape[0])
            if len(shape) == 3:
                return v.rearrange("p (a b c) -> p a b c", a=shape[0], b=shape[1])
            return v

        g.part = part
        g.m1 = {n: part(big, 1536 * i, 3, 512) for i, n in enumerate(("naq", "nak", "rq", "rk", "gate"))}
        g.m1["nav"], g.m1["rv"] = part(big, 7680, 4, 384), part(big, 9216, 4, 384)
        g.m1["pool"] = part(big, 10752, 4, 256)
        g.bias, g.bias_flat = part(big, 11776, 12, 256), big[:, 11776:14848]
        g.hid = part(big, 0, KF, 512)
        g.probs, g.probsT = part(tmp, 0, 3, 512), part(tmp, 1536, 3, 512)
        g.banded = part(tmp, 3072, 2, 512)
        g.ret_e, g.ret_f, g.ret_a = part(tmp, 0, 4, 384), tmp[:, 1536:3072].rearrange("p (a b c) -> p a b c", a=2, b=2), part(tmp, 3072, 3, 512)
        g.conv = part(tmp, 0, 2, 2, 512)
        g.half_upper = lambda k: g.aT[:, k, L:T2]
        g.n1_upper = lambda k: tmp[:, T2 * k:T2 * k + T2]

        def n2_upper(l, k):
            if l == 1:
                return g.half_upper(k)
            return tmp[:, 2048:2560] if k == KD - 1 else big[:, KF * T2 + T2 * k:KF * T2 + T2 * k + T2]

        g.n2_upper = n2_upper
        second_places(g)
        g.rounds = ctx.enter_context(nc.sbuf_tensor("rounds", [P, 1], mybir.dt.int32))
        g.s = {n: ctx.enter_context(nc.semaphore(n)) for n in SEMAPHORES}
        g.counts = {n: 0 for n in SEMAPHORES}
        g.psum = [ctx.enter_context(nc.psum_tensor(f"bank{i}", [P, 512], F32)) for i in range(8)]
        g.slab_in = [ctx.enter_context(nc.semaphore(f"slab_in_slot{i}")) for i in range(RING)]
        g.const_in = {n: ctx.enter_context(nc.semaphore(f"{n}_in")) for n in ("vec", "h0", "tab_a", "tab_b", "pool_w")}
        g.expert_in = [ctx.enter_context(nc.semaphore(f"expert_slab_in_slot{i}")) for i in range(EXPERT_RING)]
        g.bias_in, g.out_sem = ctx.enter_context(nc.semaphore("bias_in")), ctx.enter_context(nc.semaphore("out_stored"))
        block = ctx.enter_context(nc.Block())

        def run(kind, e):
            g.tab_at = packed(tables_a())[1]
            g.uppers, g.lowers = 0, 0
            try:
                first_block(g, kind, e)
                second_block(g, kind, e)
            except Stop:
                pass

        @block.tensor
        def _(pe):
            run("pe", pe)
            g.used_slabs = g.next_slab

        @block.scalar
        def _(act):
            run("act", act)

        @block.vector
        def _(dve):
            dve.memset(g.eps[:, 0:1], EPS).then_inc(g.s["dve_start"], 1)
            g.count("dve_start")
            dve.memset(g.eps[:, 1:2], 64e-5).then_inc(g.s["dve_start"], 1)
            g.count("dve_start", "eps")
            run("dve", dve)

        @block.gpsimd
        def _(pool):
            run("pool", pool)

        @block.sync
        def _(sp):
            if g.stop:
                g.slabs = g.slabs[:g.used_slabs]
            loads_sp(g, sp)
            if not g.stop:
                experts_sp(g, sp)
            for name in g.const_issued:
                sp.wait_ge(g.const_in[name], 16)
            sp.wait_ge(g.bias_in, 16 * g.biases)
    return g


def kernel(**inputs):
    import numpy as _np
    import concourse.bacc as _bacc
    from concourse.bass_utils import run_bass_kernel_spmd as _run

    arrays = {f"in_{k}": v for k, v in lay_out({k: _np.asarray(v) for k, v in inputs.items()}).items()}

    def program(at):
        nc = _bacc.Bacc("TRN2", target_bir_lowering=False, num_devices=1)
        io = {k[3:]: nc.dram_tensor(k, v.shape, F32, kind="ExternalInput").ap() for k, v in arrays.items()}
        io["out"] = nc.dram_tensor("out", (L, D), F32, kind="ExternalOutput").ap()
        return nc, build(nc, io, at)

    _, counted = program({})
    _, counted = program(counted.now)
    nc, _ = program(counted.now)
    got = _run(nc, [arrays], core_ids=[0]).results[0]["out"]
    return got.reshape(1, L, D)
```
